# Optimizing a Trainium2 kernel written in Bass

```python
import jax, jax.numpy as jnp
from jax import lax
import numpy as np

D_MODEL = 1024
BATCH = 1
SEQ = 256
DEPTH = 2

CHUNK = 64
RMS_EPS = 1e-6
MLSTM_WIDTH = D_MODEL // 2
MLSTM_HEADS = 4
MLSTM_HEAD_DIM = MLSTM_WIDTH // MLSTM_HEADS
MLSTM_STAB_INIT = -1e30
SCONV_WIDTH = D_MODEL - MLSTM_WIDTH
SCONV_KERNEL = 3
S5_WIDTH = D_MODEL // 2
S5_GROUP_CH = 16
S5_GROUPS = S5_WIDTH // S5_GROUP_CH
S5_STATE = 64
HGRN_WIDTH = D_MODEL - S5_WIDTH
HGRN_HEADS = 4
HGRN_HEAD_DIM = HGRN_WIDTH // HGRN_HEADS
MOE_GROUPS = 4
MOE_EXPERTS_PER_GROUP = 8
MOE_EXPERTS = MOE_GROUPS * MOE_EXPERTS_PER_GROUP
MOE_TOP_K = 2
MOE_FF = D_MODEL // 4
AB_SIZES = (MLSTM_WIDTH,) * 4 + (MLSTM_HEADS,) * 2 + (SCONV_WIDTH,) * 3
CD_SIZES = (S5_WIDTH,) + (HGRN_WIDTH,) * 4

kernel_name = "hybrid_mlstm_conv_s5_hgrn2_hmoe"

def _offsets(sizes):
    return [int(v) for v in np.cumsum(sizes)[:-1]]

def rmsnorm(x, w):
    xf = x.astype(jnp.float32)
    y = xf * lax.rsqrt(jnp.mean(xf * xf, axis=-1, keepdims=True) + RMS_EPS)
    return (y * w.astype(jnp.float32)).astype(x.dtype)

def head_rmsnorm(h, w):
    return h * lax.rsqrt(jnp.mean(h * h, axis=-1, keepdims=True) + RMS_EPS) * w.astype(jnp.float32)

def to_chunks(t):
    b, s, h = t.shape[:3]
    t = t.reshape((b, s // CHUNK, CHUNK, h) + t.shape[3:])
    return t.transpose((1, 0, 3, 2) + tuple(range(4, t.ndim)))

def from_chunks(t):
    nc, b, h, l = t.shape[:4]
    t = t.transpose((1, 0, 3, 2) + tuple(range(4, t.ndim)))
    return t.reshape((b, nc * l, h) + t.shape[4:])

def mlstm_chunkwise(q, k, v, i_pre, f_pre):
    b, s, h, dh = q.shape
    causal = jnp.tril(jnp.ones((CHUNK, CHUNK), dtype=bool))
    xs = (to_chunks(q), to_chunks(k), to_chunks(v), to_chunks(i_pre),
          to_chunks(jax.nn.log_sigmoid(f_pre)))

    def step(carry, chunk):
        c_mat, n_vec, m = carry
        q_, k_, v_, i_, lf = chunk
        bcum = jnp.cumsum(lf, axis=-1)
        logw = jnp.where(causal, bcum[..., :, None] - bcum[..., None, :] + i_[..., None, :], -jnp.inf)
        inter = bcum + m[..., None]
        m_row = jnp.maximum(jnp.max(logw, axis=-1), inter)
        scores = jnp.einsum('bhld,bhsd->bhls', q_, k_) * jnp.exp(logw - m_row[..., None])
        inter_scale = jnp.exp(inter - m_row)
        num = (jnp.einsum('bhls,bhsd->bhld', scores, v_)
               + inter_scale[..., None] * jnp.einsum('bhek,bhlk->bhle', c_mat, q_))
        den = jnp.sum(scores, axis=-1) + inter_scale * jnp.einsum('bhk,bhlk->bhl', n_vec, q_)
        h_out = num / jnp.maximum(jnp.abs(den), jnp.exp(-m_row))[..., None]
        b_end = bcum[..., -1]
        logg = b_end[..., None] - bcum + i_
        m_new = jnp.maximum(b_end + m, jnp.max(logg, axis=-1))
        wk = jnp.exp(logg - m_new[..., None])
        decay = jnp.exp(b_end + m - m_new)
        c_new = decay[..., None, None] * c_mat + jnp.einsum('bhl,bhle,bhlk->bhek', wk, v_, k_)
        n_new = decay[..., None] * n_vec + jnp.einsum('bhl,bhlk->bhk', wk, k_)
        return (c_new, n_new, m_new), h_out

    init = (jnp.zeros((b, h, dh, dh), jnp.float32), jnp.zeros((b, h, dh), jnp.float32),
            jnp.full((b, h), MLSTM_STAB_INIT, jnp.float32))
    _, hs = lax.scan(step, init, xs)
    return from_chunks(hs)

def causal_dwconv(z, w):
    c = z.shape[-1]
    return lax.conv_general_dilated(z, w[:, None, :].astype(z.dtype), window_strides=(1,),
                                    padding=[(SCONV_KERNEL - 1, 0)],
                                    dimension_numbers=('NWC', 'WIO', 'NWC'),
                                    feature_group_count=c)

def mixer_ab(xn, w_in, gate_bias, head_norm, conv_w, w_out):
    bsz, s, _ = xn.shape
    proj = xn @ w_in
    q, k, v, o, ig, fg, gb, gc, xin = jnp.split(proj, _offsets(AB_SIZES), axis=-1)
    heads = lambda t: t.astype(jnp.float32).reshape(bsz, s, MLSTM_HEADS, MLSTM_HEAD_DIM)
    gbias = gate_bias.astype(jnp.float32)
    i_pre = ig.astype(jnp.float32) + gbias[:MLSTM_HEADS]
    f_pre = fg.astype(jnp.float32) + gbias[MLSTM_HEADS:]
    hm = mlstm_chunkwise(heads(q), heads(k) * (MLSTM_HEAD_DIM ** -0.5), heads(v), i_pre, f_pre)
    hm = head_rmsnorm(hm, head_norm.reshape(MLSTM_HEADS, MLSTM_HEAD_DIM)) * jax.nn.sigmoid(heads(o))
    hm = hm.reshape(bsz, s, MLSTM_WIDTH).astype(xn.dtype)
    yc = gb * causal_dwconv(gc * xin, conv_w)
    return jnp.concatenate([hm, yc], axis=-1) @ w_out

def s5_mixer(u, lam_re, lam_im, b_re, b_im, c_re, c_im, d_skip, log_dt, w_glu, b_glu):
    f32 = jnp.float32
    bsz, s, _ = u.shape
    uf = u.astype(f32).reshape(bsz, s, S5_GROUPS, S5_GROUP_CH)
    lam = lax.complex(lam_re.astype(f32), lam_im.astype(f32))
    dt = jnp.exp(log_dt.astype(f32))[:, None]
    lam_bar = jnp.exp(lam * dt)
    b_bar = ((lam_bar - 1.0) / lam)[..., None] * lax.complex(b_re.astype(f32), b_im.astype(f32))
    bu = jnp.einsum('bsgc,gpc->bsgp', uf.astype(jnp.complex64), b_bar)
    a = jnp.broadcast_to(lam_bar, bu.shape)

    def combine(e1, e2):
        a1, x1 = e1
        a2, x2 = e2
        return a2 * a1, a2 * x1 + x2

    _, states = lax.associative_scan(combine, (a, bu), axis=1)
    cmat = lax.complex(c_re.astype(f32), c_im.astype(f32))
    y = jnp.real(jnp.einsum('bsgp,gcp->bsgc', states, cmat)) + d_skip.astype(f32).reshape(S5_GROUPS, S5_GROUP_CH) * uf
    z = jax.nn.gelu(y.reshape(bsz, s, S5_WIDTH))
    return z * jax.nn.sigmoid(z @ w_glu.astype(f32) + b_glu.astype(f32))

def hgrn2_chunkwise(q, log_f, k, v):
    b, s, h, dk = q.shape
    dv = v.shape[-1]
    causal = jnp.tril(jnp.ones((CHUNK, CHUNK), dtype=bool))

    def step(state, chunk):
        q_, lf, k_, v_ = chunk
        bcum = jnp.cumsum(lf, axis=-2)
        diff = bcum[..., :, None, :] - bcum[..., None, :, :]
        decay = jnp.exp(jnp.where(causal[:, :, None], diff, -jnp.inf))
        attn = jnp.einsum('bhjk,bhjsk,bhsk->bhjs', q_, decay, k_)
        o = (jnp.einsum('bhjs,bhsv->bhjv', attn, v_)
             + jnp.einsum('bhjk,bhkv->bhjv', q_ * jnp.exp(bcum), state))
        b_end = bcum[..., -1, :]
        state_new = (jnp.exp(b_end)[..., None] * state
                     + jnp.einsum('bhsk,bhsv->bhkv', k_ * jnp.exp(b_end[..., None, :] - bcum), v_))
        return state_new, o

    init = jnp.zeros((b, h, dk, dv), jnp.float32)
    _, os_ = lax.scan(step, init, (to_chunks(q), to_chunks(log_f), to_chunks(k), to_chunks(v)))
    return from_chunks(os_)

def hgrn_lower_bound(lb_param, layer):
    sm = jax.nn.softmax(lb_param.astype(jnp.float32), axis=0)
    return jnp.cumsum(sm, axis=0)[layer] - sm[0]

def mixer_cd(xn, w_in, lam_re, lam_im, b_re, b_im, c_re, c_im, d_skip, log_dt, w_glu, b_glu,
             lower_bound, out_norm, w_out):
    bsz, s, _ = xn.shape
    proj = xn @ w_in
    u, q, fg, ig, og = jnp.split(proj, _offsets(CD_SIZES), axis=-1)
    y_s5 = s5_mixer(u, lam_re, lam_im, b_re, b_im, c_re, c_im, d_skip, log_dt, w_glu, b_glu)
    heads = lambda t: t.astype(jnp.float32).reshape(bsz, s, HGRN_HEADS, HGRN_HEAD_DIM)
    lb = lower_bound.reshape(HGRN_HEADS, HGRN_HEAD_DIM)
    log_f = jnp.logaddexp(jnp.log(lb), jnp.log1p(-lb) + jax.nn.log_sigmoid(heads(fg)))
    k = -jnp.expm1(log_f)
    o = hgrn2_chunkwise(heads(q), log_f, k, heads(ig))
    o = head_rmsnorm(o, out_norm.reshape(HGRN_HEADS, HGRN_HEAD_DIM)) * jax.nn.silu(heads(og))
    o = o.reshape(bsz, s, HGRN_WIDTH)
    mixed = jnp.concatenate([y_s5.astype(xn.dtype), o.astype(xn.dtype)], axis=-1)
    return mixed @ w_out

def hier_moe(xn, w_group, b_group, w_router, b_router, w_gate, w_up, w_down):
    f32 = jnp.float32
    bsz, s, d = xn.shape
    xf = xn.reshape(-1, d)
    t = xf.shape[0]
    grp_prob = jax.nn.softmax(xf.astype(f32) @ w_group.astype(f32) + b_group.astype(f32), axis=-1)
    g_val, g_idx = lax.top_k(grp_prob, 1)
    exp_logits = (xf.astype(f32) @ w_router.astype(f32) + b_router.astype(f32)).reshape(
        t, MOE_GROUPS, MOE_EXPERTS_PER_GROUP)
    sel = jnp.take_along_axis(exp_logits, g_idx[:, :, None], axis=1)[:, 0]
    e_val, e_idx = lax.top_k(jax.nn.softmax(sel, axis=-1), MOE_TOP_K)
    weights = g_val * e_val / jnp.sum(e_val, axis=-1, keepdims=True)
    expert_id = g_idx * MOE_EXPERTS_PER_GROUP + e_idx
    combine = jnp.einsum('tk,tke->te', weights, jax.nn.one_hot(expert_id, MOE_EXPERTS, dtype=f32))
    y = jnp.zeros((t, d), f32)
    for e in range(MOE_EXPERTS):
        hid = jax.nn.silu(xf @ w_gate[e]) * (xf @ w_up[e])
        y = y + combine[:, e:e + 1] * (hid @ w_down[e]).astype(f32)
    return y.astype(xn.dtype).reshape(bsz, s, d)

def setup_inputs(seed: int = 0) -> dict:
    key = jax.random.key(seed)
    ks = jax.random.split(key, 32)
    f32 = jnp.float32
    n_even = (DEPTH + 1) // 2
    n_odd = DEPTH // 2
    nrm = lambda k, shape, scale: jax.random.normal(k, shape, f32) * scale
    gain = lambda k, shape: 1.0 + nrm(k, shape, 0.05)
    d = D_MODEL
    gate_bias = jnp.concatenate(
        [nrm(ks[5], (n_even, MLSTM_HEADS), 0.1),
         jnp.linspace(3.0, 6.0, MLSTM_HEADS, dtype=f32)[None] + nrm(ks[6], (n_even, MLSTM_HEADS), 0.1)], axis=-1)
    lam_im = jnp.pi * jnp.arange(S5_STATE, dtype=f32)
    return {
        "x": nrm(ks[0], (BATCH, SEQ, d), 1.0),
        "norm_mix": gain(ks[1], (DEPTH, d)),
        "norm_ffn": gain(ks[2], (DEPTH, d)),
        "norm_final": gain(ks[3], (d,)),
        "ab_w_in": nrm(ks[4], (n_even, d, sum(AB_SIZES)), d ** -0.5),
        "ab_gate_bias": gate_bias,
        "ab_head_norm": gain(ks[7], (n_even, MLSTM_WIDTH)),
        "ab_conv_w": nrm(ks[8], (n_even, SCONV_KERNEL, SCONV_WIDTH), SCONV_KERNEL ** -0.5),
        "ab_w_out": nrm(ks[9], (n_even, MLSTM_WIDTH + SCONV_WIDTH, d), d ** -0.5),
        "cd_w_in": nrm(ks[10], (n_odd, d, sum(CD_SIZES)), d ** -0.5),
        "s5_lambda_re": -0.5 + nrm(ks[11], (n_odd, S5_GROUPS, S5_STATE), 0.01),
        "s5_lambda_im": lam_im + nrm(ks[12], (n_odd, S5_GROUPS, S5_STATE), 0.01),
        "s5_b_re": nrm(ks[13], (n_odd, S5_GROUPS, S5_STATE, S5_GROUP_CH), (2 * S5_GROUP_CH) ** -0.5),
        "s5_b_im": nrm(ks[14], (n_odd, S5_GROUPS, S5_STATE, S5_GROUP_CH), (2 * S5_GROUP_CH) ** -0.5),
        "s5_c_re": nrm(ks[15], (n_odd, S5_GROUPS, S5_GROUP_CH, S5_STATE), 0.5),
        "s5_c_im": nrm(ks[16], (n_odd, S5_GROUPS, S5_GROUP_CH, S5_STATE), 0.5),
        "s5_d": nrm(ks[17], (n_odd, S5_WIDTH), 1.0),
        "s5_log_dt": jax.random.uniform(ks[18], (n_odd, S5_GROUPS), f32, np.log(0.001), np.log(0.1)),
        "s5_w_glu": nrm(ks[19], (n_odd, S5_WIDTH, S5_WIDTH), S5_WIDTH ** -0.5),
        "s5_b_glu": nrm(ks[20], (n_odd, S5_WIDTH), 0.01),
        "hgrn_lb": nrm(ks[21], (DEPTH, HGRN_WIDTH), 0.1),
        "hgrn_out_norm": gain(ks[22], (n_odd, HGRN_WIDTH)),
        "cd_w_out": nrm(ks[23], (n_odd, S5_WIDTH + HGRN_WIDTH, d), d ** -0.5),
        "moe_w_group": nrm(ks[24], (DEPTH, d, MOE_GROUPS), d ** -0.5),
        "moe_b_group": nrm(ks[25], (DEPTH, MOE_GROUPS), 0.01),
        "moe_w_router": nrm(ks[26], (DEPTH, d, MOE_EXPERTS), d ** -0.5),
        "moe_b_router": nrm(ks[27], (DEPTH, MOE_EXPERTS), 0.01),
        "moe_w_gate": nrm(ks[28], (DEPTH, MOE_EXPERTS, d, MOE_FF), d ** -0.5),
        "moe_w_up": nrm(ks[29], (DEPTH, MOE_EXPERTS, d, MOE_FF), d ** -0.5),
        "moe_w_down": nrm(ks[30], (DEPTH, MOE_EXPERTS, MOE_FF, d), MOE_FF ** -0.5),
    }

def reference(x, norm_mix, norm_ffn, norm_final, ab_w_in, ab_gate_bias, ab_head_norm, ab_conv_w,
              ab_w_out, cd_w_in, s5_lambda_re, s5_lambda_im, s5_b_re, s5_b_im, s5_c_re, s5_c_im,
              s5_d, s5_log_dt, s5_w_glu, s5_b_glu, hgrn_lb, hgrn_out_norm, cd_w_out,
              moe_w_group, moe_b_group, moe_w_router, moe_b_router, moe_w_gate, moe_w_up,
              moe_w_down):
    h = x
    for layer in range(DEPTH):
        j = layer // 2
        hn = rmsnorm(h, norm_mix[layer])
        if layer % 2 == 0:
            mix = mixer_ab(hn, ab_w_in[j], ab_gate_bias[j], ab_head_norm[j], ab_conv_w[j], ab_w_out[j])
        else:
            mix = mixer_cd(hn, cd_w_in[j], s5_lambda_re[j], s5_lambda_im[j], s5_b_re[j], s5_b_im[j],
                           s5_c_re[j], s5_c_im[j], s5_d[j], s5_log_dt[j], s5_w_glu[j], s5_b_glu[j],
                           hgrn_lower_bound(hgrn_lb, layer), hgrn_out_norm[j], cd_w_out[j])
        h = h + mix
        h = h + hier_moe(rmsnorm(h, norm_ffn[layer]), moe_w_group[layer], moe_b_group[layer],
                         moe_w_router[layer], moe_b_router[layer], moe_w_gate[layer],
                         moe_w_up[layer], moe_w_down[layer])
    return rmsnorm(h, norm_final)


_drawn_inputs = setup_inputs


def setup_inputs(seed=0):
    import zlib

    import numpy as np

    out = dict(_drawn_inputs(seed))
    spreads = {}
    factors = {'s5_lambda_re': 8.0, 's5_b_glu': 8.0, 'moe_b_group': 4.539, 'moe_b_router': 6.309}
    for name, (base, spread) in spreads.items():
        noise = np.random.default_rng([zlib.crc32(name.encode()), seed]).standard_normal(out[name].shape)
        drawn = base * np.exp(spread * noise) if base else spread * noise
        out[name] = __import__('jax').numpy.asarray(drawn.astype(out[name].dtype))
    for name, factor in factors.items():
        out[name] = (out[name] * factor).astype(out[name].dtype)
    return out
```

```python
from contextlib import ExitStack

import numpy as np

import concourse.bass as bass
from concourse import mybir

F32 = mybir.dt.float32
I32 = mybir.dt.int32
U32 = mybir.dt.uint32
ALU = mybir.AluOpType
ACT = mybir.ActivationFunctionType
AX = mybir.AxisListType

P = 128
D = 1024
T = 256
NB = T // P
KC = D // P
W2 = D // 2
NH = 4
DH = W2 // NH
UNIT = 2048
UC = UNIT // KC
SLOTS = 12
E = 32
NG = 4
EG = E // NG
FF = D // 4
QE = 4
CAP = P // QE
NQ = E // QE
XB = 2 * T // CAP
XQ = XB // QE
NBLK = E + XB
S5T = 16
GCH = 16
FIRST_LEVEL = 8
LEVELS = [128, 64, 32, 16, 8, 4, 2, 1]
EPS = 1e-6
NEG = -1e30
TWO_PI = 6.283185


class Steps:

    def __init__(self, eng, sem):
        self.eng, self.sem, self.n = eng, sem, 0

    def add(self, ins):
        ins.then_inc(self.sem, 1)
        self.n += 1

    def wait(self):
        self.eng.wait_ge(self.sem, self.n)

    def then(self, ins):
        self.add(ins)
        self.wait()


def hybrid_trunk(nc, x, norm_mix, norm_ffn, norm_final, ab_w_in, ab_gate_bias, ab_head_norm,
                 ab_conv_w, ab_w_out, cd_w_in, s5_lambda_re, s5_lambda_im, s5_b_re, s5_b_im,
                 s5_c_re, s5_c_im, s5_d, s5_log_dt, s5_w_glu, s5_b_glu, hgrn_lb, hgrn_out_norm,
                 cd_w_out, moe_w_group, moe_b_group, moe_w_router, moe_b_router, moe_w_gate,
                 moe_w_up, moe_w_down, out):
    ctx = ExitStack()
    with ctx:
        def sb(name, shape, dt=F32):
            return ctx.enter_context(nc.sbuf_tensor(name, shape, dt))

        def sem(name):
            return ctx.enter_context(nc.semaphore(name))

        ring = sb("ring", [P, SLOTS, UNIT])
        H = sb("H", [P, NB, D])
        XN = sb("XN", [P, NB, D])
        XT = sb("XT", [P, KC, T])
        COS = sb("COS", [P, S5T, P])
        SIN = sb("SIN", [P, S5T, P])
        BT = sb("BT", [P, 2, NH, P])
        CT = sb("CT", [P, 3, NH, P])
        ident = sb("ident", [P, P])
        before = sb("before", [P, P])
        ones = sb("ones", [P, P])
        causal = sb("causal", [P, T])
        headsel = sb("headsel", [NH, NH, P])
        iota = sb("iota", [P, T])
        iota_i = sb("iota_i", [P, T], I32)
        row_i = sb("row_i", [P, 32], I32)
        lvl_mask = sb("lvl_mask", [P, 6, 32], I32)
        cst = sb("cst", [P, 4])
        caps = sb("caps", [P, 8])
        NW = sb("NW", [P, 4, KC])
        hnw = sb("hnw", [P, W2])
        prow = sb("prow", [P, P])
        PT = sb("PT", [P, 76])
        logdt = sb("logdt", [S5T, 2])
        s5 = sb("s5", [P, 24, S5T])
        lbc = sb("lbc", [P, 6, NH])
        stat = sb("stat", [P, 16])
        rms = sb("rms", [P, 16])
        rinv = sb("rinv", [P, 16])
        posm = sb("posm", [P, NB, NBLK])
        comb = sb("comb", [P, NB, NBLK])
        xid = sb("xid", [P, XB + 1], I32)
        wr = sb("wr", [P, 2, KC, NG + E])
        rb = sb("rb", [P, 2, NG + E])
        mtmp = sb("mtmp", [P, 6, 32])
        chmask = sb("chmask", [P, 2])

        room = (nc.sbuf_bytes_remaining // 4) // 32 * 32
        arena = sb("arena", [P, room])

        class Carve:
            def __init__(self, start=0):
                self.at = start

            def __call__(self, *shape, dt=F32):
                a = arena[:, self.at:self.at + int(np.prod(shape))]
                self.at += int(np.prod(shape))
                assert self.at <= room, (self.at, room)
                return shaped(a if dt == F32 else a.bitcast(dt), *shape)

        def shaped(a, *shape):
            names = "abcd"[:len(shape)]
            if len(shape) == 1:
                return a
            return a.rearrange(f"p ({' '.join(names)}) -> p {' '.join(names)}",
                               **dict(zip(names[1:], shape[1:])))

        cut = Carve()
        qT, kT = cut(NH, T), cut(NH, T)
        V0 = cut(NB, NH, DH + 2)
        SO = cut(NB, W2)
        GB, GC = cut(NH, T), cut(NH, T)
        rows = cut(6, T)
        cols = cut(2, NB, NH)
        em = cut(NB, NH)
        den = cut(NB, NH)
        gbias = cut(2)
        wg = cut(KC, 2 * NH)
        prep = cut.at
        conv_in = cut(NH, T + 2)
        DEC = cut(NH, 3 * P)
        HN = cut(NB, NH, DH)
        MT0 = shaped(arena[:, 0:2 * NH * T], 2 * NH, T)
        SQ = shaped(DEC.rearrange("p a b -> p (a b)")[:, 0:NB * W2], NB, NH, DH)
        cut = Carve(prep)
        bnat = cut(2, S5T, GCH)
        bbar = cut(2, S5T, GCH)
        BZ = cut(2, S5T, 2, GCH)
        cnat = cut(2, NH, 64)
        CZ = cut(2, NH, 2, 64)
        cut = Carve()
        uT = cut(NH, T)
        mixed = cut.at
        q1T, k1T, bT = cut(NH, T), cut(NH, T), cut(NH, T)
        MT1 = shaped(arena[:, mixed:mixed + 2 * NH * T], 2 * NH, T)
        V1 = cut(NB, NH, DH)
        SO1 = cut(NB, W2)
        qk_flat, le_flat = cut(NH * T), cut(NH * T)
        QK, LE = shaped(qk_flat, NH, T), shaped(le_flat, NH, T)
        HN1, SQ1 = shaped(qk_flat, NB, NH, DH), shaped(le_flat, NB, NH, DH)
        FT = LE
        A = cut(NH, 3, P)
        AD = cut(NH * NB, 32)
        mod = shaped(XN[:, 0, :], 2, 4, P)
        zst = shaped(XN[:, 1, 0:4 * P], 4, P)
        prod_flat = cut(8 * P)
        prod = shaped(prod_flat, 2, 4, P)
        glu_gate = shaped(prod_flat, NH, T)
        zin = cut(4)
        cut = Carve()
        XG = cut(KC, P)
        SG, HID = cut(FF), cut(FF)
        HT = cut(2, P)
        Y = cut(D)
        S = cut(NB, P)
        SW = cut(NB, P)
        Q = cut(NB, P)
        LG = cut(NB, NG + E)
        G8 = cut(NB, 8)
        gmx, smx = cut(NB, 8), cut(NB, 8)
        gix, six = cut(NB, 8, dt=U32), cut(NB, 8, dt=U32)
        ggf, gval, e2 = cut(NB, 1), cut(NB, 1), cut(NB, 1)
        eg, goh = cut(NB, NG), cut(NB, NG)
        selm = cut(NB, EG, NG)
        SEL = cut(NB, EG)
        wt, idc, gs = cut(2, NB, 1), cut(2, NB, 1), cut(2, NB, 1)
        MC = cut(2, NB, E)
        MM, pos, vv = cut(NB, E), cut(NB, E), cut(NB, E)
        cnt, nbk, endb = cut(E), cut(E), cut(E)
        over = cut(E, 8)
        t32 = cut(2, NB, E)
        vk, ink, tk = cut(2, NB, XB), cut(2, NB, XB), cut(2, NB, XB)
        eix = cut(XB, E)
        exf = cut(XB)
        fin = XT[:, :, :].rearrange("p c t -> p (c t)")

        bank = [ctx.enter_context(nc.psum_tensor(f"bank{i}", [P, 512], F32)) for i in range(8)]

        uses = [0] * SLOTS
        at = [0]

        def take():
            s = at[0] % SLOTS
            at[0] += 1
            uses[s] += 1
            return s, uses[s]

        ab_in = ab_w_in[0].rearrange("(p c) n -> p c n", p=P)
        ab_out = ab_w_out[0].rearrange("(k p) n -> p k n", p=P)
        cd_in = cd_w_in[0].rearrange("(p c) n -> p c n", p=P)
        cd_out = cd_w_out[0].rearrange("(k p) n -> p k n", p=P)
        glu = s5_w_glu[0].rearrange("(k p) n -> p k n", p=P)
        GATES = 4 * W2
        CONV = GATES + 2 * NH

        mix0 = [("q", 0), ("q", 1), ("k", 0), ("k", 1), ("v", 0), ("v", 1), ("gb", 0), ("gb", 1),
                ("gc", 0), ("gc", 1), ("x", 0), ("x", 1), ("o", 0), ("o", 1)]
        first0 = {"q": 0, "k": W2, "v": 2 * W2, "o": 3 * W2, "gb": CONV, "gc": CONV + W2,
                  "x": CONV + 2 * W2}
        plan0 = [(kind, half, *take()) for kind, half in mix0]
        outs0 = [(pair, *take()) for pair in (2, 3, 0, 1)]
        moe_use = [None, None]

        def plan_moe(layer):
            slots, base = [], []
            for _ in range(3 * QE):
                s, n = take()
                slots.append(s)
                base.append(n)
            for _ in range(3 * QE * (NQ - 1)):
                take()
            moe_use[layer] = (slots, base)

        plan_moe(0)
        mix1 = [("u", 0), ("u", 1), ("f", 0), ("f", 1), ("q", 0), ("q", 1), ("i", 0), ("i", 1),
                ("g", 0), ("g", 1)]
        first1 = {"u": 0, "q": W2, "f": 2 * W2, "i": 3 * W2, "g": 4 * W2}
        plan1 = [(kind, half, *take()) for kind, half in mix1]
        glu_at = take()
        outs1 = [(pair, *take()) for pair in (0, 1, 2, 3)]
        plan_moe(1)

        loaded = [sem(f"loaded{s}") for s in range(SLOTS)]
        done = [sem(f"done{s}") for s in range(SLOTS)]
        x_in, small_in, late_in = sem("x_in"), sem("small_in"), sem("late_in")
        lam_in, bc_in, wr_in = sem("lam_in"), sem("bc_in"), sem("wr_in")
        hn_in, out_done = sem("hn_in"), sem("out_done")
        act_step, dve_step, pool_step = sem("act_step"), sem("dve_step"), sem("pool_step")
        consts = sem("consts")
        rms_ready, xn_ready = sem("rms_ready"), sem("xn_ready")
        xt_psum, xt_ready = sem("xt_psum"), sem("xt_ready")
        copied0 = sem("copied0")
        gates_psum, gates_biased, softplus = sem("gates_psum"), sem("gates_biased"), sem("softplus")
        rows_ready = sem("rows_ready")
        cols_psum, cols_ready, em_ready = sem("cols_psum"), sem("cols_ready"), sem("em_ready")
        bcast_psum, arg_ready, decay_ready = sem("bcast_psum"), sem("arg_ready"), sem("decay_ready")
        scores_psum, weights_ready, num_psum = sem("scores_psum"), sem("weights_ready"), sem("num_psum")
        hss_ready, hrms_ready, hn_ready = sem("hss_ready"), sem("hrms_ready"), sem("hn_ready")
        hT_psum, mt_ready, conv_ready = sem("hT_psum"), sem("mt_ready"), sem("conv_ready")
        out_psum = sem("out_psum")
        h_ready = sem("h_ready")
        prow_ready, pt_psum, pt_ready = sem("prow_ready"), sem("pt_psum"), sem("pt_ready")
        s5_act, s5_dve, tab_ready = sem("s5_act"), sem("s5_dve"), sem("tab_ready")
        bz_ready, bct_psum = sem("bz_ready"), sem("bct_psum")
        bct_ready, phase_ready = sem("bct_ready"), sem("phase_ready")
        logit_psum, rt_act, rt_dve = sem("logit_psum"), sem("rt_act"), sem("rt_dve")
        choice_ready, pos_psum, route_ready = sem("choice_ready"), sem("pos_psum"), sem("route_ready")
        f_ready, f_log = sem("f_ready"), sem("f_log")
        copied1 = sem("copied1")
        bu_psum, bu_used, z_ready = sem("bu_psum"), sem("bu_used"), sem("z_ready")
        pc_ready, ps_ready, y_psum = sem("pc_ready"), sem("ps_ready"), sem("y_psum")
        y_ready, gelu_ready, glu_psum, glu_sig = sem("y_ready"), sem("gelu_ready"), sem("glu_psum"), sem("glu_sig")
        ys5_ready, b_ready, so_ready = sem("ys5_ready"), sem("b_ready"), sem("so_ready")
        larg, lexp, lqk, lpsum = sem("larg"), sem("lexp"), sem("lqk"), sem("lpsum")
        lcopied, o_psum, o_ready = sem("lcopied"), sem("o_psum"), sem("o_ready")
        a_zero, a_full = sem("a_zero"), sem("a_full")

        class Pass:

            def __init__(self, tag):
                self.onehot, self.onehotw = sem(f"onehot{tag}"), sem(f"onehotw{tag}")
                self.xg_psum, self.xg = sem(f"xg_psum{tag}"), sem(f"xg{tag}")
                self.q_psum, self.q = sem(f"q_psum{tag}"), sem(f"q{tag}")
                self.silu, self.hid = sem(f"silu{tag}"), sem(f"hid{tag}")
                self.ht_psum, self.ht = sem(f"ht_psum{tag}"), sem(f"ht{tag}")
                self.y = sem(f"y{tag}")
                self.acc_psum, self.added = sem(f"acc_psum{tag}"), sem(f"added{tag}")

        main = Pass("")
        extra = [Pass(f"_x{layer}") for layer in range(2)]
        xloaded = [[sem(f"xloaded{layer}_{k}") for k in range(3)] for layer in range(2)]
        xdone = [[sem(f"xdone{layer}_{k}") for k in range(3)] for layer in range(2)]

        block = ctx.enter_context(nc.Block())

        @block.sync
        def _(sp):
            def load(dst, src, s, n):
                if n > 1:
                    sp.wait_ge(done[s], n - 1)
                sp.dma_start(dst, src).then_inc(loaded[s], 16)

            def in_unit(w, first, kind, half, s, n):
                c0 = first[kind] + half * UC
                load(ring[:, s, :].rearrange("p (c n) -> p c n", c=KC), w[:, :, c0:c0 + UC], s, n)

            def out_unit(w, pair, s, n):
                load(ring[:, s, :].rearrange("p (k n) -> p k n", k=2), w[:, 2 * pair:2 * pair + 2, :], s, n)

            def experts(layer):
                slots, base = moe_use[layer]
                mats = [moe_w_gate, moe_w_up, moe_w_down]

                def src(k, e):
                    return mats[k][layer, e].rearrange("(p c) n -> p (c n)", p=P)

                with sp.Fori(0, NQ) as i:
                    for k in range(3):
                        for r in range(QE):
                            s, n = slots[k * QE + r], base[k * QE + r]
                            sp.wait_ge(done[s], i + (n - 1))
                            sp.wait_ge(done[s], n - 1)
                            sp.dma_start(ring[:, s, :], src(k, i * QE + r)).then_inc(loaded[s], 16)
                sp.wait_ge(route_ready, layer + 1)
                n_extra = sp.value_load(xid[0:1, XB:XB + 1], min_val=0, max_val=XB)
                with sp.If(n_extra > 0):
                    for s, n in zip(slots, base):
                        sp.wait_ge(done[s], n - 1 + NQ)
                    with sp.Fori(0, XQ) as i:
                        for k in range(3):
                            for r in range(QE):
                                e = sp.value_load(xid[0:1, bass.ds(i * QE + r, 1)], min_val=0, max_val=E - 1)
                                sp.wait_ge(extra[layer].xg_psum, i + 1)
                                sp.wait_ge(done[slots[k * QE + r]], 1)
                                sp.dma_start(ring[:, slots[k * QE + r], :], src(k, e)).then_inc(xloaded[layer][k], 16)
                    sp.wait_ge(xdone[layer][2], XQ)

            xv = x[0].rearrange("(b p) n -> p b n", p=P)
            for b in range(NB):
                sp.dma_start(H[:, b, :], xv[:, b, :]).then_inc(x_in, 16)
            for unit in plan0:
                in_unit(ab_in, first0, *unit)
            for unit in outs0:
                out_unit(ab_out, *unit)
            experts(0)
            for unit in plan1:
                in_unit(cd_in, first1, *unit)
            s, n = glu_at
            load(ring[:, s, :].rearrange("p (k n) -> p k n", k=4), glu, s, n)
            for unit in outs1:
                out_unit(cd_out, *unit)
            experts(1)

        @block.gpsimd
        def _(pool):
            g = Steps(pool, pool_step)
            g.add(pool.memset(ident[:, :], 0.0))
            g.add(pool.memset(ones[:, :], 1.0))
            g.add(pool.memset(before[:, :], 1.0))
            g.add(pool.memset(causal[:, :], 0.0))
            g.add(pool.memset(headsel[:, :, :], 0.0))
            g.add(pool.memset(cst[:, 0:1], EPS))
            g.add(pool.memset(cst[:, 1:2], 1.0))
            g.add(pool.memset(cst[:, 2:3], float(np.pi / 2)))
            g.wait()
            g.add(pool.affine_select(out=ident[:, :], in_=ident[:, :], compare_op=ALU.not_equal, fill=1.0,
                                     base=0, pattern=[[-1, P]], channel_multiplier=1))
            g.add(pool.affine_select(out=before[:, :], in_=before[:, :], compare_op=ALU.is_gt, fill=0.0,
                                     base=0, pattern=[[1, P]], channel_multiplier=-1))
            g.add(pool.affine_select(out=causal[:, :], in_=causal[:, :], compare_op=ALU.is_ge, fill=NEG,
                                     base=0, pattern=[[1, T]], channel_multiplier=-1))
            g.add(pool.affine_select(out=headsel[:, :, :], in_=headsel[:, :, :], compare_op=ALU.not_equal,
                                     fill=1.0, base=0, pattern=[[-1, NH], [0, P]], channel_multiplier=1))
            g.add(pool.iota(iota_i[:, :], [[1, T]], base=0, channel_multiplier=0))
            g.add(pool.iota(row_i[:, :], [[0, 32]], base=0, channel_multiplier=1))
            g.add(pool.memset(V0[:, :, :, DH:DH + 2], 1.0))
            g.wait()
            g.then(pool.tensor_copy(iota[:, :], iota_i[:, :]))
            pool.tensor_scalar(caps[:, :], iota[:, 0:8], float(CAP), float(CAP), ALU.mult, ALU.add)\
                .then_inc(consts, 1)
            pool.dma_start(logdt[:, :], s5_log_dt.rearrange("o (i a) -> (o i) a", a=2)).then_inc(lam_in, 16)
            for r0, w in ((16, s5_lambda_re[0]), (32, s5_lambda_im[0])):
                for gg in range(2):
                    pool.dma_start(prow[r0:r0 + S5T, 64 * gg:64 * gg + 64],
                                   w.rearrange("(i a) s -> a i s", a=2)[gg]).then_inc(lam_in, 16)
            for r0, v in ((48, ab_conv_w[0].rearrange("k (j c) -> (k j) c", c=P)),
                          (60, s5_d[0].rearrange("(j c) -> j c", c=P)),
                          (64, s5_b_glu[0].rearrange("(j c) -> j c", c=P)),
                          (68, hgrn_lb.rearrange("l (j c) -> (l j) c", c=P))):
                pool.dma_start(prow[r0:r0 + v.shape[0], :], v).then_inc(lam_in, 16)
            for k, w in enumerate((s5_b_re, s5_b_im)):
                wv = w[0].rearrange("(i a) s c -> a s i c", a=2)
                for gg in range(2):
                    pool.dma_start(bnat[64 * gg:64 * gg + 64, k], wv[gg]).then_inc(bc_in, 16)
            for k, w in enumerate((s5_c_re, s5_c_im)):
                pool.dma_start(cnat[:, k], w[0].rearrange("(j g) c s -> (g c) j s", g=8)).then_inc(bc_in, 16)
            for k, (wg_, we_) in enumerate(((moe_w_group[0], moe_w_router[0]), (moe_w_group[1], moe_w_router[1]))):
                pool.dma_start(wr[:, k, :, 0:NG], wg_.rearrange("(p c) n -> p c n", p=P)).then_inc(wr_in, 16)
                pool.dma_start(wr[:, k, :, NG:], we_.rearrange("(p c) n -> p c n", p=P)).then_inc(wr_in, 16)
                pool.dma_start(rb[:, k, 0:NG], moe_b_group[k:k + 1, :].to_broadcast([P, NG])).then_inc(wr_in, 16)
                pool.dma_start(rb[:, k, NG:], moe_b_router[k:k + 1, :].to_broadcast([P, E])).then_inc(wr_in, 16)

            pool.wait_ge(s5_dve, 1)
            g.then(pool.tensor_tensor(COS[:, :, :], iota[:, 0:P].unsqueeze(1).to_broadcast([P, S5T, P]),
                                      s5[:, 3, :].unsqueeze(2).to_broadcast([P, S5T, P]), ALU.mult))
            g.then(pool.tensor_copy(SIN[:, :, :].bitcast(I32), COS[:, :, :]))
            g.then(pool.tensor_copy(SIN[:, :, :], SIN[:, :, :].bitcast(I32)))
            pool.tensor_tensor(SIN[:, :, :], COS[:, :, :], SIN[:, :, :], ALU.subtract)\
                .then_inc(phase_ready, 1)

            pool.wait_ge(h_ready, 4)
            pool.dma_start(hnw[:, :], hgrn_out_norm[0:1, :].to_broadcast([P, W2])).then_inc(hn_in, 16)
            pool.memset(A[:, :, :, :], 0.0).then_inc(a_zero, 1)

            def level_arg(l):
                h = LEVELS[l]
                n = NH * T // (2 * h)
                bv = bT.rearrange("p h (n w) -> p (h n) w", w=2 * h)
                ev = LE.rearrange("p h (n w) -> p (h n) w", w=2 * h)
                mid = bv[:, :, h - 1:h].to_broadcast([P, n, h])
                if l == 0:
                    pool.wait_ge(b_ready, NH)
                else:
                    pool.wait_ge(lqk, l)
                g.add(pool.tensor_tensor(ev[:, :, 0:h], mid, bv[:, :, 0:h], ALU.subtract))
                pool.tensor_tensor(ev[:, :, h:2 * h], bv[:, :, h:2 * h], mid, ALU.subtract).then_inc(larg, 1)

            pool.wait_ge(tab_ready, 1)
            for i in range(S5T):
                if i >= FIRST_LEVEL:
                    level_arg(i - FIRST_LEVEL)
                pool.wait_ge(z_ready, i + 1)
                if i >= 1:
                    pool.wait_ge(y_psum, i)
                pool.tensor_tensor(prod[:, 1], zst, SIN[:, i:i + 1, :].to_broadcast([P, 4, P]), ALU.mult)\
                    .then_inc(ps_ready, 1)

        @block.scalar
        def _(act):
            a = Steps(act, act_step)
            sc = nc.scalar
            for k, w in enumerate((norm_mix[0], norm_ffn[0], norm_mix[1], norm_ffn[1])):
                act.dma_start(NW[:, k, :], w.rearrange("(p c) -> p c", p=P)).then_inc(small_in, 16)
            act.dma_start(wg, ab_in[:, :, GATES:GATES + 2 * NH]).then_inc(small_in, 16)
            for k in range(2):
                act.dma_start(gbias[0:NH, k:k + 1], ab_gate_bias[0, k * NH:(k + 1) * NH].rearrange("(h o) -> h o", o=1))\
                    .then_inc(small_in, 16)
            act.dma_start(hnw[:, :], ab_head_norm[0:1, :].to_broadcast([P, W2])).then_inc(small_in, 16)

            def norm(k):
                a.add(sc.activation(rms[:, 15:16], cst[:, 1:2], ACT.Sqrt))
                for b in range(NB):
                    j = 2 * k + b
                    if k == 0:
                        act.wait_ge(x_in, NB * 16)
                    else:
                        act.wait_ge(h_ready, 2 * (k - 1) + b + 1)
                    junk = XN[:, b, :] if k == 4 else XT[:, 4 * b:4 * b + 4, :].rearrange("p c t -> p (c t)")
                    a.then(sc.activation(junk, H[:, b, :], ACT.Square, accum_out=stat[:, j:j + 1]))
                    sc.activation(rms[:, j:j + 1], stat[:, j:j + 1], ACT.Sqrt, bias=cst[:, 0:1], scale=1.0 / D)\
                        .then_inc(rms_ready, 1)

            def head_rms(k):
                act.wait_ge(hss_ready, k + 1)
                sc.activation(s5[:, 22, 0:8], s5[:, 21, 0:8], ACT.Sqrt, bias=cst[:, 0:1], scale=1.0 / DH)\
                    .then_inc(hrms_ready, 1)

            def moe(layer):
                act.wait_ge(rt_dve, 2 * layer + 1)
                sc.activation(eg, eg, ACT.Exp).then_inc(rt_act, 1)
                act.wait_ge(rt_dve, 2 * layer + 2)
                sc.activation(e2, e2, ACT.Exp).then_inc(rt_act, 1)
                slots, base = moe_use[layer]

                def one(sems, wait_gate, wait_down):
                    wait_gate()
                    sc.activation(SG, bank[2][:, 0:FF], ACT.Silu).then_inc(sems.silu, 1)
                    wait_down()
                    sc.activation(Y[:, 0:512], bank[4][:, :], ACT.Copy)
                    sc.activation(Y[:, 512:1024], bank[5][:, :], ACT.Copy).then_inc(sems.y, 1)

                g_at, d_at = QE - 1, 3 * QE - 1
                with act.Fori(0, NQ) as i:
                    one(main, lambda: act.wait_ge(done[slots[g_at]], i + base[g_at]),
                        lambda: act.wait_ge(done[slots[d_at]], i + base[d_at]))
                act.wait_ge(route_ready, layer + 1)
                n_extra = act.value_load(xid[0:1, XB:XB + 1], min_val=0, max_val=XB)
                with act.If(n_extra > 0):
                    with act.Fori(0, XQ) as i:
                        one(extra[layer], lambda: act.wait_ge(xdone[layer][0], i + 1),
                            lambda: act.wait_ge(xdone[layer][2], i + 1))

            def s5_parameters():
                act.wait_ge(pt_ready, 1)
                sc.activation(s5[:, 0, :], PT[:, 0:16], ACT.Exp).then_inc(s5_act, 1)
                act.wait_ge(s5_dve, 1)
                a.add(sc.activation(s5[:, 4, :], s5[:, 3, :], ACT.Sin, scale=TWO_PI))
                a.add(sc.activation(s5[:, 5, :], s5[:, 3, :], ACT.Sin, scale=TWO_PI / 2))
                a.add(sc.activation(s5[:, 17, :], s5[:, 16, :], ACT.Sin, scale=TWO_PI))
                a.add(sc.activation(s5[:, 18, :], s5[:, 16, :], ACT.Sin, scale=TWO_PI / 2))
                a.add(sc.activation(lbc[:, 0:2, :], lbc[:, 0:2, :], ACT.Exp))
                sc.activation(s5[:, 6, :], s5[:, 1, :], ACT.Tanh, scale=0.5).then_inc(s5_act, 1)

            act.wait_ge(consts, 1)
            norm(0)
            for n, (kind, half, s, use) in enumerate(plan0):
                if n == 11:
                    head_rms(0)
                if kind == "x":
                    continue
                act.wait_ge(done[s], use)
                ps = bank[n % 4][:, :].rearrange("p (g t) -> p g t", g=2)
                two = slice(2 * half, 2 * half + 2)
                if kind == "q":
                    sc.activation(qT[:, two, :], ps, ACT.Copy).then_inc(copied0, 1)
                elif kind == "k":
                    sc.activation(kT[:, two, :], ps, ACT.Copy, scale=DH ** -0.5).then_inc(copied0, 1)
                elif kind == "v":
                    sc.activation(V0[:, :, two, 0:DH], ps.rearrange("p b (h e) -> p b h e", e=DH),
                                  ACT.Copy).then_inc(copied0, 1)
                elif kind == "o":
                    sc.activation(SO[:, :, half * UC:(half + 1) * UC], ps, ACT.Sigmoid).then_inc(copied0, 1)
                elif kind == "gb":
                    sc.activation(GB[:, two, :], ps, ACT.Copy).then_inc(copied0, 1)
                else:
                    sc.activation(GC[:, two, :], ps, ACT.Copy).then_inc(copied0, 1)
                if n == 0:
                    act.wait_ge(gates_biased, 1)
                    a.then(sc.activation(rows[0:NH, 3], rows[0:NH, 0], ACT.Abs))
                    a.then(sc.activation(rows[0:NH, 3], rows[0:NH, 3], ACT.Exp, scale=-1.0))
                    sc.activation(rows[0:NH, 3], rows[0:NH, 3], ACT.Ln, bias=cst[0:NH, 1:2]).then_inc(softplus, 1)
                if n == 1:
                    s5_parameters()
                if n == 7:
                    act.wait_ge(cols_ready, 1)
                    sc.activation(em, cols[:, 1], ACT.Exp).then_inc(em_ready, 1)
                    for h in range(NH):
                        act.wait_ge(arg_ready, h + 1)
                        sc.activation(DEC[:, h], DEC[:, h], ACT.Exp).then_inc(decay_ready, 1)
            act.wait_ge(phase_ready, 1)
            a.then(sc.activation(COS[:, :, :], SIN[:, :, :], ACT.Abs))
            a.add(sc.activation(COS[:, :, :], COS[:, :, :], ACT.Sin, bias=cst[:, 2:3], scale=-TWO_PI))
            sc.activation(SIN[:, :, :], SIN[:, :, :], ACT.Sin, scale=TWO_PI).then_inc(tab_ready, 1)
            for b in range(NB):
                act.wait_ge(hT_psum, b + 1)
                sc.activation(MT0[:, 0:NH, b * P:(b + 1) * P], bank[5 + b][:, :].rearrange("p (h t) -> p h t", t=P),
                              ACT.Copy).then_inc(mt_ready, 1)
            norm(1)
            moe(0)
            norm(2)

            for n, (kind, half, s, use) in enumerate(plan1):
                if n == 4:
                    act.wait_ge(f_ready, 1)
                    sc.activation(FT, FT, ACT.Ln).then_inc(f_log, 1)
                if n >= 6:
                    for l in (2 * (n - 6), 2 * (n - 6) + 1):
                        act.wait_ge(larg, l + 1)
                        sc.activation(LE, LE, ACT.Exp).then_inc(lexp, 1)
                act.wait_ge(done[s], use)
                ps = bank[n % 2][:, :].rearrange("p (g t) -> p g t", g=2)
                two = slice(2 * half, 2 * half + 2)
                if kind == "u":
                    sc.activation(uT[:, two, :], ps, ACT.Copy).then_inc(copied1, 1)
                elif kind == "f":
                    a.add(sc.activation(FT[:, two, :], ps, ACT.Sigmoid))
                    sc.activation(k1T[:, two, :], ps, ACT.Sigmoid, scale=-1.0).then_inc(copied1, 1)
                elif kind == "q":
                    sc.activation(q1T[:, two, :], ps, ACT.Copy).then_inc(copied1, 1)
                elif kind == "i":
                    sc.activation(V1[:, :, two, :], ps.rearrange("p b (h e) -> p b h e", e=DH),
                                  ACT.Copy).then_inc(copied1, 1)
                else:
                    sc.activation(SO1[:, :, half * UC:(half + 1) * UC], ps, ACT.Copy).then_inc(copied1, 1)
            act.wait_ge(copied1, 10)
            sc.activation(SO1, SO1, ACT.Silu).then_inc(so_ready, 1)
            for j in range(NH):
                act.wait_ge(y_ready, j + 1)
                sc.activation(uT[:, j, :], uT[:, j, :], ACT.Gelu_apprx_tanh).then_inc(gelu_ready, 1)
            for b in range(NB):
                act.wait_ge(o_psum, b + 1)
                sc.activation(HN1[:, b], bank[2 + b][:, :].rearrange("p (h e) -> p h e", e=DH), ACT.Copy)\
                    .then_inc(o_ready, 1)
            head_rms(1)
            for j in range(NH):
                if j < 2:
                    act.wait_ge(glu_psum, 1)
                else:
                    act.wait_ge(done[glu_at[0]], glu_at[1])
                sc.activation(glu_gate[:, j, :], bank[j // 2][:, (j % 2) * T:(j % 2 + 1) * T], ACT.Sigmoid,
                              bias=PT[:, 64 + j:65 + j]).then_inc(glu_sig, 1)
            for b in range(NB):
                act.wait_ge(hT_psum, NB + b + 1)
                sc.activation(MT1[:, NH:2 * NH, b * P:(b + 1) * P],
                              bank[2 + b][:, :].rearrange("p (h t) -> p h t", t=P), ACT.Copy).then_inc(mt_ready, 1)
            norm(3)
            moe(1)
            act.wait_ge(h_ready, 8)
            act.dma_start(fin[:, 0:D], norm_final.rearrange("(o n) -> o n", o=1).to_broadcast([P, D]))\
                .then_inc(late_in, 16)
            norm(4)
            ov = out[0].rearrange("(b p) n -> p b n", p=P)
            for b in range(NB):
                act.wait_ge(xn_ready, 2 * 4 + b + 1)
                act.dma_start(ov[:, b, :], XN[:, b, :]).then_inc(out_done, 16)
            act.wait_ge(out_done, NB * 16)

        @block.vector
        def _(dve):
            d = Steps(dve, dve_step)
            v = nc.vector

            def norm(k):
                for b in range(NB):
                    j = 2 * k + b
                    dve.wait_ge(rms_ready, j + 1)
                    d.then(v.reciprocal(rinv[:, j:j + 1], rms[:, j:j + 1]))
                    if k < 4:
                        v.tensor_scalar(XN[:, b, :], H[:, b, :], rinv[:, j:j + 1], None, ALU.mult)\
                            .then_inc(xn_ready, 1)
                        continue
                    dve.wait_ge(late_in, 16)
                    v.scalar_tensor_tensor(out=XN[:, b, :], in0=H[:, b, :], scalar=rinv[:, j:j + 1],
                                           in1=fin[:, 0:D], op0=ALU.mult, op1=ALU.mult).then_inc(xn_ready, 1)
                if k == 4:
                    return
                if k == 0:
                    dve.wait_ge(small_in, 8 * 16)
                for b in range(NB):
                    for g in range(2):
                        dve.wait_ge(xt_psum, 4 * k + 2 * b + g + 1)
                        v.tensor_tensor(XT[:, 4 * g:4 * g + 4, b * P:(b + 1) * P],
                                        bank[2 * b + g][:, :].rearrange("p (c t) -> p c t", t=P),
                                        NW[:, k, 4 * g:4 * g + 4].unsqueeze(2).to_broadcast([P, 4, P]), ALU.mult)\
                            .then_inc(xt_ready, 1)

            def head_squares(hn, sq):
                d.then(v.tensor_tensor(sq, hn, hn, ALU.mult))
                v.tensor_reduce(s5[:, 21, 0:8], sq.rearrange("p b h e -> p (b h) e"), AX.X, ALU.add)\
                    .then_inc(hss_ready, 1)

            def head_scale(k, hn, so):
                dve.wait_ge(hrms_ready, k + 1)
                d.then(v.reciprocal(s5[:, 23, 0:8], s5[:, 22, 0:8]))
                h8 = hn.rearrange("p b h e -> p (b h) e")
                d.then(v.tensor_tensor(h8, h8, s5[:, 23, 0:8].unsqueeze(2).to_broadcast([P, NB * NH, DH]), ALU.mult))
                for b in range(NB):
                    hb = hn[:, b].rearrange("p h e -> p (h e)")
                    v.tensor_tensor(hb, hb, so[:, b], ALU.mult).then_inc(hn_ready, 1)

            def gate_weight(so):
                d.then(v.tensor_tensor(so, so, hnw[:, :].unsqueeze(1).to_broadcast([P, NB, W2]), ALU.mult))

            def add_out(first, s, use):
                for b in range(NB):
                    if b == 0:
                        dve.wait_ge(out_psum, first // 4 + 1)
                    else:
                        dve.wait_ge(done[s], use)
                    for n in range(2):
                        hv = H[:, b, n * 512:(n + 1) * 512]
                        ins = v.tensor_tensor(hv, hv, bank[first + 2 * b + n][:, :], ALU.add)
                    ins.then_inc(h_ready, 1)

            def route(layer):
                dve.wait_ge(logit_psum, layer + 1)
                d.then(v.memset(G8, -3e38))
                d.then(v.tensor_tensor(LG, bank[4][:, 0:NB * (NG + E)].rearrange("p (b n) -> p b n", n=NG + E),
                                       rb[:, layer:layer + 1, :].to_broadcast([P, NB, NG + E]), ALU.add))
                d.then(v.tensor_copy(G8[:, :, 0:NG], LG[:, :, 0:NG]))
                for b in range(NB):
                    d.then(v.max(gmx[:, b], G8[:, b]))
                    d.then(v.max_index(gix[:, b], gmx[:, b], G8[:, b]))
                v.tensor_tensor(eg, LG[:, :, 0:NG], gmx[:, :, 0:1].to_broadcast([P, NB, NG]), ALU.subtract)\
                    .then_inc(rt_dve, 1)
                d.then(v.tensor_copy(ggf, gix[:, :, 0:1]))
                d.then(v.tensor_tensor(goh, iota[:, 0:NG].unsqueeze(1).to_broadcast([P, NB, NG]),
                                       ggf.to_broadcast([P, NB, NG]), ALU.is_equal))
                for b in range(NB):
                    d.then(v.tensor_tensor(selm[:, b], LG[:, b, NG:].rearrange("p (g j) -> p j g", j=EG),
                                          goh[:, b:b + 1, :].to_broadcast([P, EG, NG]), ALU.mult))
                d.then(v.tensor_reduce(SEL, selm, AX.X, ALU.add))
                for b in range(NB):
                    d.then(v.max(smx[:, b], SEL[:, b]))
                    d.then(v.max_index(six[:, b], smx[:, b], SEL[:, b]))
                v.tensor_tensor(e2, smx[:, :, 1:2], smx[:, :, 0:1], ALU.subtract).then_inc(rt_dve, 1)
                for c in range(2):
                    d.then(v.tensor_copy(idc[:, c], six[:, :, c:c + 1]))
                    d.then(v.scalar_tensor_tensor(out=idc[:, c], in0=ggf, scalar=float(EG), in1=idc[:, c],
                                                  op0=ALU.mult, op1=ALU.add))
                    d.then(v.tensor_tensor(MC[:, c], iota[:, 0:E].unsqueeze(1).to_broadcast([P, NB, E]),
                                           idc[:, c].to_broadcast([P, NB, E]), ALU.is_equal))
                v.tensor_tensor(MM, MC[:, 0], MC[:, 1], ALU.add).then_inc(choice_ready, 1)
                dve.wait_ge(pos_psum, layer + 1)
                d.then(v.tensor_copy(pos, bank[5][:, 0:2 * E].rearrange("p (b e) -> p b e", e=E)))
                d.then(v.tensor_copy(cnt, bank[5][:, 2 * E:3 * E]))
                d.then(v.scalar_tensor_tensor(out=posm[:, :, 0:E], in0=pos, scalar=1.0, in1=MM,
                                              op0=ALU.add, op1=ALU.mult))
                d.then(v.tensor_scalar(posm[:, :, 0:E], posm[:, :, 0:E], -1.0, None, ALU.add))

            def choice_weights(layer):
                dve.wait_ge(rt_act, 2 * layer + 2)
                d.then(v.tensor_reduce(gval, eg, AX.X, ALU.add))
                d.then(v.scalar_tensor_tensor(out=gval, in0=e2, scalar=1.0, in1=gval, op0=ALU.add, op1=ALU.mult))
                d.then(v.reciprocal(wt[:, 0], gval))
                d.then(v.tensor_tensor(wt[:, 1], e2, wt[:, 0], ALU.mult))
                for c in range(2):
                    d.then(v.tensor_tensor(t32[:, c], MC[:, c], wt[:, c].to_broadcast([P, NB, E]), ALU.mult))
                d.then(v.tensor_tensor(comb[:, :, 0:E], t32[:, 0], t32[:, 1], ALU.add))

            def further_lists():
                d.then(v.tensor_tensor(over, cnt.unsqueeze(2).to_broadcast([P, E, 8]),
                                       caps[:, :].unsqueeze(1).to_broadcast([P, E, 8]), ALU.is_gt))
                d.then(v.tensor_reduce(nbk, over, AX.X, ALU.add))
                d.then(v.tensor_tensor_scan(endb, ones[:, 0:E], nbk, 0.0, ALU.mult, ALU.add))
                d.then(v.tensor_tensor(nbk, endb, nbk, ALU.subtract))
                for b in range(NB):
                    d.then(v.scalar_tensor_tensor(out=vv[:, b], in0=nbk, scalar=float(CAP), in1=pos[:, b],
                                                 op0=ALU.mult, op1=ALU.add))
                d.then(v.tensor_scalar(t32[:, 0], pos, float(CAP), -1e6, ALU.is_lt, ALU.mult))
                d.then(v.scalar_tensor_tensor(out=vv, in0=vv, scalar=-float(CAP), in1=t32[:, 0],
                                              op0=ALU.add, op1=ALU.add))

            def further_blocks(layer):
                for c in range(2):
                    d.then(v.tensor_tensor(t32[:, c], MC[:, c], vv, ALU.mult))
                    d.then(v.tensor_reduce(gs[:, c], t32[:, c], AX.X, ALU.add))
                    for b in range(NB):
                        d.then(v.scalar_tensor_tensor(out=vk[:, c, b], in0=iota[:, 0:XB], scalar=-float(CAP),
                                                     in1=gs[:, c, b].to_broadcast([P, XB]),
                                                     op0=ALU.mult, op1=ALU.add))
                    d.then(v.tensor_scalar(ink[:, c], vk[:, c], 0.0, None, ALU.is_ge))
                    d.then(v.tensor_scalar(tk[:, c], vk[:, c], float(CAP), None, ALU.is_lt))
                    d.then(v.tensor_tensor(ink[:, c], ink[:, c], tk[:, c], ALU.mult))
                    d.then(v.scalar_tensor_tensor(out=vk[:, c], in0=vk[:, c], scalar=1.0, in1=ink[:, c],
                                                 op0=ALU.add, op1=ALU.mult))
                    d.then(v.tensor_tensor(tk[:, c], ink[:, c], wt[:, c].to_broadcast([P, NB, XB]), ALU.mult))
                d.then(v.scalar_tensor_tensor(out=posm[:, :, E:], in0=vk[:, 0], scalar=-1.0, in1=vk[:, 1],
                                             op0=ALU.add, op1=ALU.add))
                d.then(v.tensor_tensor(comb[:, :, E:], tk[:, 0], tk[:, 1], ALU.add))
                d.then(v.tensor_tensor(eix, endb.unsqueeze(1).to_broadcast([P, XB, E]),
                                       iota[:, 0:XB].unsqueeze(2).to_broadcast([P, XB, E]), ALU.is_le))
                d.then(v.tensor_reduce(exf, eix, AX.X, ALU.add))
                d.then(v.tensor_scalar(xid[:, 0:XB], exf, float(E - 1), None, ALU.min))
                v.tensor_copy(xid[:, XB:XB + 1], endb[:, E - 1:E]).then_inc(route_ready, 1)
                dve.wait_ge(route_ready, layer + 1)

            def moe(layer):
                route(layer)
                slots, base = moe_use[layer]

                def one(i, sems, n0, first, wait_up, routing=False):
                    at = bass.ds(i * QE + first, QE)
                    slot = iota[:, 0:CAP].unsqueeze(1).to_broadcast([P, QE, CAP])
                    for b in range(NB):
                        ins = v.tensor_tensor(S[:, b].rearrange("p (r j) -> p r j", j=CAP), slot,
                                              posm[:, b, at].unsqueeze(2).to_broadcast([P, QE, CAP]), ALU.is_equal)
                    ins.then_inc(sems.onehot, 1)
                    dve.wait_ge(sems.onehot, i + (n0 + 1))
                    if routing:
                        choice_weights(layer)
                    for b in range(NB):
                        ins = v.tensor_tensor(SW[:, b].rearrange("p (r j) -> p r j", j=CAP),
                                              S[:, b].rearrange("p (r j) -> p r j", j=CAP),
                                              comb[:, b, at].unsqueeze(2).to_broadcast([P, QE, CAP]), ALU.mult)
                    ins.then_inc(sems.onehotw, 1)
                    dve.wait_ge(sems.xg_psum, i + (n0 + 1))
                    for g in range(2):
                        ins = v.tensor_tensor(XG[:, 4 * g:4 * g + 4, :],
                                              bank[g][:, :].rearrange("p (c t) -> p c t", t=P),
                                              NW[:, 2 * layer + 1, 4 * g:4 * g + 4].unsqueeze(2)
                                              .to_broadcast([P, 4, P]), ALU.mult)
                    ins.then_inc(sems.xg, 1)
                    if routing:
                        further_lists()
                    dve.wait_ge(sems.q_psum, i + (n0 + 1))
                    v.tensor_copy(Q.rearrange("p b t -> p (b t)"), bank[1][:, 0:T]).then_inc(sems.q, 1)
                    dve.wait_ge(sems.silu, i + (n0 + 1))
                    wait_up()
                    v.tensor_tensor(HID, SG, bank[3][:, 0:FF], ALU.mult).then_inc(sems.hid, 1)
                    dve.wait_ge(sems.ht_psum, i + (n0 + 1))
                    v.tensor_copy(HT.rearrange("p c t -> p (c t)"), bank[0][:, 0:T]).then_inc(sems.ht, 1)
                    if routing:
                        further_blocks(layer)
                    for b in range(NB):
                        dve.wait_ge(sems.acc_psum, 2 * i + (2 * n0 + b + 1))
                        for n in range(2):
                            hv = H[:, b, n * 512:(n + 1) * 512]
                            ins = v.tensor_tensor(hv, hv, bank[6 + n][:, :], ALU.add)
                        ins.then_inc(sems.added, 1)

                u_at = 2 * QE - 1
                one(0, main, NQ * layer, 0, lambda: dve.wait_ge(done[slots[u_at]], base[u_at]), True)
                with dve.Fori(1, NQ) as i:
                    one(i, main, NQ * layer, 0, lambda: dve.wait_ge(done[slots[u_at]], i + base[u_at]))
                dve.wait_ge(main.added, 2 * NQ * (layer + 1))
                n_extra = dve.value_load(xid[0:1, XB:XB + 1], min_val=0, max_val=XB)
                with dve.If(n_extra > 0):
                    with dve.Fori(0, XQ) as i:
                        one(i, extra[layer], 0, E, lambda: dve.wait_ge(xdone[layer][1], i + 1))
                    dve.wait_ge(extra[layer].added, 2 * XQ)
                v.memset(stat[:, 15:16], 0.0).then_inc(h_ready, NB)

            dve.wait_ge(consts, 1)
            norm(0)
            dve.wait_ge(gates_psum, 1)
            d.then(v.tensor_scalar(rows[0:NH, 1, :], bank[4][0:NH, 0:T], gbias[0:NH, 0:1], None, ALU.add))
            d.then(v.tensor_copy(rows[0:NH, 0, :], bank[4][32:32 + NH, 0:T]))
            v.tensor_scalar(rows[0:NH, 0, :], rows[0:NH, 0, :], gbias[0:NH, 1:2], None, ALU.add)\
                .then_inc(gates_biased, 1)
            dve.wait_ge(lam_in, 9 * 16)
            for g in range(2):
                ins = v.tensor_copy(prow[0:S5T, 64 * g:64 * g + 64], logdt[:, g:g + 1].to_broadcast([S5T, 64]))
            ins.then_inc(prow_ready, 1)
            dve.wait_ge(pt_psum, 1)
            v.tensor_copy(PT[:, :], bank[7][:, 0:76]).then_inc(pt_ready, 1)
            dve.wait_ge(pt_ready, 1)
            re, im = PT[:, 16:32], PT[:, 32:48]
            lbp = PT[:, 68:76].rearrange("p (l j) -> p l j", l=2)
            d.then(v.tensor_tensor(lbc[:, 2, :], lbp[:, 0], lbp[:, 1], ALU.max))
            d.then(v.tensor_tensor(lbc[:, 0:2, :], lbp, lbc[:, 2:3, :].to_broadcast([P, 2, NH]), ALU.subtract))
            dve.wait_ge(s5_act, 1)
            d.then(v.tensor_tensor(s5[:, 1, :], re, s5[:, 0, :], ALU.mult))
            d.then(v.tensor_tensor(s5[:, 2, :], im, s5[:, 0, :], ALU.mult))
            d.then(v.tensor_scalar(s5[:, 2, :], s5[:, 2, :], float(1.0 / (2 * np.pi)), None, ALU.mult))
            d.then(v.tensor_copy(s5[:, 7, :].bitcast(I32), s5[:, 2, :]))
            d.then(v.tensor_tensor(s5[:, 3, :], s5[:, 2, :], s5[:, 7, :].bitcast(I32), ALU.subtract))
            d.then(v.tensor_scalar(s5[:, 15, :], s5[:, 3, :], float(P), None, ALU.mult))
            d.then(v.tensor_copy(s5[:, 7, :].bitcast(I32), s5[:, 15, :]))
            v.tensor_tensor(s5[:, 16, :], s5[:, 15, :], s5[:, 7, :].bitcast(I32), ALU.subtract).then_inc(s5_dve, 1)
            dve.wait_ge(softplus, 1)
            r4 = rows[0:NH]
            d.then(v.memset(r4[:, 5, :], 1.0))
            d.then(v.scalar_tensor_tensor(out=r4[:, 0, :], in0=r4[:, 0, :], scalar=0.0, in1=r4[:, 3, :],
                                          op0=ALU.min, op1=ALU.subtract))
            d.then(v.tensor_tensor_scan(r4[:, 2, :], r4[:, 5, :], r4[:, 0, :], 0.0, ALU.mult, ALU.add))
            d.then(v.tensor_tensor(r4[:, 3, :], r4[:, 1, :], r4[:, 2, :], ALU.subtract))
            d.then(v.tensor_tensor_scan(r4[:, 4, :], r4[:, 3, :], r4[:, 3, :], NEG, ALU.max, ALU.max))
            d.then(v.tensor_scalar(r4[:, 4, :], r4[:, 4, :], -1.0, None, ALU.mult))
            v.tensor_tensor(r4[:, 5, :], r4[:, 4, :], r4[:, 2, :], ALU.subtract).then_inc(rows_ready, 1)

            dve.wait_ge(s5_act, 2)
            col = [s5[:, k, :] for k in range(24)]
            d.then(v.tensor_scalar(col[7], col[6], -1.0, 1.0, ALU.mult, ALU.add))
            d.then(v.tensor_tensor(col[5], col[5], col[5], ALU.mult))
            d.then(v.reciprocal(col[7], col[7]))
            d.then(v.tensor_scalar(col[5], col[5], 2.0, None, ALU.mult))
            d.then(v.scalar_tensor_tensor(out=col[8], in0=col[6], scalar=1.0, in1=col[7], op0=ALU.add, op1=ALU.mult))
            d.then(v.scalar_tensor_tensor(out=col[9], in0=col[6], scalar=2.0, in1=col[7], op0=ALU.mult, op1=ALU.mult))
            d.then(v.tensor_scalar(col[10], col[5], -1.0, 1.0, ALU.mult, ALU.add))
            d.then(v.tensor_tensor(col[9], col[9], col[10], ALU.mult))
            d.then(v.tensor_tensor(col[9], col[9], col[5], ALU.subtract))
            d.then(v.tensor_tensor(col[11], col[8], col[4], ALU.mult))
            d.then(v.tensor_tensor(col[12], re, re, ALU.mult))
            d.then(v.tensor_tensor(col[13], im, im, ALU.mult))
            d.then(v.tensor_tensor(col[12], col[12], col[13], ALU.add))
            d.then(v.reciprocal(col[12], col[12]))
            d.then(v.tensor_tensor(col[13], col[9], re, ALU.mult))
            d.then(v.tensor_tensor(col[14], col[11], im, ALU.mult))
            d.then(v.tensor_tensor(col[15], col[11], re, ALU.mult))
            d.then(v.tensor_tensor(col[19], col[9], im, ALU.mult))
            d.then(v.tensor_tensor(col[13], col[13], col[14], ALU.add))
            d.then(v.tensor_tensor(col[14], col[15], col[19], ALU.subtract))
            d.then(v.tensor_tensor(col[13], col[13], col[12], ALU.mult))
            d.then(v.tensor_tensor(col[14], col[14], col[12], ALU.mult))
            d.then(v.tensor_tensor(col[18], col[18], col[18], ALU.mult))
            d.then(v.tensor_scalar(col[18], col[18], -2.0, 1.0, ALU.mult, ALU.add))
            cr = col[13].unsqueeze(2).to_broadcast([P, S5T, GCH])
            ci = col[14].unsqueeze(2).to_broadcast([P, S5T, GCH])
            tmp = shaped(BZ.rearrange("p a b c d -> p (a b c d)")[:, 0:S5T * GCH], S5T, GCH)
            dve.wait_ge(bc_in, 6 * 16)
            d.then(v.tensor_tensor(bbar[:, 0], bnat[:, 0], cr, ALU.mult))
            d.then(v.tensor_tensor(tmp, bnat[:, 1], ci, ALU.mult))
            d.then(v.tensor_tensor(bbar[:, 0], bbar[:, 0], tmp, ALU.subtract))
            d.then(v.tensor_tensor(bbar[:, 1], bnat[:, 1], cr, ALU.mult))
            d.then(v.tensor_tensor(tmp, bnat[:, 0], ci, ALU.mult))
            d.then(v.tensor_tensor(bbar[:, 1], bbar[:, 1], tmp, ALU.add))
            d.then(v.memset(BZ.rearrange("p a b c d -> p (a b c d)"), 0.0))
            for k in range(2):
                for g in range(2):
                    half = slice(64 * g, 64 * g + 64)
                    d.then(v.tensor_copy(BZ[half, k, :, g, :], bbar[half, k]))
            par = mtmp[:, 0, 0:2].bitcast(I32)
            d.then(v.tensor_scalar(par, row_i[:, 0:2], 4, 1, ALU.logical_shift_right, ALU.bitwise_and))
            d.then(v.tensor_copy(chmask[:, 0:2], par))
            d.then(v.tensor_scalar(chmask[:, 0:1], chmask[:, 0:1], -1.0, 1.0, ALU.mult, ALU.add))
            for k in range(2):
                for g in range(2):
                    ins = v.tensor_scalar(CZ[:, k, :, g, :], cnat[:, k], chmask[:, g:g + 1], None, ALU.mult)
                    if k == 1 and g == 1:
                        ins.then_inc(bz_ready, 1)
                    else:
                        d.then(ins)
            for k in range(2):
                dve.wait_ge(bct_psum, k + 1)
                v.tensor_copy(BT[:, k], bank[5 + k][:, :].rearrange("p (j s) -> p j s", s=P)).then_inc(bct_ready, 1)
            dve.wait_ge(bct_psum, 3)
            d.then(v.tensor_copy(CT[:, 0], bank[7][:, :].rearrange("p (j s) -> p j s", s=P)))
            v.tensor_scalar(CT[:, 1], bank[7][:, :].rearrange("p (j s) -> p j s", s=P), -1.0, None, ALU.mult)\
                .then_inc(bct_ready, 1)
            dve.wait_ge(bct_psum, 4)
            v.tensor_scalar(CT[:, 2], bank[5][:, :].rearrange("p (j s) -> p j s", s=P), -1.0, None, ALU.mult)\
                .then_inc(bct_ready, 1)
            d.then(v.tensor_tensor(lbc[:, 2, :], lbc[:, 0, :], lbc[:, 1, :], ALU.add))
            d.then(v.reciprocal(lbc[:, 2, :], lbc[:, 2, :]))
            d.then(v.tensor_tensor(lbc[:, 0:2, :], lbc[:, 0:2, :], lbc[:, 2:3, :].to_broadcast([P, 2, NH]), ALU.mult))
            d.then(v.tensor_tensor(lbc[:, 2, :], lbc[:, 0, :], lbc[:, 1, :], ALU.add))
            d.then(v.tensor_tensor(lbc[:, 2, :], lbc[:, 2, :], lbc[:, 0, :], ALU.subtract))
            d.then(v.tensor_scalar(lbc[:, 3, :], lbc[:, 2, :], -1.0, 1.0, ALU.mult, ALU.add))
            mi = [mtmp[:, k, :].bitcast(I32) for k in range(6)]
            mf = [mtmp[:, k, :] for k in range(6)]
            d.then(v.tensor_tensor(mi[0], row_i[:, :], iota_i[:, 0:32], ALU.bitwise_xor))
            d.then(v.tensor_scalar(mi[0], mi[0], 31, None, ALU.bitwise_and))
            d.then(v.tensor_scalar(mi[1], row_i[:, :], 31, None, ALU.bitwise_and))
            d.then(v.tensor_copy(mf[2], mi[0]))
            d.then(v.tensor_copy(mf[3], mi[1]))
            d.then(v.tensor_tensor(mf[3], iota[:, 0:32], mf[3], ALU.subtract))
            d.then(v.tensor_scalar(mf[4], mf[3], 0.0, None, ALU.is_gt))
            d.then(v.tensor_scalar(mf[5], mf[3], 0.0, None, ALU.is_lt))
            d.then(v.tensor_tensor(mf[2], mf[2], mf[4], ALU.mult))
            d.then(v.tensor_tensor(mf[2], mf[2], mf[5], ALU.subtract))
            for k, (lo, hi) in enumerate([(h, 2 * h) for h in LEVELS[3:]] + [(0, 1)]):
                d.then(v.tensor_scalar(mf[3], mf[2], float(lo), None, ALU.is_ge))
                d.then(v.tensor_scalar(mf[4], mf[2], float(hi), None, ALU.is_lt))
                d.then(v.tensor_tensor(lvl_mask[:, k, :], mf[3], mf[4], ALU.mult))

            dve.wait_ge(cols_psum, 1)
            v.tensor_copy(cols.rearrange("p k b h -> p (k b h)"), bank[4][:, 0:4 * NH]).then_inc(cols_ready, 1)
            dve.wait_ge(cols_ready, 1)
            for h in range(NH):
                dve.wait_ge(bcast_psum, h // 2 + 1)
                nm = bank[5 + h // 2][:, (h % 2) * T:(h % 2 + 1) * T]
                d.then(v.scalar_tensor_tensor(out=DEC[:, h, 0:T], in0=nm, scalar=cols[:, 0, 0, h:h + 1],
                                             in1=causal[:, :], op0=ALU.add, op1=ALU.add))
                v.scalar_tensor_tensor(out=DEC[:, h, T:T + P], in0=nm[:, P:T], scalar=cols[:, 0, 1, h:h + 1],
                                       in1=causal[:, 0:P], op0=ALU.add, op1=ALU.add).then_inc(arg_ready, 1)
            for h in range(NH):
                dve.wait_ge(decay_ready, h + 1)
                dve.wait_ge(scores_psum, h + 1)
                v.tensor_tensor(DEC[:, h], DEC[:, h], bank[7 if h % 2 == 0 else 4][:, 0:3 * P], ALU.mult)\
                    .then_inc(weights_ready, 1)
            dve.wait_ge(em_ready, 1)
            for n, (b, hp) in enumerate(((0, 0), (0, 1), (1, 0), (1, 1))):
                dve.wait_ge(num_psum, n + 1)
                ps = bank[(5, 6, 7, 4)[n]][:, 0:2 * (DH + 2)].rearrange("p (h e) -> p h e", e=DH + 2)
                dn = den[:, b, 2 * hp:2 * hp + 2].unsqueeze(2)
                eh = em[:, b, 2 * hp:2 * hp + 2].unsqueeze(2)
                d.then(v.tensor_copy(dn, ps[:, :, DH:DH + 1]))
                d.then(v.scalar_tensor_tensor(out=eh, in0=dn, scalar=-1.0, in1=eh, op0=ALU.mult, op1=ALU.max))
                d.then(v.tensor_tensor(dn, dn, eh, ALU.max))
                d.then(v.reciprocal(dn, dn))
                d.then(v.tensor_tensor(HN[:, b, 2 * hp:2 * hp + 2, :], ps[:, :, 0:DH],
                                      dn.to_broadcast([P, 2, DH]), ALU.mult))
            head_squares(HN, SQ)
            d.then(v.memset(conv_in[:, :, 0:2], 0.0))
            dve.wait_ge(copied0, 10)
            for half, (kind, hf, s, use) in enumerate(plan0[10:12]):
                dve.wait_ge(done[s], use)
                two = slice(2 * half, 2 * half + 2)
                d.then(v.tensor_tensor(conv_in[:, two, 2:], bank[(10 + half) % 4][:, :].rearrange("p (g t) -> p g t", g=2),
                                      GC[:, two, :], ALU.mult))
            for j in range(NH):
                d.then(v.tensor_scalar(GC[:, j, :], conv_in[:, j, 0:T], PT[:, 48 + j:49 + j], None, ALU.mult))
                for k in (1, 2):
                    d.then(v.scalar_tensor_tensor(out=GC[:, j, :], in0=conv_in[:, j, k:k + T],
                                                  scalar=PT[:, 48 + 4 * k + j:49 + 4 * k + j], in1=GC[:, j, :],
                                                  op0=ALU.mult, op1=ALU.add))
                v.tensor_tensor(MT0[:, NH + j, :], GC[:, j, :], GB[:, j, :], ALU.mult).then_inc(conv_ready, 1)
            dve.wait_ge(copied0, 12)
            gate_weight(SO)
            head_scale(0, HN, SO)
            add_out(0, *outs0[-1][1:])
            norm(1)
            moe(0)
            norm(2)

            dve.wait_ge(a_zero, 1)
            dve.wait_ge(tab_ready, 1)
            d.then(v.memset(AD, 0.0))

            def level_copy(l):
                dve.wait_ge(lpsum, l + 1)
                ps = bank[2 + l % 2]
                if l == 0:
                    ins = v.tensor_copy(A[:, :, 1, :], ps[:, :].rearrange("p (h t) -> p h t", t=P))
                elif l == 1:
                    for b in range(NB):
                        ins = v.tensor_copy(A[0:64, :, 2 * b, 64:P],
                                            ps[0:64, :].rearrange("p (h b t) -> p h b t", b=NB, t=64)[:, :, b])
                elif l == 2:
                    for i in range(2):
                        r = slice(64 * i, 64 * i + 32)
                        for b in range(NB):
                            ins = v.tensor_copy(A[r, :, 2 * b, 64 * i + 32:64 * i + 64],
                                                ps[r, 0:T].rearrange("p (h b t) -> p h b t", b=NB, t=32)[:, :, b])
                else:
                    ins = v.copy_predicated(AD, lvl_mask[:, l - 3:l - 2, :].to_broadcast([P, NH * NB, 32]),
                                            ps[:, 0:T].rearrange("p (n t) -> p n t", t=32))
                ins.then_inc(lcopied, 1)
                dve.wait_ge(lcopied, l + 1)

            def level_scale(l):
                h = LEVELS[l]
                dve.wait_ge(lexp, l + 1)
                cutup = lambda t: t.rearrange("p h (n w) -> p (h n) w", w=2 * h)
                d.then(v.tensor_tensor(cutup(QK)[:, :, 0:h], cutup(k1T)[:, :, 0:h], cutup(LE)[:, :, 0:h], ALU.mult))
                v.tensor_tensor(cutup(QK)[:, :, h:2 * h], cutup(q1T)[:, :, h:2 * h], cutup(LE)[:, :, h:2 * h],
                                ALU.mult).then_inc(lqk, 1)

            def s5_tile(i):
                dve.wait_ge(bu_psum, i + 1)
                bu = bank[4 + i % 2][:, :].rearrange("p (k t) -> p k t", t=P)
                cs, sn = COS[:, i:i + 1, :].to_broadcast([P, 4, P]), SIN[:, i:i + 1, :].to_broadcast([P, 4, P])
                d.then(v.tensor_tensor(mod[:, 0], bu, cs, ALU.mult))
                v.tensor_tensor(mod[:, 1], bu, sn, ALU.mult).then_inc(bu_used, 1)
                dve.wait_ge(bu_used, i + 1)
                if i >= 1:
                    dve.wait_ge(ps_ready, i)
                d.then(v.tensor_tensor(zst[:, 0:2], mod[:, 0, 0:2], mod[:, 1, 2:4], ALU.add))
                d.then(v.tensor_tensor(zst[:, 2:4], mod[:, 0, 2:4], mod[:, 1, 0:2], ALU.subtract))
                rho = s5[:, 8, i:i + 1].to_broadcast([P, P])
                d.then(v.tensor_tensor_scan(zst[:, 0], rho, zst[:, 0], 0.0, ALU.mult, ALU.add))
                d.then(v.tensor_tensor_scan(zst[:, 2], rho, zst[:, 2], 0.0, ALU.mult, ALU.add))
                c128, s128 = s5[:, 18, i:i + 1], s5[:, 17, i:i + 1]
                zr, zi = zst[:, 0, P - 1:P], zst[:, 2, P - 1:P]
                d.then(v.tensor_tensor(zin[:, 0:1], zi, s128, ALU.mult))
                d.then(v.tensor_tensor(zin[:, 1:2], zr, s128, ALU.mult))
                d.then(v.scalar_tensor_tensor(out=zin[:, 2:3], in0=zr, scalar=c128, in1=zin[:, 0:1],
                                             op0=ALU.mult, op1=ALU.subtract))
                d.then(v.scalar_tensor_tensor(out=zin[:, 3:4], in0=zi, scalar=c128, in1=zin[:, 1:2],
                                              op0=ALU.mult, op1=ALU.add))
                d.then(v.tensor_tensor_scan(zst[:, 1], rho, zst[:, 1], zin[:, 2:3], ALU.mult, ALU.add))
                v.tensor_tensor_scan(zst[:, 3], rho, zst[:, 3], zin[:, 3:4], ALU.mult, ALU.add).then_inc(z_ready, 1)
                dve.wait_ge(z_ready, i + 1)
                if i >= 1:
                    dve.wait_ge(y_psum, i)
                v.tensor_tensor(prod[:, 0], zst, cs, ALU.mult).then_inc(pc_ready, 1)

            def s5_skip(j):
                dve.wait_ge(y_psum, 4 * j + 4)
                v.scalar_tensor_tensor(out=uT[:, j, :], in0=uT[:, j, :], scalar=PT[:, 60 + j:61 + j],
                                       in1=bank[6 + j % 2][:, 0:T], op0=ALU.mult, op1=ALU.add).then_inc(y_ready, 1)

            for i in range(S5T):
                s5_tile(i)
                if i % 4 == 0 and i > 0:
                    s5_skip(i // 4 - 1)
                if i == 4:
                    dve.wait_ge(copied1, 4)
                    for h in range(NH):
                        d.add(v.tensor_scalar(k1T[:, h, :], k1T[:, h, :], lbc[:, 3, h:h + 1], None, ALU.mult))
                        ins = v.tensor_scalar(FT[:, h, :], FT[:, h, :], lbc[:, 3, h:h + 1], lbc[:, 2, h:h + 1],
                                              ALU.mult, ALU.add)
                    ins.then_inc(f_ready, 1)
                if i == 6:
                    dve.wait_ge(f_log, 1)
                    for h in range(NH):
                        v.tensor_tensor_scan(bT[:, h, :], ones[:, 0:1].to_broadcast([P, T]), FT[:, h, :], 0.0,
                                             ALU.mult, ALU.add).then_inc(b_ready, 1)
                l = i - FIRST_LEVEL
                if l == 0:
                    dve.wait_ge(copied1, 6)
                    d.wait()
                if l >= 0:
                    if l >= 1:
                        level_copy(l - 1)
                    level_scale(l)
            s5_skip(3)
            dve.wait_ge(so_ready, 1)
            dve.wait_ge(hn_in, 16)
            gate_weight(SO1)
            level_copy(7)
            level_copy(8)
            for i in range(4):
                r = slice(32 * i, 32 * i + 32)
                for b in range(NB):
                    ins = v.tensor_copy(A[r, :, 2 * b, r], AD.rearrange("p (h b) t -> p h b t", b=NB)[r, :, b])
            ins.then_inc(a_full, 1)
            dve.wait_ge(o_ready, 2)
            head_squares(HN1, SQ1)
            head_scale(1, HN1, SO1)
            for j in range(NH):
                dve.wait_ge(glu_sig, j + 1)
                v.tensor_tensor(MT1[:, j, :], uT[:, j, :], glu_gate[:, j, :], ALU.mult).then_inc(ys5_ready, 1)
            add_out(4, *outs1[-1][1:])
            norm(3)
            moe(1)
            norm(4)

        @block.tensor
        def _(pe):
            mm, tp = nc.tensor.matmul, nc.tensor.transpose

            def norm(k):
                for b in range(NB):
                    pe.wait_ge(xn_ready, 2 * k + b + 1)
                    xc = XN[:, b, :].rearrange("p (q c) -> p c q", c=KC)
                    for g in range(2):
                        for c in range(4):
                            ins = tp(bank[2 * b + g][:, c * P:(c + 1) * P], xc[:, 4 * g + c, :], ident[:, :])
                        ins.then_inc(xt_psum, 1)

            def unit(s, use):
                pe.wait_ge(loaded[s], 16 * use)
                return ring[:, s, :]

            def project(ps, s, use, transposed, halves=(0, 1)):
                w = (unit(s, use) if 0 in halves else ring[:, s, :]).rearrange("p (c n) -> p c n", c=KC)
                for g in halves:
                    for c in range(KC):
                        if transposed:
                            ins = mm(ps[:, g * T:(g + 1) * T], w[:, c, g * P:(g + 1) * P], XT[:, c, :],
                                     start=c == 0, stop=c == KC - 1)
                        else:
                            ins = mm(ps[:, g * UC:(g + 1) * UC], XT[:, c, g * P:(g + 1) * P], w[:, c, :],
                                     start=c == 0, stop=c == KC - 1)
                if 1 in halves:
                    ins.then_inc(done[s], 1)

            def out_unit(first, pair, s, use, start, stop):
                w = unit(s, use).rearrange("p (k n) -> p k n", k=2)
                for b in range(NB):
                    for k in range(2):
                        for n in range(2):
                            ins = mm(bank[first + 2 * b + n][:, :], (MT1 if first else MT0)[:, 2 * pair + k, b * P:(b + 1) * P],
                                     w[:, k, n * 512:(n + 1) * 512], start=start and k == 0, stop=stop and k == 1)
                    if stop and b == 0:
                        ins.then_inc(out_psum, 1)
                ins.then_inc(done[s], 1)

            def head_transposes(k, hn, first):
                for b in range(NB):
                    pe.wait_ge(hn_ready, NB * k + b + 1)
                    for h in range(NH):
                        ins = tp(bank[first + b][:, h * P:(h + 1) * P], hn[:, b, h, :], ident[:, :])
                    ins.then_inc(hT_psum, 1)

            def route(layer):
                k = 2 * layer + 1
                pe.wait_ge(xt_ready, 4 * k + 4)
                pe.wait_ge(wr_in, 8 * 16)
                for b in range(NB):
                    for c in range(KC):
                        ins = mm(bank[4][:, b * (NG + E):(b + 1) * (NG + E)], XT[:, c, b * P:(b + 1) * P],
                                 wr[:, layer, c, :], start=c == 0, stop=c == KC - 1)
                ins.then_inc(logit_psum, 1)
                pe.wait_ge(choice_ready, layer + 1)
                mm(bank[5][:, 0:E], before[:, :], MM[:, 0], start=True, stop=True)
                mm(bank[5][:, E:2 * E], before[:, :], MM[:, 1], start=True, stop=False)
                mm(bank[5][:, E:2 * E], ones[:, :], MM[:, 0], start=False, stop=True)
                mm(bank[5][:, 2 * E:3 * E], ones[:, :], MM[:, 0], start=True, stop=False)
                mm(bank[5][:, 2 * E:3 * E], ones[:, :], MM[:, 1], start=False, stop=True).then_inc(pos_psum, 1)

            def moe(layer):
                route(layer)
                slots, base = moe_use[layer]

                def one(i, sems, n0, wait_loaded, finish):
                    cols_of = [slice(r * CAP, (r + 1) * CAP) for r in range(QE)]
                    pe.wait_ge(sems.onehot, i + (n0 + 1))
                    xc = XN[:, :, :].rearrange("p b (q c) -> p b c q", c=KC)
                    for c in range(KC):
                        for b in range(NB):
                            ins = mm(bank[c // 4][:, (c % 4) * P:(c % 4 + 1) * P], xc[:, b, c, :], S[:, b],
                                     start=b == 0, stop=b == NB - 1)
                    ins.then_inc(sems.xg_psum, 1)
                    pe.wait_ge(sems.xg, i + (n0 + 1))
                    for k in range(2):
                        for r in range(QE):
                            wait_loaded(k, r)
                        for c in range(KC):
                            for r in range(QE):
                                w = ring[:, slots[k * QE + r], :].rearrange("p (c n) -> p c n", c=KC)
                                ins = mm(bank[2 + k][cols_of[r], 0:FF], XG[:, c, cols_of[r]], w[:, c, :],
                                         start=c == 0, stop=c == KC - 1)
                                if c == KC - 1:
                                    finish(ins, k, r)
                        if k == 0:
                            pe.wait_ge(sems.onehotw, i + (n0 + 1))
                            for b in range(NB):
                                ins = tp(bank[1][:, b * P:(b + 1) * P], SW[:, b], ident[:, :])
                            ins.then_inc(sems.q_psum, 1)
                    pe.wait_ge(sems.hid, i + (n0 + 1))
                    hc = HID.rearrange("p (q c) -> p c q", c=2)
                    for c in range(2):
                        ins = tp(bank[0][:, c * P:(c + 1) * P], hc[:, c, :], ident[:, :])
                    ins.then_inc(sems.ht_psum, 1)
                    pe.wait_ge(sems.ht, i + (n0 + 1))
                    for r in range(QE):
                        wait_loaded(2, r)
                    for n in range(2):
                        for c in range(2):
                            for r in range(QE):
                                w = ring[:, slots[2 * QE + r], :].rearrange("p (c n) -> p c n", c=2)
                                ins = mm(bank[4 + n][cols_of[r], :], HT[:, c, cols_of[r]],
                                         w[:, c, n * 512:(n + 1) * 512], start=c == 0, stop=c == 1)
                                if n == 1 and c == 1:
                                    finish(ins, 2, r)
                    pe.wait_ge(sems.q, i + (n0 + 1))
                    pe.wait_ge(sems.y, i + (n0 + 1))
                    for b in range(NB):
                        for n in range(2):
                            ins = mm(bank[6 + n][:, :], Q[:, b], Y[:, n * 512:(n + 1) * 512], start=True, stop=True)
                        ins.then_inc(sems.acc_psum, 1)
                        pe.wait_ge(sems.added, 2 * i + (2 * n0 + b + 1))

                with pe.Fori(0, NQ) as i:
                    one(i, main, NQ * layer,
                        lambda k, r: pe.wait_ge(loaded[slots[k * QE + r]], 16 * i + 16 * base[k * QE + r]),
                        lambda ins, k, r: ins.then_inc(done[slots[k * QE + r]], 1))
                pe.wait_ge(route_ready, layer + 1)
                n_extra = pe.value_load(xid[0:1, XB:XB + 1], min_val=0, max_val=XB)
                with pe.If(n_extra > 0):
                    with pe.Fori(0, XQ) as i:
                        one(i, extra[layer], 0,
                            lambda k, r: pe.wait_ge(xloaded[layer][k], 16 * QE * i + 16 * QE) if r == 0 else None,
                            lambda ins, k, r: ins.then_inc(xdone[layer][k], 1) if r == QE - 1 else None)

            pe.wait_ge(consts, 1)
            norm(0)
            pe.wait_ge(xt_ready, 4)
            pe.wait_ge(small_in, 8 * 16)
            for n, (kind, half, s, use) in enumerate(plan0):
                if n >= 4:
                    pe.wait_ge(copied0, n - 3)
                project(bank[n % 4], s, use, kind not in "vo")
                if n == 0:
                    for c in range(KC):
                        for k in range(2):
                            ins = mm(bank[4][32 * k:32 * k + NH, 0:T], wg[:, c, k * NH:(k + 1) * NH], XT[:, c, :],
                                     start=c == 0, stop=c == KC - 1)
                    ins.then_inc(gates_psum, 1)
                if n == 1:
                    pe.wait_ge(lam_in, 9 * 16)
                    pe.wait_ge(prow_ready, 1)
                    tp(bank[7][:, 0:76], prow[0:76, :], ident[0:76, 0:76]).then_inc(pt_psum, 1)
                if n == 4:
                    pe.wait_ge(bz_ready, 1)
                    pe.wait_ge(pt_ready, 1)
                    for k in range(3):
                        m = BZ[:, k].rearrange("p (j r) a c -> p j (r a c)", r=4) if k < 2 else \
                            CZ[:, 0].rearrange("p j a s -> p j (a s)")
                        for j in range(NH):
                            ins = tp(bank[5 + k][:, j * P:(j + 1) * P], m[:, j, :], ident[:, :])
                        ins.then_inc(bct_psum, 1)
                if n == 5:
                    pe.wait_ge(bct_ready, 1)
                    for j in range(NH):
                        ins = tp(bank[5][:, j * P:(j + 1) * P], CZ[:, 1, j].rearrange("p a s -> p (a s)"), ident[:, :])
                    ins.then_inc(bct_psum, 1)
                if n == 6:
                    pe.wait_ge(rows_ready, 1)
                    for b in range(NB):
                        for k, row in enumerate((3, 5)):
                            o = (k * NB + b) * NH
                            ins = tp(bank[4][:, o:o + NH], rows[0:NH, row, b * P:(b + 1) * P], ident[0:NH, 0:NH])
                    ins.then_inc(cols_psum, 1)
                    pe.wait_ge(bct_ready, 4)
                    for h in range(NH):
                        ins = mm(bank[5 + h // 2][:, (h % 2) * T:(h % 2 + 1) * T], headsel[:, h, :], rows[0:NH, 4, :],
                                 start=True, stop=True)
                        if h % 2:
                            ins.then_inc(bcast_psum, 1)
                if n == 8:
                    pe.wait_ge(cols_ready, 1)
                    pe.wait_ge(copied0, 4)
                    for h in range(NH):
                        if h >= 2:
                            pe.wait_ge(weights_ready, h - 1)
                        ps = bank[7 if h % 2 == 0 else 4]
                        mm(ps[:, 0:T], kT[:, h, 0:P], qT[:, h, :], start=True, stop=True)
                        mm(ps[:, T:T + P], kT[:, h, P:T], qT[:, h, P:T], start=True, stop=True).then_inc(scores_psum, 1)
                if n == 10:
                    pe.wait_ge(weights_ready, NH)
                    pe.wait_ge(copied0, 6)
                    for m, (b, hp) in enumerate(((0, 0), (0, 1), (1, 0), (1, 1))):
                        for h in (2 * hp, 2 * hp + 1):
                            ps = bank[(5, 6, 7, 4)[m]][:, (h % 2) * (DH + 2):(h % 2 + 1) * (DH + 2)]
                            if b == 0:
                                ins = mm(ps, DEC[:, h, 0:P], V0[:, 0, h, :], start=True, stop=True)
                            else:
                                mm(ps, DEC[:, h, P:T], V0[:, 0, h, :], start=True, stop=False)
                                ins = mm(ps, DEC[:, h, T:T + P], V0[:, 1, h, :], start=False, stop=True)
                        ins.then_inc(num_psum, 1)
            pe.wait_ge(copied0, 12)
            pe.wait_ge(conv_ready, NH)
            for n, (pair, s, use) in enumerate(outs0):
                if n == 2:
                    head_transposes(0, HN, 5)
                    pe.wait_ge(mt_ready, NB)
                out_unit(0, pair, s, use, n == 0, n == 3)
            norm(1)
            moe(0)
            norm(2)

            pe.wait_ge(xt_ready, 4 * 2 + 4)

            def s5_in(i):
                j, r = i // 4, slice(32 * (i % 4), 32 * (i % 4) + 32)
                if i >= 2:
                    pe.wait_ge(bu_used, i - 1)
                for k in range(2):
                    ins = mm(bank[4 + i % 2][:, k * T:(k + 1) * T], BT[r, k, j, :], uT[r, j, :], start=True, stop=True)
                ins.then_inc(bu_psum, 1)

            def s5_out(i):
                j, r = i // 4, slice(32 * (i % 4), 32 * (i % 4) + 32)
                if i % 4 == 0 and j >= 2:
                    pe.wait_ge(y_ready, j - 1)
                pe.wait_ge(pc_ready, i + 1)
                pe.wait_ge(ps_ready, i + 1)
                terms = ((0, 0, 0), (1, 1, 2), (2, 1, 0), (2, 0, 2))
                for n, (q, k, z) in enumerate(terms):
                    ins = mm(bank[6 + j % 2][r, 0:T], CT[:, q, j, r], prod[:, k, z:z + 2].rearrange("p a t -> p (a t)"),
                             start=n == 0, stop=n == 3)
                ins.then_inc(y_psum, 1)

            def level(l):
                ps = bank[2 + l % 2]
                if l < 8:
                    pe.wait_ge(lqk, l + 1)
                else:
                    pe.wait_ge(lcopied, 7)
                left, right = (QK, QK) if l < 8 else (k1T, q1T)
                for h in range(NH):
                    if l == 0:
                        ins = mm(ps[:, h * P:(h + 1) * P], left[:, h, 0:P], right[:, h, P:T], start=True, stop=True)
                        continue
                    for b in range(NB):
                        n = h * NB + b
                        if l == 1:
                            o = b * P
                            ins = mm(ps[0:64, n * 64:n * 64 + 64], left[:, h, o:o + 64], right[:, h, o + 64:o + P],
                                     start=True, stop=True)
                        elif l == 2:
                            for i in range(2):
                                o = b * P + 64 * i
                                ins = mm(ps[64 * i:64 * i + 32, n * 32:n * 32 + 32], left[:, h, o:o + 32],
                                         right[:, h, o + 32:o + 64], start=True, stop=True)
                        else:
                            for i in range(4):
                                o = b * P + 32 * i
                                ins = mm(ps[32 * i:32 * i + 32, n * 32:n * 32 + 32], left[:, h, o:o + 32],
                                         right[:, h, o:o + 32], start=True, stop=True)
                ins.then_inc(lpsum, 1)

            for n, (kind, half, s, use) in enumerate(plan1[:2]):
                project(bank[n], s, use, True)
            pe.wait_ge(copied1, 2)
            pe.wait_ge(bct_ready, 4)
            s5_in(0)
            for i in range(S5T):
                n, g = 2 + i // 2, i % 2
                kind, half, s, use = plan1[n]
                if i + 1 < S5T:
                    s5_in(i + 1)
                if g == 0:
                    pe.wait_ge(copied1, n - 1)
                project(bank[n % 2], s, use, kind not in "ig", (g,))
                if i >= FIRST_LEVEL + 1:
                    level(i - FIRST_LEVEL - 1)
                s5_out(i)
            level(7)
            level(8)
            pe.wait_ge(copied1, 10)
            pe.wait_ge(a_full, 1)
            for b in range(NB):
                for h in range(NH):
                    ps = bank[2 + b][:, h * P:(h + 1) * P]
                    if b == 0:
                        ins = mm(ps, A[:, h, 0, :], V1[:, 0, h, :], start=True, stop=True)
                    else:
                        mm(ps, A[:, h, 1, :], V1[:, 0, h, :], start=True, stop=False)
                        ins = mm(ps, A[:, h, 2, :], V1[:, 1, h, :], start=False, stop=True)
                ins.then_inc(o_psum, 1)
            pe.wait_ge(gelu_ready, NH)
            s, use = glu_at
            w = unit(s, use).rearrange("p (k n) -> p k n", k=NH)
            for j in range(NH):
                for k in range(NH):
                    ins = mm(bank[j // 2][:, (j % 2) * T:(j % 2 + 1) * T], w[:, k, j * P:(j + 1) * P], uT[:, k, :],
                             start=k == 0, stop=k == NH - 1)
                if j == 1:
                    ins.then_inc(glu_psum, 1)
            ins.then_inc(done[s], 1)
            head_transposes(1, HN1, 2)
            pe.wait_ge(ys5_ready, NH)
            pe.wait_ge(bu_used, S5T)
            for n, (pair, s, use) in enumerate(outs1):
                if n == 2:
                    pe.wait_ge(mt_ready, 2 * NB)
                out_unit(4, pair, s, use, n == 0, n == 3)
            norm(3)
            moe(1)


_OUTS = [((1, 256, 1024), 'float32')]


def kernel(**inputs):
    import numpy as _np
    import concourse.bacc as _bacc
    from concourse import mybir as _mybir
    from concourse.bass_utils import run_bass_kernel_spmd as _run

    names = ['x', 'norm_mix', 'norm_ffn', 'norm_final', 'ab_w_in', 'ab_gate_bias', 'ab_head_norm', 'ab_conv_w',
             'ab_w_out', 'cd_w_in', 's5_lambda_re', 's5_lambda_im', 's5_b_re', 's5_b_im', 's5_c_re', 's5_c_im',
             's5_d', 's5_log_dt', 's5_w_glu', 's5_b_glu', 'hgrn_lb', 'hgrn_out_norm', 'cd_w_out', 'moe_w_group',
             'moe_b_group', 'moe_w_router', 'moe_b_router', 'moe_w_gate', 'moe_w_up', 'moe_w_down']
    nc = _bacc.Bacc("TRN2", target_bir_lowering=False, num_devices=1)
    arrays, args = {}, []
    for name in names:
        a = _np.ascontiguousarray(inputs[name])
        arrays[f"in_{name}_dram"] = a
        args.append(nc.dram_tensor(f"in_{name}_dram", a.shape, _mybir.dt.from_np(a.dtype),
                                   kind="ExternalInput").ap())
    for i, (shape, dtype) in enumerate(_OUTS):
        dt = _mybir.dt.from_np(_np.dtype(dtype))
        args.append(nc.dram_tensor(f"out_{i}_dram", shape, dt, kind="ExternalOutput").ap())
    hybrid_trunk(nc, *args)
    r = _run(nc, [arrays], core_ids=[0])
    got = tuple(r.results[0][f"out_{i}_dram"] for i in range(len(_OUTS)))
    return got[0]
```

```python
from contextlib import ExitStack

import numpy as np

import concourse.bass as bass
from concourse import mybir

F32 = mybir.dt.float32
F32R = mybir.dt.float32r
I32 = mybir.dt.int32
U32 = mybir.dt.uint32
ALU = mybir.AluOpType
ACT = mybir.ActivationFunctionType
AX = mybir.AxisListType

P = 128
D = 1024
T = 256
NB = T // P
KC = D // P
W2 = D // 2
NH = 4
DH = W2 // NH
UNIT = 2048
UC = UNIT // KC
HALF = UNIT // 2
HI = 3
SLOTS = 12
E = 32
NG = 4
EG = E // NG
FF = D // 4
QE = 4
CAP = P // QE
NQ = E // QE
XB = 2 * T // CAP
XQ = XB // QE
NBLK = E + XB
S5T = 16
GCH = 16
FIRST_LEVEL = 4
LEVELS = [128, 64, 32, 16, 8, 4, 2, 1]
EPS = 1e-6
NEG = -1e30
TWO_PI = 6.283185


class Steps:

    def __init__(self, eng, sem):
        self.eng, self.sem, self.n = eng, sem, 0

    def add(self, ins):
        ins.then_inc(self.sem, 1)
        self.n += 1
        return self.n

    def wait(self, n=None):
        self.eng.wait_ge(self.sem, n or self.n)

    def then(self, ins):
        self.add(ins)
        self.wait()


def hybrid_trunk(nc, x, norm_mix, norm_ffn, norm_final, ab_w_in, ab_gate_bias, ab_head_norm,
                 ab_conv_w, ab_w_out, cd_w_in, s5_lambda_re, s5_lambda_im, s5_b_re, s5_b_im,
                 s5_c_re, s5_c_im, s5_d, s5_log_dt, s5_w_glu, s5_b_glu, hgrn_lb, hgrn_out_norm,
                 cd_w_out, moe_w_group, moe_b_group, moe_w_router, moe_b_router, moe_w_gate,
                 moe_w_up, moe_w_down, out):
    ctx = ExitStack()
    with ctx:
        def sb(name, shape, dt=F32):
            return ctx.enter_context(nc.sbuf_tensor(name, shape, dt))

        def sem(name):
            return ctx.enter_context(nc.semaphore(name))

        def under(name, shape, dt):
            with nc.sbuf_tensor(name, shape, dt) as t:
                return t

        ring_lo = under("ring_lo", [P, SLOTS, UNIT], F32R)
        ring = sb("ring", [P, SLOTS, UNIT])
        H = sb("H", [P, NB, D])
        XT_lo = under("XT_lo", [P, KC, T], F32R)
        XT = sb("XT", [P, KC, T])
        hi_parts = under("hi_parts", [P, KC * T + HI * HALF], F32R)
        XT_hi = hi_parts[:, 0:KC * T].rearrange("p (c t) -> p c t", t=T)
        W_hi = hi_parts[:, KC * T:].rearrange("p (i n) -> p i n", n=HALF)
        XN = sb("XN", [P, NB, D])
        SIN = sb("SIN", [P, S5T, P])
        COS = sb("COS", [P, S5T, P])
        BT = sb("BT", [P, 2, NH, P])
        CT = sb("CT", [P, 3, NH, P])
        ident = sb("ident", [P, P])
        before = sb("before", [P, P])
        ones = sb("ones", [P, P])
        tables = COS[:, 10:, :].rearrange("p i t -> p (i t)")
        headsel = tables[0:NH, 0:NH * P].rearrange("p (h t) -> p h t", t=P)
        causal = tables[:, NH * P:NH * P + T]
        iota = sb("iota", [P, T])
        iota_i = sb("iota_i", [P, T], I32)
        row_i = sb("row_i", [P, 32], I32)
        lvl_mask = sb("lvl_mask", [P, 6, 32], I32)
        cst = sb("cst", [P, 4])
        caps = sb("caps", [P, 8])
        NW = sb("NW", [P, 4, KC])
        hnw = sb("hnw", [P, W2])
        prow = sb("prow", [P, P])
        PT = sb("PT", [P, 76])
        logdt = sb("logdt", [S5T, 2])
        s5 = sb("s5", [P, 24, S5T])
        lbc = sb("lbc", [P, 6, NH])
        stat = sb("stat", [P, 16])
        rms = sb("rms", [P, 16])
        rinv = sb("rinv", [P, 16])
        posm = sb("posm", [P, NB, NBLK])
        comb = sb("comb", [P, NB, NBLK])
        xid = sb("xid", [P, XB + 1], I32)
        wr = sb("wr", [P, 2, KC, NG + E])
        rb = sb("rb", [P, 2, NG + E])
        mtmp = sb("mtmp", [P, 6, 32])
        chmask = sb("chmask", [P, 2])

        room = (nc.sbuf_bytes_remaining // 4) // 32 * 32
        arena = sb("arena", [P, room])

        class Carve:
            def __init__(self, start=0):
                self.at = start

            def __call__(self, *shape, dt=F32):
                a = arena[:, self.at:self.at + int(np.prod(shape))]
                self.at += int(np.prod(shape))
                assert self.at <= room, (self.at, room)
                return shaped(a if dt == F32 else a.bitcast(dt), *shape)

        def shaped(a, *shape):
            names = "abcd"[:len(shape)]
            if len(shape) == 1:
                return a
            return a.rearrange(f"p ({' '.join(names)}) -> p {' '.join(names)}",
                               **dict(zip(names[1:], shape[1:])))

        cut = Carve()
        qT, kT = cut(NH, T), cut(NH, T)
        V0 = cut(NB, NH, DH + 2)
        SO = cut(NB, W2)
        GB, GC = cut(NH, T), cut(NH, T)
        rows = cut(6, T)
        cols = cut(2, NB, NH)
        em = cut(NB, NH)
        den = cut(NB, NH)
        gbias = cut(2)
        wg = cut(KC, 2 * NH)
        prep = cut.at
        conv_in = cut(NH, T + 2)
        DEC = cut(NH, 3 * P)
        HN = cut(NB, NH, DH)
        MT0 = shaped(arena[:, 0:2 * NH * T], 2 * NH, T)
        SQ = shaped(DEC.rearrange("p a b -> p (a b)")[:, 0:NB * W2], NB, NH, DH)
        cut = Carve(prep)
        bnat = cut(2, S5T, GCH)
        bbar = cut(2, S5T, GCH)
        BZ = cut(2, S5T, 2, GCH)
        cnat = cut(2, NH, 64)
        CZ = cut(2, NH, 2, 64)
        cut = Carve()
        uT = cut(NH, T)
        mixed = cut.at
        q1T, k1T, bT = cut(NH, T), cut(NH, T), cut(NH, T)
        MT1 = shaped(arena[:, mixed:mixed + 2 * NH * T], 2 * NH, T)
        V1 = cut(NB, NH, DH)
        SO1 = cut(NB, W2)
        qk_flat, le_flat = cut(NH * T), cut(NH * T)
        QK, LE = shaped(qk_flat, NH, T), shaped(le_flat, NH, T)
        HN1, SQ1 = shaped(qk_flat, NB, NH, DH), shaped(le_flat, NB, NH, DH)
        FT = LE
        A = cut(NH, 3, P)
        AD = cut(NH * NB, 32)
        zst = shaped(XN[:, 0, :], 2, 4, P)
        mod = shaped(XN[:, 1, :], 2, 4, P)
        prod_flat = cut(16 * P)
        prod = shaped(prod_flat, 4, 4, P)
        glu_gate = shaped(prod_flat[:, 0:NH * T], NH, T)
        zin = cut(2, 4)
        cut = Carve()
        XG = cut(KC, P)
        SG, HID = cut(FF), cut(FF)
        HT = cut(2, P)
        Y = cut(D)
        S = cut(NB, P)
        SW = cut(NB, P)
        Q = cut(NB, P)
        LGT = cut(T)
        LG = cut(NB, NG + E)
        G8 = cut(NB, 8)
        gmx, smx = cut(NB, 8), cut(NB, 8)
        gix, six = cut(NB, 8, dt=U32), cut(NB, 8, dt=U32)
        ggf, gval, e2 = cut(NB, 1), cut(NB, 1), cut(NB, 1)
        eg, goh = cut(NB, NG), cut(NB, NG)
        selm = cut(NB, EG, NG)
        SEL = cut(NB, EG)
        wt, idc, gs = cut(2, NB, 1), cut(2, NB, 1), cut(2, NB, 1)
        MC = cut(2, NB, E)
        MM, pos, vv = cut(NB, E), cut(NB, E), cut(NB, E)
        cnt, nbk, endb = cut(E), cut(E), cut(E)
        over = cut(E, 8)
        t32 = cut(2, NB, E)
        vk, ink, tk = cut(2, NB, XB), cut(2, NB, XB), cut(2, NB, XB)
        eix = cut(XB, E)
        exf = cut(XB)
        fin = XT[:, :, :].rearrange("p c t -> p (c t)")

        pairs = [ctx.enter_context(nc.psum_tensor(f"pair{i}", [P, 2, 512], F32)) for i in range(2)]
        bank = [pairs[i // 2][:, i % 2, :] for i in range(4)]
        bank += [ctx.enter_context(nc.psum_tensor(f"bank{i}", [P, 512], F32)) for i in range(4, 8)]

        uses = [0] * SLOTS
        at = [0]

        def take():
            s = at[0] % SLOTS
            at[0] += 1
            uses[s] += 1
            return s, uses[s]

        ab_in = ab_w_in[0].rearrange("(p c) n -> p c n", p=P)
        ab_out = ab_w_out[0].rearrange("(k p) n -> p k n", p=P)
        cd_in = cd_w_in[0].rearrange("(p c) n -> p c n", p=P)
        cd_out = cd_w_out[0].rearrange("(k p) n -> p k n", p=P)
        glu = s5_w_glu[0].rearrange("(k p) n -> p k n", p=P)
        GATES = 4 * W2
        CONV = GATES + 2 * NH

        mix0 = [("q", 0), ("q", 1), ("k", 0), ("k", 1), ("v", 0), ("v", 1), ("gb", 0), ("gb", 1),
                ("gc", 0), ("gc", 1), ("x", 0), ("x", 1), ("o", 0), ("o", 1)]
        first0 = {"q": 0, "k": W2, "v": 2 * W2, "o": 3 * W2, "gb": CONV, "gc": CONV + W2,
                  "x": CONV + 2 * W2}
        plan0 = [(kind, half, *take()) for kind, half in mix0]
        outs0 = [(pair, *take()) for pair in (2, 3, 0, 1)]
        moe_use = [None, None]

        def plan_moe(layer):
            slots, base = [], []
            for _ in range(3 * QE):
                s, n = take()
                slots.append(s)
                base.append(n)
            for _ in range(3 * QE * (NQ - 1)):
                take()
            moe_use[layer] = (slots, base)

        plan_moe(0)
        mix1 = [("u", 0), ("u", 1), ("f", 0), ("f", 1), ("q", 0), ("q", 1), ("i", 0), ("i", 1),
                ("g", 0), ("g", 1)]
        first1 = {"u": 0, "q": W2, "f": 2 * W2, "i": 3 * W2, "g": 4 * W2}
        plan1 = [(kind, half, *take()) for kind, half in mix1]
        glu_at = take()
        outs1 = [(pair, *take()) for pair in (0, 1, 2, 3)]
        plan_moe(1)

        loaded = [sem(f"loaded{s}") for s in range(SLOTS)]
        done = [sem(f"done{s}") for s in range(SLOTS)]
        x_in = [sem(f"x_in{b}") for b in range(NB)]
        nw_in, wg_in = sem("nw_in"), sem("wg_in")
        small_in, late_in = sem("small_in"), sem("late_in")
        lam_in, bc_in, wr_in = sem("lam_in"), sem("bc_in"), sem("wr_in")
        out_done = sem("out_done")
        act_step, dve_step, pool_step = sem("act_step"), sem("dve_step"), sem("pool_step")
        consts = sem("consts")
        rms_ready, xn_ready = sem("rms_ready"), sem("xn_ready")
        xt_psum, xt_ready = sem("xt_psum"), sem("xt_ready")
        copied0 = sem("copied0")
        gates_psum, gates_biased, softplus = sem("gates_psum"), sem("gates_biased"), sem("softplus")
        rows_ready = sem("rows_ready")
        cols_psum, cols_ready, em_ready = sem("cols_psum"), sem("cols_ready"), sem("em_ready")
        bcast_psum, arg_ready, decay_ready = sem("bcast_psum"), sem("arg_ready"), sem("decay_ready")
        scores_psum, weights_ready, num_psum = sem("scores_psum"), sem("weights_ready"), sem("num_psum")
        hss_ready, hrms_ready, hn_ready = sem("hss_ready"), sem("hrms_ready"), sem("hn_ready")
        hT_psum, mt_ready, conv_ready = sem("hT_psum"), sem("mt_ready"), sem("conv_ready")
        hi_ready, lo_ready, half_used = sem("hi_ready"), sem("lo_ready"), sem("half_used")
        xt_split, x_used = sem("xt_split"), sem("x_used")
        out_psum = sem("out_psum")
        h_ready = sem("h_ready")
        prow_ready, pt_psum, pt_ready = sem("prow_ready"), sem("pt_psum"), sem("pt_ready")
        s5_act, s5_dve, tab_ready = sem("s5_act"), sem("s5_dve"), sem("tab_ready")
        bz_ready, bct_psum = sem("bz_ready"), sem("bct_psum")
        bct_ready, phase_ready = sem("bct_ready"), sem("phase_ready")
        logitT_psum, logitT_ready = sem("logitT_psum"), sem("logitT_ready")
        logit_psum, rt_act, rt_dve = sem("logit_psum"), sem("rt_act"), sem("rt_dve")
        choice_ready, pos_psum, route_ready = sem("choice_ready"), sem("pos_psum"), sem("route_ready")
        f_ready, f_log = sem("f_ready"), sem("f_log")
        copied1 = sem("copied1")
        bu_psum, bu_used, z_ready = sem("bu_psum"), sem("bu_used"), sem("z_ready")
        pc_ready, ps_ready, y_psum = sem("pc_ready"), sem("ps_ready"), sem("y_psum")
        y_ready, gelu_ready, glu_psum, glu_sig = sem("y_ready"), sem("gelu_ready"), sem("glu_psum"), sem("glu_sig")
        ys5_ready, b_ready, so_ready = sem("ys5_ready"), sem("b_ready"), sem("so_ready")
        larg, lexp, lqk, lpsum = sem("larg"), sem("lexp"), sem("lqk"), sem("lpsum")
        lcopied, o_psum, o_ready = sem("lcopied"), sem("o_psum"), sem("o_ready")
        a_zero, a_full = sem("a_zero"), sem("a_full")

        class Pass:

            def __init__(self, tag):
                self.onehot = sem(f"onehot{tag}")
                self.xg_psum, self.xg = sem(f"xg_psum{tag}"), sem(f"xg{tag}")
                self.q_psum, self.q = sem(f"q_psum{tag}"), sem(f"q{tag}")
                self.silu, self.hid = sem(f"silu{tag}"), sem(f"hid{tag}")
                self.ht_psum, self.ht = sem(f"ht_psum{tag}"), sem(f"ht{tag}")
                self.down0 = sem(f"down0{tag}")
                self.y, self.acc_psum, self.added = sem(f"y{tag}"), sem(f"acc_psum{tag}"), sem(f"added{tag}")

        main = Pass("")
        extra = [Pass(f"_x{layer}") for layer in range(2)]
        xloaded = [sem(f"xloaded{layer}") for layer in range(2)]
        xdone = [sem(f"xdone{layer}") for layer in range(2)]

        block = ctx.enter_context(nc.Block())

        @block.sync
        def _(sp):
            def load(dst, src, s, n):
                if n > 1:
                    sp.wait_ge(done[s], n - 1)
                sp.dma_start(dst, src).then_inc(loaded[s], 16)

            def in_unit(w, first, kind, half, s, n):
                c0 = first[kind] + half * UC
                load(ring[:, s, :].rearrange("p (c n) -> p c n", c=KC), w[:, :, c0:c0 + UC], s, n)

            def out_unit(w, pair, s, n):
                load(ring[:, s, :].rearrange("p (k n) -> p k n", k=2), w[:, 2 * pair:2 * pair + 2, :], s, n)

            def experts(layer):
                slots, base = moe_use[layer]
                mats = [moe_w_gate, moe_w_up, moe_w_down]

                def src(k, e):
                    return mats[k][layer, e].rearrange("(p c) n -> p (c n)", p=P)

                with sp.Fori(0, NQ) as i:
                    for k in range(3):
                        for r in range(QE):
                            s, n = slots[k * QE + r], base[k * QE + r]
                            sp.wait_ge(done[s], i + (n - 1))
                            sp.wait_ge(done[s], n - 1)
                            sp.dma_start(ring[:, s, :], src(k, i * QE + r)).then_inc(loaded[s], 16)
                sp.wait_ge(route_ready, layer + 1)
                n_extra = sp.value_load(xid[0:1, XB:XB + 1], min_val=0, max_val=XB)
                with sp.If(n_extra > 0):
                    for s, n in zip(slots, base):
                        sp.wait_ge(done[s], n - 1 + NQ)
                    with sp.Fori(0, XQ) as i:
                        for k in range(3):
                            for r in range(QE):
                                e = sp.value_load(xid[0:1, bass.ds(i * QE + r, 1)], min_val=0, max_val=E - 1)
                                sp.wait_ge(extra[layer].xg_psum, i + 1)
                                sp.wait_ge(done[slots[k * QE + r]], 1)
                                sp.dma_start(ring[:, slots[k * QE + r], :], src(k, e)).then_inc(xloaded[layer], 16)
                    sp.wait_ge(xdone[layer], 3 * XQ)

            xv = x[0].rearrange("(b p) n -> p b n", p=P)
            for b in range(NB):
                sp.dma_start(H[:, b, :], xv[:, b, :]).then_inc(x_in[b], 16)
            sp.dma_start(NW[:, 0, :], norm_mix[0].rearrange("(p c) -> p c", p=P)).then_inc(nw_in, 16)
            sp.dma_start(wg, ab_in[:, :, GATES:GATES + 2 * NH]).then_inc(wg_in, 16)
            for k in range(2):
                sp.dma_start(gbias[0:NH, k:k + 1], ab_gate_bias[0, k * NH:(k + 1) * NH].rearrange("(h o) -> h o", o=1))\
                    .then_inc(wg_in, 16)
            for n, unit in enumerate(plan0):
                in_unit(ab_in, first0, *unit)
                if n == 2:
                    sp.dma_start(logdt[:, :], s5_log_dt.rearrange("o (i a) -> (o i) a", a=2)).then_inc(lam_in, 16)
                    for r0, w in ((16, s5_lambda_re[0]), (32, s5_lambda_im[0])):
                        for gg in range(2):
                            sp.dma_start(prow[r0:r0 + S5T, 64 * gg:64 * gg + 64],
                                           w.rearrange("(i a) s -> a i s", a=2)[gg]).then_inc(lam_in, 16)
                    for r0, v in ((48, ab_conv_w[0].rearrange("k (j c) -> (k j) c", c=P)),
                                  (60, s5_d[0].rearrange("(j c) -> j c", c=P)),
                                  (64, s5_b_glu[0].rearrange("(j c) -> j c", c=P)),
                                  (68, hgrn_lb.rearrange("l (j c) -> (l j) c", c=P))):
                        sp.dma_start(prow[r0:r0 + v.shape[0], :], v).then_inc(lam_in, 16)
                if n == 4:
                    for k, w in enumerate((s5_b_re, s5_b_im)):
                        wv = w[0].rearrange("(i a) s c -> a s i c", a=2)
                        for gg in range(2):
                            sp.dma_start(bnat[64 * gg:64 * gg + 64, k], wv[gg]).then_inc(bc_in, 16)
                    for k, w in enumerate((s5_c_re, s5_c_im)):
                        sp.dma_start(cnat[:, k], w[0].rearrange("(j g) c s -> (g c) j s", g=8)).then_inc(bc_in, 16)
                if n == 8:
                    for k, (wg_, we_) in enumerate(((moe_w_group[0], moe_w_router[0]), (moe_w_group[1], moe_w_router[1]))):
                        sp.dma_start(wr[:, k, :, 0:NG], wg_.rearrange("(p c) n -> p c n", p=P)).then_inc(wr_in, 16)
                        sp.dma_start(wr[:, k, :, NG:], we_.rearrange("(p c) n -> p c n", p=P)).then_inc(wr_in, 16)
                        sp.dma_start(rb[:, k, 0:NG], moe_b_group[k:k + 1, :].to_broadcast([P, NG])).then_inc(wr_in, 16)
                        sp.dma_start(rb[:, k, NG:], moe_b_router[k:k + 1, :].to_broadcast([P, E])).then_inc(wr_in, 16)
            for unit in outs0:
                out_unit(ab_out, *unit)
            experts(0)
            for unit in plan1:
                in_unit(cd_in, first1, *unit)
            s, n = glu_at
            load(ring[:, s, :].rearrange("p (k n) -> p k n", k=4), glu, s, n)
            for unit in outs1:
                out_unit(cd_out, *unit)
            experts(1)

        @block.gpsimd
        def _(pool):
            g = Steps(pool, pool_step)
            g.add(pool.memset(ident[:, :], 0.0))
            g.add(pool.memset(ones[:, :], 1.0))
            g.add(pool.memset(before[:, :], 1.0))
            g.add(pool.memset(causal[:, :], 0.0))
            g.add(pool.memset(headsel[:, :, :], 0.0))
            g.add(pool.memset(cst[:, 0:1], EPS))
            g.add(pool.memset(cst[:, 1:2], 1.0))
            g.add(pool.memset(cst[:, 2:3], float(np.pi / 2)))
            g.wait()
            g.add(pool.affine_select(out=ident[:, :], in_=ident[:, :], compare_op=ALU.not_equal, fill=1.0,
                                     base=0, pattern=[[-1, P]], channel_multiplier=1))
            g.add(pool.affine_select(out=before[:, :], in_=before[:, :], compare_op=ALU.is_gt, fill=0.0,
                                     base=0, pattern=[[1, P]], channel_multiplier=-1))
            g.add(pool.affine_select(out=causal[:, :], in_=causal[:, :], compare_op=ALU.is_ge, fill=NEG,
                                     base=0, pattern=[[1, T]], channel_multiplier=-1))
            g.add(pool.affine_select(out=headsel, in_=headsel, compare_op=ALU.not_equal,
                                     fill=1.0, base=0, pattern=[[-1, NH], [0, P]], channel_multiplier=1))
            g.add(pool.iota(iota_i[:, :], [[1, T]], base=0, channel_multiplier=0))
            g.add(pool.iota(row_i[:, :], [[0, 32]], base=0, channel_multiplier=1))
            g.add(pool.memset(V0[:, :, :, DH:DH + 2], 1.0))
            g.wait()
            g.then(pool.tensor_copy(iota[:, :], iota_i[:, :]))
            pool.tensor_scalar(caps[:, :], iota[:, 0:8], float(CAP), float(CAP), ALU.mult, ALU.add)\
                .then_inc(consts, 1)
            for n, (kind, half, s, use) in enumerate(plan0[1:]):
                for h in range(2):
                    q = 2 * n + h
                    part = slice(h * HALF, (h + 1) * HALF)
                    pool.wait_ge(hi_ready, q + 1)
                    pool.tensor_tensor(ring_lo[:, s, part], ring[:, s, part], W_hi[:, q % HI].bitcast(F32),
                                       ALU.subtract).then_inc(lo_ready, 1)
            pool.wait_ge(s5_dve, 1)
            pool.wait_ge(bcast_psum, 2)
            pool.wait_ge(arg_ready, NH)
            pool.wait_ge(done[plan0[-1][2]], plan0[-1][3])
            g.then(pool.tensor_tensor(COS[:, :, :], iota[:, 0:P].unsqueeze(1).to_broadcast([P, S5T, P]),
                                      s5[:, 3, :].unsqueeze(2).to_broadcast([P, S5T, P]), ALU.mult))
            g.then(pool.tensor_copy(SIN[:, :, :].bitcast(I32), COS[:, :, :]))
            g.then(pool.tensor_copy(SIN[:, :, :], SIN[:, :, :].bitcast(I32)))
            pool.tensor_tensor(SIN[:, :, :], COS[:, :, :], SIN[:, :, :], ALU.subtract)\
                .then_inc(phase_ready, 1)

            pool.wait_ge(h_ready, 4)
            pool.memset(A[:, :, :, :], 0.0).then_inc(a_zero, 1)

            def level_arg(l):
                h = LEVELS[l]
                n = NH * T // (2 * h)
                bv = bT.rearrange("p h (n w) -> p (h n) w", w=2 * h)
                ev = LE.rearrange("p h (n w) -> p (h n) w", w=2 * h)
                mid = bv[:, :, h - 1:h].to_broadcast([P, n, h])
                if l == 0:
                    pool.wait_ge(b_ready, NH)
                else:
                    pool.wait_ge(lqk, l)
                g.add(pool.tensor_tensor(ev[:, :, 0:h], mid, bv[:, :, 0:h], ALU.subtract))
                pool.tensor_tensor(ev[:, :, h:2 * h], bv[:, :, h:2 * h], mid, ALU.subtract).then_inc(larg, 1)

            pool.wait_ge(tab_ready, 1)
            for p in range(S5T // 2):
                if p >= FIRST_LEVEL:
                    level_arg(2 * (p - FIRST_LEVEL))
                    level_arg(2 * (p - FIRST_LEVEL) + 1)
                for k in range(2):
                    i = 2 * p + k
                    pool.wait_ge(z_ready, i + 1)
                    if p >= 1:
                        pool.wait_ge(y_psum, p)
                    pool.tensor_tensor(prod[:, 2 * k + 1], zst[:, k], SIN[:, i:i + 1, :].to_broadcast([P, 4, P]),
                                       ALU.mult).then_inc(ps_ready, 1)

        @block.scalar
        def _(act):
            a = Steps(act, act_step)
            sc = nc.scalar
            def norm(k):
                a.add(sc.activation(rms[:, 15:16], cst[:, 1:2], ACT.Sqrt))
                for b in range(NB):
                    j = 2 * k + b
                    if k == 0:
                        act.wait_ge(x_in[b], 16)
                    else:
                        act.wait_ge(h_ready, 2 * (k - 1) + b + 1)
                    junk = XN[:, b, :] if k == 4 else XT[:, 4 * b:4 * b + 4, :].rearrange("p c t -> p (c t)")
                    a.then(sc.activation(junk, H[:, b, :], ACT.Square, accum_out=stat[:, j:j + 1]))
                    sc.activation(rms[:, j:j + 1], stat[:, j:j + 1], ACT.Sqrt, bias=cst[:, 0:1], scale=1.0 / D)\
                        .then_inc(rms_ready, 1)

            def head_rms(k):
                act.wait_ge(hss_ready, k + 1)
                sc.activation(s5[:, 22, 0:8], s5[:, 21, 0:8], ACT.Sqrt, bias=cst[:, 0:1], scale=1.0 / DH)\
                    .then_inc(hrms_ready, 1)

            def moe(layer):
                act.wait_ge(rt_dve, 2 * layer + 1)
                sc.activation(eg, eg, ACT.Exp).then_inc(rt_act, 1)
                act.wait_ge(rt_dve, 2 * layer + 2)
                sc.activation(e2, e2, ACT.Exp).then_inc(rt_act, 1)
                slots, base = moe_use[layer]

                def one(i, sems, n0, wait_gate, wait_down):
                    wait_gate()
                    sc.activation(SG, bank[2][:, 0:FF], ACT.Silu).then_inc(sems.silu, 1)
                    act.wait_ge(sems.down0, i + (n0 + 1))
                    sc.activation(Y[:, 0:512], bank[4][:, :], ACT.Copy).then_inc(sems.y, 1)
                    wait_down()
                    sc.activation(Y[:, 512:1024], bank[5][:, :], ACT.Copy).then_inc(sems.y, 1)

                g_at, d_at = QE - 1, 3 * QE - 1
                with act.Fori(0, NQ) as i:
                    one(i, main, NQ * layer, lambda: act.wait_ge(done[slots[g_at]], i + base[g_at]),
                        lambda: act.wait_ge(done[slots[d_at]], i + base[d_at]))
                act.wait_ge(route_ready, layer + 1)
                n_extra = act.value_load(xid[0:1, XB:XB + 1], min_val=0, max_val=XB)
                with act.If(n_extra > 0):
                    with act.Fori(0, XQ) as i:
                        one(i, extra[layer], 0, lambda: act.wait_ge(xdone[layer], 3 * i + 1),
                            lambda: act.wait_ge(xdone[layer], 3 * i + 3))

            def s5_step():
                act.wait_ge(pt_ready, 1)
                sc.activation(s5[:, 0, :], PT[:, 0:16], ACT.Exp).then_inc(s5_act, 1)

            def s5_parameters():
                act.wait_ge(s5_dve, 1)
                a.add(sc.activation(s5[:, 4, :], s5[:, 3, :], ACT.Sin, scale=TWO_PI))
                a.add(sc.activation(s5[:, 5, :], s5[:, 3, :], ACT.Sin, scale=TWO_PI / 2))
                a.add(sc.activation(s5[:, 17, :], s5[:, 16, :], ACT.Sin, scale=TWO_PI))
                a.add(sc.activation(s5[:, 18, :], s5[:, 16, :], ACT.Sin, scale=TWO_PI / 2))
                a.add(sc.activation(lbc[:, 0:2, :], lbc[:, 0:2, :], ACT.Exp))
                sc.activation(s5[:, 6, :], s5[:, 1, :], ACT.Tanh, scale=0.5).then_inc(s5_act, 1)

            act.wait_ge(consts, 1)
            norm(0)
            for k, w in ((1, norm_ffn[0]), (2, norm_mix[1]), (3, norm_ffn[1])):
                act.dma_start(NW[:, k, :], w.rearrange("(p c) -> p c", p=P)).then_inc(small_in, 16)
            act.dma_start(hnw[:, :], ab_head_norm[0:1, :].to_broadcast([P, W2])).then_inc(small_in, 16)
            act.wait_ge(xt_ready, 4)
            sc.activation(XT_hi, XT[:, :, :], ACT.Copy).then_inc(xt_split, 1)

            def hi(q):
                kind, half, s, use = plan0[1 + q // 2]
                if q % 2 == 0:
                    act.wait_ge(loaded[s], 16 * use)
                if q >= HI:
                    last = q - HI
                    if last % 2 == 0:
                        act.wait_ge(half_used, last // 2 + 1)
                    else:
                        act.wait_ge(done[plan0[1 + last // 2][2]], plan0[1 + last // 2][3])
                sc.activation(W_hi[:, q % HI], ring[:, s, (q % 2) * HALF:(q % 2 + 1) * HALF], ACT.Copy)\
                    .then_inc(hi_ready, 1)

            HALVES = 2 * (len(plan0) - 1)
            for q in range(HI):
                hi(q)
            for n, (kind, half, s, use) in enumerate(plan0):
                if n == 11:
                    head_rms(0)
                if 1 <= n and 2 * n + 1 < HALVES:
                    hi(2 * n + 1)
                if kind == "x":
                    hi(2 * n + 2)
                    continue
                act.wait_ge(done[s], use)
                ps = pairs[n % 2][:, :, 0:T]
                two = slice(2 * half, 2 * half + 2)
                if kind == "q":
                    sc.activation(qT[:, two, :], ps, ACT.Copy).then_inc(copied0, 1)
                elif kind == "k":
                    sc.activation(kT[:, two, :], ps, ACT.Copy, scale=DH ** -0.5).then_inc(copied0, 1)
                elif kind == "v":
                    sc.activation(V0[:, :, two, 0:DH], ps.rearrange("p b (h e) -> p b h e", e=DH),
                                  ACT.Copy).then_inc(copied0, 1)
                elif kind == "o":
                    sc.activation(SO[:, :, half * UC:(half + 1) * UC], ps, ACT.Sigmoid).then_inc(copied0, 1)
                elif kind == "gb":
                    sc.activation(GB[:, two, :], ps, ACT.Copy).then_inc(copied0, 1)
                else:
                    sc.activation(GC[:, two, :], ps, ACT.Copy).then_inc(copied0, 1)
                if 1 <= n and 2 * n + 2 < HALVES:
                    hi(2 * n + 2)
                if n == 0:
                    act.wait_ge(gates_biased, 1)
                    a.then(sc.activation(rows[0:NH, 3], rows[0:NH, 0], ACT.Abs))
                    a.then(sc.activation(rows[0:NH, 3], rows[0:NH, 3], ACT.Exp, scale=-1.0))
                    sc.activation(rows[0:NH, 3], rows[0:NH, 3], ACT.Ln, bias=cst[0:NH, 1:2]).then_inc(softplus, 1)
                if n == 1:
                    s5_step()
                if n == 2:
                    s5_parameters()
                if n == 7:
                    act.wait_ge(cols_ready, 1)
                    sc.activation(em, cols[:, 1], ACT.Exp).then_inc(em_ready, 1)
                    for h in range(NH):
                        act.wait_ge(arg_ready, h + 1)
                        sc.activation(DEC[:, h], DEC[:, h], ACT.Exp).then_inc(decay_ready, 1)
            for b in range(NB):
                act.wait_ge(hT_psum, b + 1)
                sc.activation(MT0[:, 0:NH, b * P:(b + 1) * P], bank[5 + b][:, :].rearrange("p (h t) -> p h t", t=P),
                              ACT.Copy).then_inc(mt_ready, 1)
            act.wait_ge(phase_ready, 1)
            a.then(sc.activation(COS[:, :, :], SIN[:, :, :], ACT.Abs))
            a.add(sc.activation(COS[:, :, :], COS[:, :, :], ACT.Sin, bias=cst[:, 2:3], scale=-TWO_PI))
            sc.activation(SIN[:, :, :], SIN[:, :, :], ACT.Sin, scale=TWO_PI).then_inc(tab_ready, 1)
            norm(1)
            moe(0)
            norm(2)
            act.dma_start(hnw[:, :], hgrn_out_norm[0:1, :].to_broadcast([P, W2])).then_inc(late_in, 16)

            for n, (kind, half, s, use) in enumerate(plan1):
                if n == 4:
                    act.wait_ge(f_ready, 1)
                    sc.activation(FT, FT, ACT.Ln).then_inc(f_log, 1)
                if n >= 6:
                    for l in (2 * (n - 6), 2 * (n - 6) + 1):
                        act.wait_ge(larg, l + 1)
                        sc.activation(LE, LE, ACT.Exp).then_inc(lexp, 1)
                act.wait_ge(done[s], use)
                ps = bank[n % 2][:, :].rearrange("p (g t) -> p g t", g=2)
                two = slice(2 * half, 2 * half + 2)
                if kind == "u":
                    sc.activation(uT[:, two, :], ps, ACT.Copy).then_inc(copied1, 1)
                elif kind == "f":
                    a.add(sc.activation(FT[:, two, :], ps, ACT.Sigmoid))
                    sc.activation(k1T[:, two, :], ps, ACT.Sigmoid, scale=-1.0).then_inc(copied1, 1)
                elif kind == "q":
                    sc.activation(q1T[:, two, :], ps, ACT.Copy).then_inc(copied1, 1)
                elif kind == "i":
                    sc.activation(V1[:, :, two, :], ps.rearrange("p b (h e) -> p b h e", e=DH),
                                  ACT.Copy).then_inc(copied1, 1)
                else:
                    sc.activation(SO1[:, :, half * UC:(half + 1) * UC], ps, ACT.Copy).then_inc(copied1, 1)
            act.wait_ge(copied1, 10)
            sc.activation(SO1, SO1, ACT.Silu).then_inc(so_ready, 1)
            for j in range(NH):
                act.wait_ge(y_ready, j + 1)
                sc.activation(uT[:, j, :], uT[:, j, :], ACT.Gelu_apprx_tanh).then_inc(gelu_ready, 1)
            for b in range(NB):
                act.wait_ge(o_psum, b + 1)
                sc.activation(HN1[:, b], bank[2 + b][:, :].rearrange("p (h e) -> p h e", e=DH), ACT.Copy)\
                    .then_inc(o_ready, 1)
            head_rms(1)
            for j in range(NH):
                if j < 2:
                    act.wait_ge(glu_psum, 1)
                else:
                    act.wait_ge(done[glu_at[0]], glu_at[1])
                sc.activation(glu_gate[:, j, :], bank[j // 2][:, (j % 2) * T:(j % 2 + 1) * T], ACT.Sigmoid,
                              bias=PT[:, 64 + j:65 + j]).then_inc(glu_sig, 1)
            for b in range(NB):
                act.wait_ge(hT_psum, NB + b + 1)
                sc.activation(MT1[:, NH:2 * NH, b * P:(b + 1) * P],
                              bank[2 + b][:, :].rearrange("p (h t) -> p h t", t=P), ACT.Copy).then_inc(mt_ready, 1)
            norm(3)
            act.wait_ge(logitT_psum, 2)
            act.dma_start(fin[:, 0:D], norm_final.rearrange("(o n) -> o n", o=1).to_broadcast([P, D]))\
                .then_inc(late_in, 16)
            moe(1)
            norm(4)
            ov = out[0].rearrange("(b p) n -> p b n", p=P)
            for b in range(NB):
                act.wait_ge(xn_ready, 2 * 4 + b + 1)
                act.dma_start(ov[:, b, :], XN[:, b, :]).then_inc(out_done, 16)
            act.wait_ge(out_done, NB * 16)

        @block.vector
        def _(dve):
            d = Steps(dve, dve_step)
            v = nc.vector

            def norm(k):
                for b in range(NB):
                    j = 2 * k + b
                    dve.wait_ge(rms_ready, j + 1)
                    d.then(v.reciprocal(rinv[:, j:j + 1], rms[:, j:j + 1]))
                    if k < 4:
                        v.tensor_scalar(XN[:, b, :], H[:, b, :], rinv[:, j:j + 1], None, ALU.mult)\
                            .then_inc(xn_ready, 1)
                        continue
                    dve.wait_ge(late_in, 2 * 16)
                    v.scalar_tensor_tensor(out=XN[:, b, :], in0=H[:, b, :], scalar=rinv[:, j:j + 1],
                                           in1=fin[:, 0:D], op0=ALU.mult, op1=ALU.mult).then_inc(xn_ready, 1)
                if k == 4:
                    return
                if k == 0:
                    dve.wait_ge(nw_in, 16)
                elif k == 1:
                    dve.wait_ge(small_in, 4 * 16)
                for b in range(NB):
                    for g in range(2):
                        dve.wait_ge(xt_psum, 4 * k + 2 * b + g + 1)
                        v.tensor_tensor(XT[:, 4 * g:4 * g + 4, b * P:(b + 1) * P],
                                        bank[2 * b + g][:, :].rearrange("p (c t) -> p c t", t=P),
                                        NW[:, k, 4 * g:4 * g + 4].unsqueeze(2).to_broadcast([P, 4, P]), ALU.mult)\
                            .then_inc(xt_ready, 1)

            def head_squares(hn, sq):
                d.then(v.tensor_tensor(sq, hn, hn, ALU.mult))
                v.tensor_reduce(s5[:, 21, 0:8], sq.rearrange("p b h e -> p (b h) e"), AX.X, ALU.add)\
                    .then_inc(hss_ready, 1)

            def head_scale(k, hn, so):
                dve.wait_ge(hrms_ready, k + 1)
                d.then(v.reciprocal(s5[:, 23, 0:8], s5[:, 22, 0:8]))
                h8 = hn.rearrange("p b h e -> p (b h) e")
                d.then(v.tensor_tensor(h8, h8, s5[:, 23, 0:8].unsqueeze(2).to_broadcast([P, NB * NH, DH]), ALU.mult))
                for b in range(NB):
                    hb = hn[:, b].rearrange("p h e -> p (h e)")
                    v.tensor_tensor(hb, hb, so[:, b], ALU.mult).then_inc(hn_ready, 1)

            def gate_weight(so):
                d.then(v.tensor_tensor(so, so, hnw[:, :].unsqueeze(1).to_broadcast([P, NB, W2]), ALU.mult))

            def add_out(first, s, use):
                for b in range(NB):
                    if b == 0:
                        dve.wait_ge(out_psum, first // 4 + 1)
                    else:
                        dve.wait_ge(done[s], use)
                    for n in range(2):
                        hv = H[:, b, n * 512:(n + 1) * 512]
                        ins = v.tensor_tensor(hv, hv, bank[first + 2 * b + n][:, :], ALU.add)
                    ins.then_inc(h_ready, 1)

            def route(layer):
                d.then(v.memset(G8, -3e38))
                dve.wait_ge(logitT_psum, layer + 1)
                v.tensor_copy(LGT[0:NG + E], bank[5][0:NG + E, 0:T]).then_inc(logitT_ready, 1)
                dve.wait_ge(logit_psum, layer + 1)
                d.then(v.tensor_tensor(LG, bank[4][:, 0:NB * (NG + E)].rearrange("p (b n) -> p b n", n=NG + E),
                                       rb[:, layer:layer + 1, :].to_broadcast([P, NB, NG + E]), ALU.add))
                d.then(v.tensor_copy(G8[:, :, 0:NG], LG[:, :, 0:NG]))
                for b in range(NB):
                    d.then(v.max(gmx[:, b], G8[:, b]))
                    d.then(v.max_index(gix[:, b], gmx[:, b], G8[:, b]))
                v.tensor_tensor(eg, LG[:, :, 0:NG], gmx[:, :, 0:1].to_broadcast([P, NB, NG]), ALU.subtract)\
                    .then_inc(rt_dve, 1)
                d.then(v.tensor_copy(ggf, gix[:, :, 0:1]))
                d.then(v.tensor_tensor(goh, iota[:, 0:NG].unsqueeze(1).to_broadcast([P, NB, NG]),
                                       ggf.to_broadcast([P, NB, NG]), ALU.is_equal))
                for b in range(NB):
                    d.then(v.tensor_tensor(selm[:, b], LG[:, b, NG:].rearrange("p (g j) -> p j g", j=EG),
                                          goh[:, b:b + 1, :].to_broadcast([P, EG, NG]), ALU.mult))
                d.then(v.tensor_reduce(SEL, selm, AX.X, ALU.add))
                for b in range(NB):
                    d.then(v.max(smx[:, b], SEL[:, b]))
                    d.then(v.max_index(six[:, b], smx[:, b], SEL[:, b]))
                v.tensor_tensor(e2, smx[:, :, 1:2], smx[:, :, 0:1], ALU.subtract).then_inc(rt_dve, 1)
                for c in range(2):
                    d.then(v.tensor_copy(idc[:, c], six[:, :, c:c + 1]))
                    d.then(v.scalar_tensor_tensor(out=idc[:, c], in0=ggf, scalar=float(EG), in1=idc[:, c],
                                                  op0=ALU.mult, op1=ALU.add))
                    d.then(v.tensor_tensor(MC[:, c], iota[:, 0:E].unsqueeze(1).to_broadcast([P, NB, E]),
                                           idc[:, c].to_broadcast([P, NB, E]), ALU.is_equal))
                v.tensor_tensor(MM, MC[:, 0], MC[:, 1], ALU.add).then_inc(choice_ready, 1)
                dve.wait_ge(pos_psum, layer + 1)
                d.then(v.tensor_copy(pos, bank[5][:, 0:2 * E].rearrange("p (b e) -> p b e", e=E)))
                d.then(v.tensor_copy(cnt, bank[5][:, 2 * E:3 * E]))
                d.then(v.scalar_tensor_tensor(out=posm[:, :, 0:E], in0=pos, scalar=1.0, in1=MM,
                                              op0=ALU.add, op1=ALU.mult))
                d.then(v.tensor_scalar(posm[:, :, 0:E], posm[:, :, 0:E], -1.0, None, ALU.add))

            def choice_weights(layer):
                dve.wait_ge(rt_act, 2 * layer + 2)
                d.then(v.tensor_reduce(gval, eg, AX.X, ALU.add))
                d.then(v.scalar_tensor_tensor(out=gval, in0=e2, scalar=1.0, in1=gval, op0=ALU.add, op1=ALU.mult))
                d.then(v.reciprocal(wt[:, 0], gval))
                d.then(v.tensor_tensor(wt[:, 1], e2, wt[:, 0], ALU.mult))
                for c in range(2):
                    d.then(v.tensor_tensor(t32[:, c], MC[:, c], wt[:, c].to_broadcast([P, NB, E]), ALU.mult))
                d.then(v.tensor_tensor(comb[:, :, 0:E], t32[:, 0], t32[:, 1], ALU.add))

            def further_lists():
                d.then(v.tensor_tensor(over, cnt.unsqueeze(2).to_broadcast([P, E, 8]),
                                       caps[:, :].unsqueeze(1).to_broadcast([P, E, 8]), ALU.is_gt))
                d.then(v.tensor_reduce(nbk, over, AX.X, ALU.add))
                d.then(v.tensor_tensor_scan(endb, ones[:, 0:E], nbk, 0.0, ALU.mult, ALU.add))
                d.then(v.tensor_tensor(nbk, endb, nbk, ALU.subtract))
                for b in range(NB):
                    d.then(v.scalar_tensor_tensor(out=vv[:, b], in0=nbk, scalar=float(CAP), in1=pos[:, b],
                                                 op0=ALU.mult, op1=ALU.add))
                d.then(v.tensor_scalar(t32[:, 0], pos, float(CAP), -1e6, ALU.is_lt, ALU.mult))
                d.then(v.scalar_tensor_tensor(out=vv, in0=vv, scalar=-float(CAP), in1=t32[:, 0],
                                              op0=ALU.add, op1=ALU.add))

            def further_blocks(layer):
                for c in range(2):
                    d.then(v.tensor_tensor(t32[:, c], MC[:, c], vv, ALU.mult))
                    d.then(v.tensor_reduce(gs[:, c], t32[:, c], AX.X, ALU.add))
                    for b in range(NB):
                        d.then(v.scalar_tensor_tensor(out=vk[:, c, b], in0=iota[:, 0:XB], scalar=-float(CAP),
                                                     in1=gs[:, c, b].to_broadcast([P, XB]),
                                                     op0=ALU.mult, op1=ALU.add))
                    d.then(v.tensor_scalar(ink[:, c], vk[:, c], 0.0, None, ALU.is_ge))
                    d.then(v.tensor_scalar(tk[:, c], vk[:, c], float(CAP), None, ALU.is_lt))
                    d.then(v.tensor_tensor(ink[:, c], ink[:, c], tk[:, c], ALU.mult))
                    d.then(v.scalar_tensor_tensor(out=vk[:, c], in0=vk[:, c], scalar=1.0, in1=ink[:, c],
                                                 op0=ALU.add, op1=ALU.mult))
                    d.then(v.tensor_tensor(tk[:, c], ink[:, c], wt[:, c].to_broadcast([P, NB, XB]), ALU.mult))
                d.then(v.scalar_tensor_tensor(out=posm[:, :, E:], in0=vk[:, 0], scalar=-1.0, in1=vk[:, 1],
                                             op0=ALU.add, op1=ALU.add))
                d.then(v.tensor_tensor(comb[:, :, E:], tk[:, 0], tk[:, 1], ALU.add))
                d.then(v.tensor_tensor(eix, endb.unsqueeze(1).to_broadcast([P, XB, E]),
                                       iota[:, 0:XB].unsqueeze(2).to_broadcast([P, XB, E]), ALU.is_le))
                d.then(v.tensor_reduce(exf, eix, AX.X, ALU.add))
                d.then(v.tensor_scalar(xid[:, 0:XB], exf, float(E - 1), None, ALU.min))
                v.tensor_copy(xid[:, XB:XB + 1], endb[:, E - 1:E]).then_inc(route_ready, 1)
                dve.wait_ge(route_ready, layer + 1)

            def moe(layer):
                route(layer)
                slots, base = moe_use[layer]

                def one(i, sems, n0, first, wait_up, routing=False):
                    at = bass.ds(i * QE + first, QE)
                    slot = iota[:, 0:CAP].unsqueeze(1).to_broadcast([P, QE, CAP])
                    for b in range(NB):
                        ins = v.tensor_tensor(S[:, b].rearrange("p (r j) -> p r j", j=CAP), slot,
                                              posm[:, b, at].unsqueeze(2).to_broadcast([P, QE, CAP]), ALU.is_equal)
                    ins.then_inc(sems.onehot, 1)
                    dve.wait_ge(sems.onehot, 2 * i + (2 * n0 + 1))
                    if routing:
                        choice_weights(layer)
                    for b in range(NB):
                        ins = v.tensor_tensor(SW[:, b].rearrange("p (r j) -> p r j", j=CAP),
                                              S[:, b].rearrange("p (r j) -> p r j", j=CAP),
                                              comb[:, b, at].unsqueeze(2).to_broadcast([P, QE, CAP]), ALU.mult)
                    ins.then_inc(sems.onehot, 1)
                    dve.wait_ge(sems.xg_psum, i + (n0 + 1))
                    for g in range(2):
                        ins = v.tensor_tensor(XG[:, 4 * g:4 * g + 4, :],
                                              bank[g][:, :].rearrange("p (c t) -> p c t", t=P),
                                              NW[:, 2 * layer + 1, 4 * g:4 * g + 4].unsqueeze(2)
                                              .to_broadcast([P, 4, P]), ALU.mult)
                    ins.then_inc(sems.xg, 1)
                    if routing:
                        further_lists()
                    dve.wait_ge(sems.q_psum, i + (n0 + 1))
                    v.tensor_copy(Q.rearrange("p b t -> p (b t)"), bank[1][:, 0:T]).then_inc(sems.q, 1)
                    dve.wait_ge(sems.silu, i + (n0 + 1))
                    wait_up()
                    v.tensor_tensor(HID, SG, bank[3][:, 0:FF], ALU.mult).then_inc(sems.hid, 1)
                    dve.wait_ge(sems.ht_psum, i + (n0 + 1))
                    v.tensor_copy(HT.rearrange("p c t -> p (c t)"), bank[0][:, 0:T]).then_inc(sems.ht, 1)
                    if routing:
                        further_blocks(layer)
                    for n in range(2):
                        dve.wait_ge(sems.acc_psum, 2 * i + (2 * n0 + n + 1))
                        for b in range(NB):
                            hv = H[:, b, n * 512:(n + 1) * 512]
                            ins = v.tensor_tensor(hv, hv, bank[(6 if b == 0 else 2) + n][:, :], ALU.add)
                        ins.then_inc(sems.added, 1)

                u_at = 2 * QE - 1
                one(0, main, NQ * layer, 0, lambda: dve.wait_ge(done[slots[u_at]], base[u_at]), True)
                with dve.Fori(1, NQ) as i:
                    one(i, main, NQ * layer, 0, lambda: dve.wait_ge(done[slots[u_at]], i + base[u_at]))
                dve.wait_ge(main.added, 2 * NQ * (layer + 1))
                n_extra = dve.value_load(xid[0:1, XB:XB + 1], min_val=0, max_val=XB)
                with dve.If(n_extra > 0):
                    with dve.Fori(0, XQ) as i:
                        one(i, extra[layer], 0, E, lambda: dve.wait_ge(xdone[layer], 3 * i + 2))
                    dve.wait_ge(extra[layer].added, 2 * XQ)
                v.memset(stat[:, 15:16], 0.0).then_inc(h_ready, NB)

            dve.wait_ge(consts, 1)
            norm(0)
            dve.wait_ge(gates_psum, 1)
            d.then(v.tensor_scalar(rows[0:NH, 1, :], bank[4][0:NH, 0:T], gbias[0:NH, 0:1], None, ALU.add))
            d.then(v.tensor_copy(rows[0:NH, 0, :], bank[4][32:32 + NH, 0:T]))
            v.tensor_scalar(rows[0:NH, 0, :], rows[0:NH, 0, :], gbias[0:NH, 1:2], None, ALU.add)\
                .then_inc(gates_biased, 1)
            dve.wait_ge(lam_in, 9 * 16)
            for g in range(2):
                ins = v.tensor_copy(prow[0:S5T, 64 * g:64 * g + 64], logdt[:, g:g + 1].to_broadcast([S5T, 64]))
            ins.then_inc(prow_ready, 1)
            dve.wait_ge(xt_split, 1)
            dve.wait_ge(done[plan0[0][2]], plan0[0][3])
            v.tensor_tensor(XT_lo[:, :, :], XT[:, :, :], XT_hi.bitcast(F32), ALU.subtract).then_inc(xt_split, 1)
            dve.wait_ge(pt_psum, 1)
            v.tensor_copy(PT[:, :], bank[7][:, 0:76]).then_inc(pt_ready, 1)
            dve.wait_ge(pt_ready, 1)
            re, im = PT[:, 16:32], PT[:, 32:48]
            lbp = PT[:, 68:76].rearrange("p (l j) -> p l j", l=2)
            d.then(v.tensor_tensor(lbc[:, 2, :], lbp[:, 0], lbp[:, 1], ALU.max))
            d.then(v.tensor_tensor(lbc[:, 0:2, :], lbp, lbc[:, 2:3, :].to_broadcast([P, 2, NH]), ALU.subtract))
            dve.wait_ge(s5_act, 1)
            d.then(v.tensor_tensor(s5[:, 1, :], re, s5[:, 0, :], ALU.mult))
            d.then(v.tensor_tensor(s5[:, 2, :], im, s5[:, 0, :], ALU.mult))
            d.then(v.tensor_scalar(s5[:, 2, :], s5[:, 2, :], float(1.0 / (2 * np.pi)), None, ALU.mult))
            d.then(v.tensor_copy(s5[:, 7, :].bitcast(I32), s5[:, 2, :]))
            d.then(v.tensor_tensor(s5[:, 3, :], s5[:, 2, :], s5[:, 7, :].bitcast(I32), ALU.subtract))
            d.then(v.tensor_scalar(s5[:, 15, :], s5[:, 3, :], float(P), None, ALU.mult))
            d.then(v.tensor_copy(s5[:, 7, :].bitcast(I32), s5[:, 15, :]))
            v.tensor_tensor(s5[:, 16, :], s5[:, 15, :], s5[:, 7, :].bitcast(I32), ALU.subtract).then_inc(s5_dve, 1)
            dve.wait_ge(softplus, 1)
            r4 = rows[0:NH]
            d.then(v.memset(r4[:, 5, :], 1.0))
            d.then(v.scalar_tensor_tensor(out=r4[:, 0, :], in0=r4[:, 0, :], scalar=0.0, in1=r4[:, 3, :],
                                          op0=ALU.min, op1=ALU.subtract))
            d.then(v.tensor_tensor_scan(r4[:, 2, :], r4[:, 5, :], r4[:, 0, :], 0.0, ALU.mult, ALU.add))
            d.then(v.tensor_tensor(r4[:, 3, :], r4[:, 1, :], r4[:, 2, :], ALU.subtract))
            d.then(v.tensor_tensor_scan(r4[:, 4, :], r4[:, 3, :], r4[:, 3, :], NEG, ALU.max, ALU.max))
            d.then(v.tensor_scalar(r4[:, 4, :], r4[:, 4, :], -1.0, None, ALU.mult))
            v.tensor_tensor(r4[:, 5, :], r4[:, 4, :], r4[:, 2, :], ALU.subtract).then_inc(rows_ready, 1)

            dve.wait_ge(s5_act, 2)
            col = [s5[:, k, :] for k in range(24)]
            d.then(v.tensor_scalar(col[7], col[6], -1.0, 1.0, ALU.mult, ALU.add))
            d.then(v.tensor_tensor(col[5], col[5], col[5], ALU.mult))
            d.then(v.reciprocal(col[7], col[7]))
            d.then(v.tensor_scalar(col[5], col[5], 2.0, None, ALU.mult))
            d.then(v.scalar_tensor_tensor(out=col[8], in0=col[6], scalar=1.0, in1=col[7], op0=ALU.add, op1=ALU.mult))
            d.then(v.scalar_tensor_tensor(out=col[9], in0=col[6], scalar=2.0, in1=col[7], op0=ALU.mult, op1=ALU.mult))
            d.then(v.tensor_scalar(col[10], col[5], -1.0, 1.0, ALU.mult, ALU.add))
            d.then(v.tensor_tensor(col[9], col[9], col[10], ALU.mult))
            d.then(v.tensor_tensor(col[9], col[9], col[5], ALU.subtract))
            d.then(v.tensor_tensor(col[11], col[8], col[4], ALU.mult))
            d.then(v.tensor_tensor(col[12], re, re, ALU.mult))
            d.then(v.tensor_tensor(col[13], im, im, ALU.mult))
            d.then(v.tensor_tensor(col[12], col[12], col[13], ALU.add))
            d.then(v.reciprocal(col[12], col[12]))
            d.then(v.tensor_tensor(col[13], col[9], re, ALU.mult))
            d.then(v.tensor_tensor(col[14], col[11], im, ALU.mult))
            d.then(v.tensor_tensor(col[15], col[11], re, ALU.mult))
            d.then(v.tensor_tensor(col[19], col[9], im, ALU.mult))
            d.then(v.tensor_tensor(col[13], col[13], col[14], ALU.add))
            d.then(v.tensor_tensor(col[14], col[15], col[19], ALU.subtract))
            d.then(v.tensor_tensor(col[13], col[13], col[12], ALU.mult))
            d.then(v.tensor_tensor(col[14], col[14], col[12], ALU.mult))
            d.then(v.tensor_tensor(col[18], col[18], col[18], ALU.mult))
            d.then(v.tensor_scalar(col[18], col[18], -2.0, 1.0, ALU.mult, ALU.add))
            cr = col[13].unsqueeze(2).to_broadcast([P, S5T, GCH])
            ci = col[14].unsqueeze(2).to_broadcast([P, S5T, GCH])
            tmp = shaped(BZ.rearrange("p a b c d -> p (a b c d)")[:, 0:S5T * GCH], S5T, GCH)
            dve.wait_ge(bc_in, 6 * 16)
            d.then(v.tensor_tensor(bbar[:, 0], bnat[:, 0], cr, ALU.mult))
            d.then(v.tensor_tensor(tmp, bnat[:, 1], ci, ALU.mult))
            d.then(v.tensor_tensor(bbar[:, 0], bbar[:, 0], tmp, ALU.subtract))
            d.then(v.tensor_tensor(bbar[:, 1], bnat[:, 1], cr, ALU.mult))
            d.then(v.tensor_tensor(tmp, bnat[:, 0], ci, ALU.mult))
            d.then(v.tensor_tensor(bbar[:, 1], bbar[:, 1], tmp, ALU.add))
            d.then(v.memset(BZ.rearrange("p a b c d -> p (a b c d)"), 0.0))
            for k in range(2):
                for g in range(2):
                    half = slice(64 * g, 64 * g + 64)
                    d.then(v.tensor_copy(BZ[half, k, :, g, :], bbar[half, k]))
            par = mtmp[:, 0, 0:2].bitcast(I32)
            d.then(v.tensor_scalar(par, row_i[:, 0:2], 4, 1, ALU.logical_shift_right, ALU.bitwise_and))
            d.then(v.tensor_copy(chmask[:, 0:2], par))
            d.then(v.tensor_scalar(chmask[:, 0:1], chmask[:, 0:1], -1.0, 1.0, ALU.mult, ALU.add))
            for k in range(2):
                for g in range(2):
                    ins = v.tensor_scalar(CZ[:, k, :, g, :], cnat[:, k], chmask[:, g:g + 1], None, ALU.mult)
                    if k == 1 and g == 1:
                        ins.then_inc(bz_ready, 1)
                    else:
                        d.then(ins)
            for k in range(2):
                dve.wait_ge(bct_psum, k + 1)
                v.tensor_copy(BT[:, k], bank[5 + k][:, :].rearrange("p (j s) -> p j s", s=P)).then_inc(bct_ready, 1)
            dve.wait_ge(bct_psum, 3)
            d.then(v.tensor_copy(CT[:, 0], bank[7][:, :].rearrange("p (j s) -> p j s", s=P)))
            v.tensor_scalar(CT[:, 1], bank[7][:, :].rearrange("p (j s) -> p j s", s=P), -1.0, None, ALU.mult)\
                .then_inc(bct_ready, 1)
            dve.wait_ge(bct_psum, 4)
            v.tensor_scalar(CT[:, 2], bank[5][:, :].rearrange("p (j s) -> p j s", s=P), -1.0, None, ALU.mult)\
                .then_inc(bct_ready, 1)
            d.then(v.tensor_tensor(lbc[:, 2, :], lbc[:, 0, :], lbc[:, 1, :], ALU.add))
            d.then(v.reciprocal(lbc[:, 2, :], lbc[:, 2, :]))
            d.then(v.tensor_tensor(lbc[:, 0:2, :], lbc[:, 0:2, :], lbc[:, 2:3, :].to_broadcast([P, 2, NH]), ALU.mult))
            d.then(v.tensor_tensor(lbc[:, 2, :], lbc[:, 0, :], lbc[:, 1, :], ALU.add))
            d.then(v.tensor_tensor(lbc[:, 2, :], lbc[:, 2, :], lbc[:, 0, :], ALU.subtract))
            d.then(v.tensor_scalar(lbc[:, 3, :], lbc[:, 2, :], -1.0, 1.0, ALU.mult, ALU.add))
            mi = [mtmp[:, k, :].bitcast(I32) for k in range(6)]
            mf = [mtmp[:, k, :] for k in range(6)]
            d.then(v.tensor_tensor(mi[0], row_i[:, :], iota_i[:, 0:32], ALU.bitwise_xor))
            d.then(v.tensor_scalar(mi[0], mi[0], 31, None, ALU.bitwise_and))
            d.then(v.tensor_scalar(mi[1], row_i[:, :], 31, None, ALU.bitwise_and))
            d.then(v.tensor_copy(mf[2], mi[0]))
            d.then(v.tensor_copy(mf[3], mi[1]))
            d.then(v.tensor_tensor(mf[3], iota[:, 0:32], mf[3], ALU.subtract))
            d.then(v.tensor_scalar(mf[4], mf[3], 0.0, None, ALU.is_gt))
            d.then(v.tensor_scalar(mf[5], mf[3], 0.0, None, ALU.is_lt))
            d.then(v.tensor_tensor(mf[2], mf[2], mf[4], ALU.mult))
            d.then(v.tensor_tensor(mf[2], mf[2], mf[5], ALU.subtract))
            for k, (lo, hi) in enumerate([(h, 2 * h) for h in LEVELS[3:]] + [(0, 1)]):
                d.then(v.tensor_scalar(mf[3], mf[2], float(lo), None, ALU.is_ge))
                d.then(v.tensor_scalar(mf[4], mf[2], float(hi), None, ALU.is_lt))
                d.then(v.tensor_tensor(lvl_mask[:, k, :], mf[3], mf[4], ALU.mult))

            dve.wait_ge(cols_psum, 1)
            v.tensor_copy(cols.rearrange("p k b h -> p (k b h)"), bank[4][:, 0:4 * NH]).then_inc(cols_ready, 1)
            dve.wait_ge(cols_ready, 1)
            for h in range(NH):
                dve.wait_ge(bcast_psum, h // 2 + 1)
                nm = bank[5 + h // 2][:, (h % 2) * T:(h % 2 + 1) * T]
                d.then(v.scalar_tensor_tensor(out=DEC[:, h, 0:T], in0=nm, scalar=cols[:, 0, 0, h:h + 1],
                                             in1=causal[:, :], op0=ALU.add, op1=ALU.add))
                v.scalar_tensor_tensor(out=DEC[:, h, T:T + P], in0=nm[:, P:T], scalar=cols[:, 0, 1, h:h + 1],
                                       in1=causal[:, 0:P], op0=ALU.add, op1=ALU.add).then_inc(arg_ready, 1)
            for h in range(NH):
                dve.wait_ge(decay_ready, h + 1)
                dve.wait_ge(scores_psum, h + 1)
                v.tensor_tensor(DEC[:, h], DEC[:, h], bank[7 if h % 2 == 0 else 4][:, 0:3 * P], ALU.mult)\
                    .then_inc(weights_ready, 1)
            dve.wait_ge(em_ready, 1)
            for n, (b, hp) in enumerate(((0, 0), (0, 1), (1, 0), (1, 1))):
                dve.wait_ge(num_psum, n + 1)
                ps = bank[(5, 6, 7, 4)[n]][:, 0:2 * (DH + 2)].rearrange("p (h e) -> p h e", e=DH + 2)
                dn = den[:, b, 2 * hp:2 * hp + 2].unsqueeze(2)
                eh = em[:, b, 2 * hp:2 * hp + 2].unsqueeze(2)
                d.then(v.tensor_copy(dn, ps[:, :, DH:DH + 1]))
                d.then(v.scalar_tensor_tensor(out=eh, in0=dn, scalar=-1.0, in1=eh, op0=ALU.mult, op1=ALU.max))
                d.then(v.tensor_tensor(dn, dn, eh, ALU.max))
                d.then(v.reciprocal(dn, dn))
                d.then(v.tensor_tensor(HN[:, b, 2 * hp:2 * hp + 2, :], ps[:, :, 0:DH],
                                      dn.to_broadcast([P, 2, DH]), ALU.mult))
            head_squares(HN, SQ)
            d.then(v.memset(conv_in[:, :, 0:2], 0.0))
            dve.wait_ge(copied0, 10)
            for half, (kind, hf, s, use) in enumerate(plan0[10:12]):
                dve.wait_ge(done[s], use)
                two = slice(2 * half, 2 * half + 2)
                v.tensor_tensor(conv_in[:, two, 2:], pairs[half][:, :, 0:T], GC[:, two, :], ALU.mult)\
                    .then_inc(x_used, 1)
            dve.wait_ge(x_used, 2)
            for j in range(NH):
                d.then(v.tensor_scalar(GC[:, j, :], conv_in[:, j, 0:T], PT[:, 48 + j:49 + j], None, ALU.mult))
                for k in (1, 2):
                    d.then(v.scalar_tensor_tensor(out=GC[:, j, :], in0=conv_in[:, j, k:k + T],
                                                  scalar=PT[:, 48 + 4 * k + j:49 + 4 * k + j], in1=GC[:, j, :],
                                                  op0=ALU.mult, op1=ALU.add))
                v.tensor_tensor(MT0[:, NH + j, :], GC[:, j, :], GB[:, j, :], ALU.mult).then_inc(conv_ready, 1)
            dve.wait_ge(copied0, 12)
            dve.wait_ge(small_in, 4 * 16)
            gate_weight(SO)
            head_scale(0, HN, SO)
            add_out(0, *outs0[-1][1:])
            norm(1)
            moe(0)
            norm(2)

            dve.wait_ge(a_zero, 1)
            dve.wait_ge(tab_ready, 1)
            d.then(v.memset(AD, 0.0))

            def level_copy(l):
                dve.wait_ge(lpsum, l + 1)
                ps = bank[2 + l % 2]
                if l == 0:
                    ins = v.tensor_copy(A[:, :, 1, :], ps[:, :].rearrange("p (h t) -> p h t", t=P))
                elif l == 1:
                    for b in range(NB):
                        ins = v.tensor_copy(A[0:64, :, 2 * b, 64:P],
                                            ps[0:64, :].rearrange("p (h b t) -> p h b t", b=NB, t=64)[:, :, b])
                elif l == 2:
                    for i in range(2):
                        r = slice(64 * i, 64 * i + 32)
                        for b in range(NB):
                            ins = v.tensor_copy(A[r, :, 2 * b, 64 * i + 32:64 * i + 64],
                                                ps[r, 0:T].rearrange("p (h b t) -> p h b t", b=NB, t=32)[:, :, b])
                else:
                    ins = v.copy_predicated(AD, lvl_mask[:, l - 3:l - 2, :].to_broadcast([P, NH * NB, 32]),
                                            ps[:, 0:T].rearrange("p (n t) -> p n t", t=32))
                ins.then_inc(lcopied, 1)
                dve.wait_ge(lcopied, l + 1)

            def level_scale(l):
                h = LEVELS[l]
                dve.wait_ge(lexp, l + 1)
                cutup = lambda t: t.rearrange("p h (n w) -> p (h n) w", w=2 * h)
                d.then(v.tensor_tensor(cutup(QK)[:, :, 0:h], cutup(k1T)[:, :, 0:h], cutup(LE)[:, :, 0:h], ALU.mult))
                v.tensor_tensor(cutup(QK)[:, :, h:2 * h], cutup(q1T)[:, :, h:2 * h], cutup(LE)[:, :, h:2 * h],
                                ALU.mult).then_inc(lqk, 1)

            def s5_states(p):
                m = [0, 0]
                bu = [bank[4 + k][:, :].rearrange("p (k t) -> p k t", t=P) for k in range(2)]
                cs = [COS[:, i:i + 1, :].to_broadcast([P, 4, P]) for i in (2 * p, 2 * p + 1)]
                sn = [SIN[:, i:i + 1, :].to_broadcast([P, 4, P]) for i in (2 * p, 2 * p + 1)]
                rho = [s5[:, 8, i:i + 1].to_broadcast([P, P]) for i in (2 * p, 2 * p + 1)]
                for k in range(2):
                    dve.wait_ge(bu_psum, 2 * p + k + 1)
                    m[k] = d.add(v.tensor_tensor(mod[:, k], bu[k], sn[k], ALU.mult))
                for k in range(2):
                    if p >= 1:
                        dve.wait_ge(pc_ready, 2 * p)
                        dve.wait_ge(ps_ready, 2 * p)
                    v.tensor_tensor(zst[:, k], bu[k], cs[k], ALU.mult).then_inc(bu_used, 1)
                for k in range(2):
                    d.wait(m[k])
                    dve.wait_ge(bu_used, 2 * p + k + 1)
                    m[k] = d.add(v.tensor_tensor(zst[:, k, 0:2], zst[:, k, 0:2], mod[:, k, 2:4], ALU.add))
                for k in range(2):
                    d.wait(m[k])
                    m[k] = d.add(v.tensor_tensor(zst[:, k, 2:4], zst[:, k, 2:4], mod[:, k, 0:2], ALU.subtract))
                for q in (0, 2):
                    for k in range(2):
                        d.wait(m[k])
                        m[k] = d.add(v.tensor_tensor_scan(zst[:, k, q], rho[k], zst[:, k, q], 0.0, ALU.mult, ALU.add))
                return m

            def s5_products(p, m):
                zr, zi = [zst[:, k, 0, P - 1:P] for k in range(2)], [zst[:, k, 2, P - 1:P] for k in range(2)]
                c128, s128 = [[s5[:, c, 2 * p + k:2 * p + k + 1] for k in range(2)] for c in (18, 17)]
                for k in range(2):
                    d.wait(m[k])
                    d.add(v.tensor_tensor(zin[:, k, 0:1], zi[k], s128[k], ALU.mult))
                    m[k] = d.add(v.tensor_tensor(zin[:, k, 1:2], zr[k], s128[k], ALU.mult))
                for k in range(2):
                    d.wait(m[k])
                    d.add(v.scalar_tensor_tensor(out=zin[:, k, 2:3], in0=zr[k], scalar=c128[k],
                                                 in1=zin[:, k, 0:1], op0=ALU.mult, op1=ALU.subtract))
                    m[k] = d.add(v.scalar_tensor_tensor(out=zin[:, k, 3:4], in0=zi[k], scalar=c128[k],
                                                        in1=zin[:, k, 1:2], op0=ALU.mult, op1=ALU.add))
                rho = [s5[:, 8, i:i + 1].to_broadcast([P, P]) for i in (2 * p, 2 * p + 1)]
                for k in range(2):
                    d.wait(m[k])
                    m[k] = d.add(v.tensor_tensor_scan(zst[:, k, 1], rho[k], zst[:, k, 1], zin[:, k, 2:3],
                                                      ALU.mult, ALU.add))
                    v.tensor_tensor_scan(zst[:, k, 3], rho[k], zst[:, k, 3], zin[:, k, 3:4], ALU.mult, ALU.add)\
                        .then_inc(z_ready, 1)
                if p >= 1:
                    dve.wait_ge(y_psum, p)
                for k in range(2):
                    d.wait(m[k])
                    dve.wait_ge(z_ready, 2 * p + k + 1)
                    v.tensor_tensor(prod[:, 2 * k], zst[:, k], COS[:, 2 * p + k:2 * p + k + 1, :]
                                    .to_broadcast([P, 4, P]), ALU.mult).then_inc(pc_ready, 1)

            def s5_skip(j):
                dve.wait_ge(y_psum, 2 * j + 2)
                v.scalar_tensor_tensor(out=uT[:, j, :], in0=uT[:, j, :], scalar=PT[:, 60 + j:61 + j],
                                       in1=bank[6 + j % 2][:, 0:T], op0=ALU.mult, op1=ALU.add).then_inc(y_ready, 1)

            def level_step(l):
                if l >= 1:
                    level_copy(l - 1)
                level_scale(l)

            for p in range(S5T // 2):
                marks = s5_states(p)
                if p % 2 == 0 and p > 0:
                    s5_skip(p // 2 - 1)
                if p == 2:
                    dve.wait_ge(copied1, 4)
                    for h in range(NH):
                        d.add(v.tensor_scalar(k1T[:, h, :], k1T[:, h, :], lbc[:, 3, h:h + 1], None, ALU.mult))
                        ins = v.tensor_scalar(FT[:, h, :], FT[:, h, :], lbc[:, 3, h:h + 1], lbc[:, 2, h:h + 1],
                                              ALU.mult, ALU.add)
                    ins.then_inc(f_ready, 1)
                if p == 3:
                    dve.wait_ge(f_log, 1)
                    for h in range(NH):
                        v.tensor_tensor_scan(bT[:, h, :], ones[:, 0:1].to_broadcast([P, T]), FT[:, h, :], 0.0,
                                             ALU.mult, ALU.add).then_inc(b_ready, 1)
                if p == FIRST_LEVEL:
                    dve.wait_ge(copied1, 6)
                if p >= FIRST_LEVEL:
                    level_step(2 * (p - FIRST_LEVEL))
                s5_products(p, marks)
                if p >= FIRST_LEVEL:
                    level_step(2 * (p - FIRST_LEVEL) + 1)
            s5_skip(3)
            dve.wait_ge(so_ready, 1)
            dve.wait_ge(late_in, 16)
            gate_weight(SO1)
            level_copy(7)
            level_copy(8)
            for i in range(4):
                r = slice(32 * i, 32 * i + 32)
                for b in range(NB):
                    ins = v.tensor_copy(A[r, :, 2 * b, r], AD.rearrange("p (h b) t -> p h b t", b=NB)[r, :, b])
            ins.then_inc(a_full, 1)
            dve.wait_ge(o_ready, 2)
            head_squares(HN1, SQ1)
            head_scale(1, HN1, SO1)
            for j in range(NH):
                dve.wait_ge(glu_sig, j + 1)
                v.tensor_tensor(MT1[:, j, :], uT[:, j, :], glu_gate[:, j, :], ALU.mult).then_inc(ys5_ready, 1)
            add_out(4, *outs1[-1][1:])
            norm(3)
            moe(1)
            norm(4)

        @block.tensor
        def _(pe):
            mm, tp = nc.tensor.matmul, nc.tensor.transpose

            def norm(k):
                for b in range(NB):
                    pe.wait_ge(xn_ready, 2 * k + b + 1)
                    xc = XN[:, b, :].rearrange("p (q c) -> p c q", c=KC)
                    for g in range(2):
                        for c in range(4):
                            ins = tp(bank[2 * b + g][:, c * P:(c + 1) * P], xc[:, 4 * g + c, :], ident[:, :])
                        ins.then_inc(xt_psum, 1)

            def unit(s, use):
                pe.wait_ge(loaded[s], 16 * use)
                return ring[:, s, :]

            def project(ps, s, use, transposed, halves=(0, 1)):
                w = (unit(s, use) if 0 in halves else ring[:, s, :]).rearrange("p (c n) -> p c n", c=KC)
                for g in halves:
                    for c in range(KC):
                        if transposed:
                            ins = mm(ps[g], w[:, c, g * P:(g + 1) * P], XT[:, c, :],
                                     start=c == 0, stop=c == KC - 1)
                        else:
                            ins = mm(ps[g], XT[:, c, g * P:(g + 1) * P], w[:, c, :],
                                     start=c == 0, stop=c == KC - 1)
                if 1 in halves:
                    ins.then_inc(done[s], 1)

            def halves_of(ps):
                return [ps[:, 0:T], ps[:, T:2 * T]]

            def out_unit(first, pair, s, use, start, stop):
                w = unit(s, use).rearrange("p (k n) -> p k n", k=2)
                for b in range(NB):
                    for k in range(2):
                        for n in range(2):
                            ins = mm(bank[first + 2 * b + n][:, :], (MT1 if first else MT0)[:, 2 * pair + k, b * P:(b + 1) * P],
                                     w[:, k, n * 512:(n + 1) * 512], start=start and k == 0, stop=stop and k == 1)
                    if stop and b == 0:
                        ins.then_inc(out_psum, 1)
                ins.then_inc(done[s], 1)

            def head_transposes(k, hn, first):
                for b in range(NB):
                    pe.wait_ge(hn_ready, NB * k + b + 1)
                    for h in range(NH):
                        ins = tp(bank[first + b][:, h * P:(h + 1) * P], hn[:, b, h, :], ident[:, :])
                    ins.then_inc(hT_psum, 1)

            def route(layer):
                k = 2 * layer + 1
                pe.wait_ge(xt_ready, 4 * k + 4)
                pe.wait_ge(wr_in, 8 * 16)
                for c in range(KC):
                    ins = mm(bank[5][0:NG + E, 0:T], wr[:, layer, c, :], XT[:, c, :], start=c == 0, stop=c == KC - 1)
                ins.then_inc(logitT_psum, 1)
                pe.wait_ge(logitT_ready, layer + 1)
                for b in range(NB):
                    ins = tp(bank[4][:, b * (NG + E):(b + 1) * (NG + E)], LGT[0:NG + E, b * P:(b + 1) * P],
                             ident[0:NG + E, 0:NG + E])
                ins.then_inc(logit_psum, 1)
                pe.wait_ge(choice_ready, layer + 1)
                mm(bank[5][:, 0:E], before[:, :], MM[:, 0], start=True, stop=True)
                mm(bank[5][:, E:2 * E], before[:, :], MM[:, 1], start=True, stop=False)
                mm(bank[5][:, E:2 * E], ones[:, :], MM[:, 0], start=False, stop=True)
                mm(bank[5][:, 2 * E:3 * E], ones[:, :], MM[:, 0], start=True, stop=False)
                mm(bank[5][:, 2 * E:3 * E], ones[:, :], MM[:, 1], start=False, stop=True).then_inc(pos_psum, 1)

            def moe(layer):
                route(layer)
                slots, base = moe_use[layer]

                def one(i, sems, n0, wait_loaded, finish):
                    cols_of = [slice(r * CAP, (r + 1) * CAP) for r in range(QE)]
                    pe.wait_ge(sems.onehot, 2 * i + (2 * n0 + 1))
                    xc = XN[:, :, :].rearrange("p b (q c) -> p b c q", c=KC)
                    for c in range(KC):
                        for b in range(NB):
                            ins = mm(bank[c // 4][:, (c % 4) * P:(c % 4 + 1) * P], xc[:, b, c, :], S[:, b],
                                     start=b == 0, stop=b == NB - 1)
                    ins.then_inc(sems.xg_psum, 1)
                    pe.wait_ge(sems.xg, i + (n0 + 1))
                    for k in range(2):
                        for r in range(QE):
                            wait_loaded(k, r)
                        for c in range(KC):
                            for r in range(QE):
                                w = ring[:, slots[k * QE + r], :].rearrange("p (c n) -> p c n", c=KC)
                                ins = mm(bank[2 + k][cols_of[r], 0:FF], XG[:, c, cols_of[r]], w[:, c, :],
                                         start=c == 0, stop=c == KC - 1)
                                if c == KC - 1:
                                    finish(ins, k, r)
                        if k == 0:
                            pe.wait_ge(sems.onehot, 2 * i + (2 * n0 + 2))
                            for b in range(NB):
                                ins = tp(bank[1][:, b * P:(b + 1) * P], SW[:, b], ident[:, :])
                            ins.then_inc(sems.q_psum, 1)
                    pe.wait_ge(sems.hid, i + (n0 + 1))
                    hc = HID.rearrange("p (q c) -> p c q", c=2)
                    for c in range(2):
                        ins = tp(bank[0][:, c * P:(c + 1) * P], hc[:, c, :], ident[:, :])
                    ins.then_inc(sems.ht_psum, 1)
                    pe.wait_ge(sems.ht, i + (n0 + 1))
                    for r in range(QE):
                        wait_loaded(2, r)
                    for n in range(2):
                        for c in range(2):
                            for r in range(QE):
                                w = ring[:, slots[2 * QE + r], :].rearrange("p (c n) -> p c n", c=2)
                                ins = mm(bank[4 + n][cols_of[r], :], HT[:, c, cols_of[r]],
                                         w[:, c, n * 512:(n + 1) * 512], start=c == 0, stop=c == 1)
                                if n == 1 and c == 1:
                                    finish(ins, 2, r)
                        if n == 0:
                            ins.then_inc(sems.down0, 1)
                    pe.wait_ge(sems.q, i + (n0 + 1))
                    for n in range(2):
                        pe.wait_ge(sems.y, 2 * i + (2 * n0 + n + 1))
                        for b in range(NB):
                            ins = mm(bank[(6 if b == 0 else 2) + n][:, :], Q[:, b], Y[:, n * 512:(n + 1) * 512],
                                     start=True, stop=True)
                        ins.then_inc(sems.acc_psum, 1)

                with pe.Fori(0, NQ) as i:
                    one(i, main, NQ * layer,
                        lambda k, r: pe.wait_ge(loaded[slots[k * QE + r]], 16 * i + 16 * base[k * QE + r]),
                        lambda ins, k, r: ins.then_inc(done[slots[k * QE + r]], 1))
                pe.wait_ge(route_ready, layer + 1)
                n_extra = pe.value_load(xid[0:1, XB:XB + 1], min_val=0, max_val=XB)
                with pe.If(n_extra > 0):
                    with pe.Fori(0, XQ) as i:
                        one(i, extra[layer], 0,
                            lambda k, r: pe.wait_ge(xloaded[layer], 48 * QE * i + 48 * QE) if k == 0 and r == 0 else None,
                            lambda ins, k, r: ins.then_inc(xdone[layer], 1) if r == QE - 1 else None)

            pe.wait_ge(consts, 1)
            norm(0)
            pe.wait_ge(xt_ready, 4)
            pe.wait_ge(wg_in, 3 * 16)
            for c in range(KC):
                for k in range(2):
                    ins = mm(bank[4][32 * k:32 * k + NH, 0:T], wg[:, c, k * NH:(k + 1) * NH], XT[:, c, :],
                             start=c == 0, stop=c == KC - 1)
            ins.then_inc(gates_psum, 1)

            def project_parts(ps, n, s, transposed):
                for h in range(2):
                    q = 2 * (n - 1) + h
                    pe.wait_ge(lo_ready, q + 1)
                    w_hi = W_hi[:, q % HI].rearrange("p (c n) -> p c n", n=UC)
                    w_lo = ring_lo[:, s, h * HALF:(h + 1) * HALF].rearrange("p (c n) -> p c n", n=UC)
                    for c in range(KC // 2):
                        cx = h * (KC // 2) + c
                        for g in range(2):
                            for m, (w, xt) in enumerate(((w_hi, XT_hi), (w_hi, XT_lo), (w_lo, XT_hi))):
                                wt, xs = w[:, c, g * P:(g + 1) * P], xt[:, cx, :]
                                if not transposed:
                                    wt, xs = xt[:, cx, g * P:(g + 1) * P], w[:, c, :]
                                ins = mm(ps[g], wt, xs, start=cx == 0 and m == 0,
                                         stop=cx == KC - 1 and m == 2)
                    ins.then_inc(half_used if h == 0 else done[s], 1)

            for n, (kind, half, s, use) in enumerate(plan0):
                ps = [pairs[n % 2][:, g, 0:T] for g in range(2)]
                if n >= 12:
                    pe.wait_ge(x_used, n - 11)
                elif n >= 2:
                    pe.wait_ge(copied0, n - 1)
                if n == 0:
                    project(ps, s, use, True)
                else:
                    if n == 1:
                        pe.wait_ge(xt_split, 2)
                    project_parts(ps, n, s, kind not in "vo")
                if n == 0:
                    pe.wait_ge(lam_in, 9 * 16)
                    pe.wait_ge(prow_ready, 1)
                    tp(bank[7][:, 0:76], prow[0:76, :], ident[0:76, 0:76]).then_inc(pt_psum, 1)
                if n == 5:
                    pe.wait_ge(bz_ready, 1)
                    pe.wait_ge(pt_ready, 1)
                    for k in range(3):
                        m = BZ[:, k].rearrange("p (j r) a c -> p j (r a c)", r=4) if k < 2 else \
                            CZ[:, 0].rearrange("p j a s -> p j (a s)")
                        for j in range(NH):
                            ins = tp(bank[5 + k][:, j * P:(j + 1) * P], m[:, j, :], ident[:, :])
                        ins.then_inc(bct_psum, 1)
                if n == 6:
                    pe.wait_ge(bct_ready, 1)
                    for j in range(NH):
                        ins = tp(bank[5][:, j * P:(j + 1) * P], CZ[:, 1, j].rearrange("p a s -> p (a s)"), ident[:, :])
                    ins.then_inc(bct_psum, 1)
                if n == 7:
                    pe.wait_ge(rows_ready, 1)
                    for b in range(NB):
                        for k, row in enumerate((3, 5)):
                            o = (k * NB + b) * NH
                            ins = tp(bank[4][:, o:o + NH], rows[0:NH, row, b * P:(b + 1) * P], ident[0:NH, 0:NH])
                    ins.then_inc(cols_psum, 1)
                    pe.wait_ge(bct_ready, 4)
                    for h in range(NH):
                        ins = mm(bank[5 + h // 2][:, (h % 2) * T:(h % 2 + 1) * T], headsel[:, h, :], rows[0:NH, 4, :],
                                 start=True, stop=True)
                        if h % 2:
                            ins.then_inc(bcast_psum, 1)
                if n == 8:
                    pe.wait_ge(cols_ready, 1)
                    pe.wait_ge(copied0, 4)
                    for h in range(NH):
                        if h >= 2:
                            pe.wait_ge(weights_ready, h - 1)
                        ps = bank[7 if h % 2 == 0 else 4]
                        mm(ps[:, 0:T], kT[:, h, 0:P], qT[:, h, :], start=True, stop=True)
                        mm(ps[:, T:T + P], kT[:, h, P:T], qT[:, h, P:T], start=True, stop=True).then_inc(scores_psum, 1)
                if n == 10:
                    pe.wait_ge(weights_ready, NH)
                    pe.wait_ge(copied0, 6)
                    for m, (b, hp) in enumerate(((0, 0), (0, 1), (1, 0), (1, 1))):
                        for h in (2 * hp, 2 * hp + 1):
                            ps = bank[(5, 6, 7, 4)[m]][:, (h % 2) * (DH + 2):(h % 2 + 1) * (DH + 2)]
                            if b == 0:
                                ins = mm(ps, DEC[:, h, 0:P], V0[:, 0, h, :], start=True, stop=True)
                            else:
                                mm(ps, DEC[:, h, P:T], V0[:, 0, h, :], start=True, stop=False)
                                ins = mm(ps, DEC[:, h, T:T + P], V0[:, 1, h, :], start=False, stop=True)
                        ins.then_inc(num_psum, 1)
            pe.wait_ge(copied0, 12)
            pe.wait_ge(conv_ready, NH)
            for n, (pair, s, use) in enumerate(outs0):
                if n == 2:
                    head_transposes(0, HN, 5)
                    pe.wait_ge(mt_ready, NB)
                out_unit(0, pair, s, use, n == 0, n == 3)
            norm(1)
            moe(0)
            norm(2)

            pe.wait_ge(xt_ready, 4 * 2 + 4)

            def s5_in(p):
                if p >= 1:
                    pe.wait_ge(bu_used, 2 * p)
                for i in (2 * p, 2 * p + 1):
                    j, r = i // 4, slice(32 * (i % 4), 32 * (i % 4) + 32)
                    for k in range(2):
                        ins = mm(bank[4 + i % 2][:, k * T:(k + 1) * T], BT[r, k, j, :], uT[r, j, :],
                                 start=True, stop=True)
                    ins.then_inc(bu_psum, 1)

            def s5_out(p):
                j = p // 2
                if p % 2 == 0 and j >= 2:
                    pe.wait_ge(y_ready, j - 1)
                pe.wait_ge(pc_ready, 2 * p + 2)
                pe.wait_ge(ps_ready, 2 * p + 2)
                terms = ((0, 0, 0), (1, 1, 2), (2, 1, 0), (2, 0, 2))
                for n, (q, c, z) in enumerate(terms):
                    for k in range(2):
                        r = slice(32 * ((2 * p + k) % 4), 32 * ((2 * p + k) % 4) + 32)
                        ins = mm(bank[6 + j % 2][r, 0:T], CT[:, q, j, r],
                                 prod[:, 2 * k + c, z:z + 2].rearrange("p a t -> p (a t)"),
                                 start=n == 0, stop=n == 3)
                ins.then_inc(y_psum, 1)

            def level(l):
                ps = bank[2 + l % 2]
                if l < 8:
                    pe.wait_ge(lqk, l + 1)
                else:
                    pe.wait_ge(lcopied, 7)
                left, right = (QK, QK) if l < 8 else (k1T, q1T)
                for h in range(NH):
                    if l == 0:
                        ins = mm(ps[:, h * P:(h + 1) * P], left[:, h, 0:P], right[:, h, P:T], start=True, stop=True)
                        continue
                    for b in range(NB):
                        n = h * NB + b
                        if l == 1:
                            o = b * P
                            ins = mm(ps[0:64, n * 64:n * 64 + 64], left[:, h, o:o + 64], right[:, h, o + 64:o + P],
                                     start=True, stop=True)
                        elif l == 2:
                            for i in range(2):
                                o = b * P + 64 * i
                                ins = mm(ps[64 * i:64 * i + 32, n * 32:n * 32 + 32], left[:, h, o:o + 32],
                                         right[:, h, o + 32:o + 64], start=True, stop=True)
                        else:
                            for i in range(4):
                                o = b * P + 32 * i
                                ins = mm(ps[32 * i:32 * i + 32, n * 32:n * 32 + 32], left[:, h, o:o + 32],
                                         right[:, h, o:o + 32], start=True, stop=True)
                ins.then_inc(lpsum, 1)

            for n, (kind, half, s, use) in enumerate(plan1[:2]):
                project(halves_of(bank[n]), s, use, True)
            pe.wait_ge(copied1, 2)
            pe.wait_ge(bct_ready, 4)
            s5_in(0)
            for p in range(S5T // 2):
                n, l = 2 + p, 2 * (p - FIRST_LEVEL)
                kind, half, s, use = plan1[n]
                pe.wait_ge(copied1, n - 1)
                project(halves_of(bank[n % 2]), s, use, kind not in "ig", (0,))
                if p + 1 < S5T // 2:
                    s5_in(p + 1)
                if l >= 2:
                    level(l - 1)
                project(halves_of(bank[n % 2]), s, use, kind not in "ig", (1,))
                if l >= 0:
                    level(l)
                s5_out(p)
            level(7)
            level(8)
            pe.wait_ge(copied1, 10)
            pe.wait_ge(a_full, 1)
            for b in range(NB):
                for h in range(NH):
                    ps = bank[2 + b][:, h * P:(h + 1) * P]
                    if b == 0:
                        ins = mm(ps, A[:, h, 0, :], V1[:, 0, h, :], start=True, stop=True)
                    else:
                        mm(ps, A[:, h, 1, :], V1[:, 0, h, :], start=True, stop=False)
                        ins = mm(ps, A[:, h, 2, :], V1[:, 1, h, :], start=False, stop=True)
                ins.then_inc(o_psum, 1)
            pe.wait_ge(gelu_ready, NH)
            s, use = glu_at
            w = unit(s, use).rearrange("p (k n) -> p k n", k=NH)
            for j in range(NH):
                for k in range(NH):
                    ins = mm(bank[j // 2][:, (j % 2) * T:(j % 2 + 1) * T], w[:, k, j * P:(j + 1) * P], uT[:, k, :],
                             start=k == 0, stop=k == NH - 1)
                if j == 1:
                    ins.then_inc(glu_psum, 1)
            ins.then_inc(done[s], 1)
            head_transposes(1, HN1, 2)
            pe.wait_ge(ys5_ready, NH)
            pe.wait_ge(bu_used, S5T)
            for n, (pair, s, use) in enumerate(outs1):
                if n == 2:
                    pe.wait_ge(mt_ready, 2 * NB)
                out_unit(4, pair, s, use, n == 0, n == 3)
            norm(3)
            moe(1)


_OUTS = [((1, 256, 1024), 'float32')]


def kernel(**inputs):
    import numpy as _np
    import concourse.bacc as _bacc
    from concourse import mybir as _mybir
    from concourse.bass_utils import run_bass_kernel_spmd as _run

    names = ['x', 'norm_mix', 'norm_ffn', 'norm_final', 'ab_w_in', 'ab_gate_bias', 'ab_head_norm', 'ab_conv_w',
             'ab_w_out', 'cd_w_in', 's5_lambda_re', 's5_lambda_im', 's5_b_re', 's5_b_im', 's5_c_re', 's5_c_im',
             's5_d', 's5_log_dt', 's5_w_glu', 's5_b_glu', 'hgrn_lb', 'hgrn_out_norm', 'cd_w_out', 'moe_w_group',
             'moe_b_group', 'moe_w_router', 'moe_b_router', 'moe_w_gate', 'moe_w_up', 'moe_w_down']
    nc = _bacc.Bacc("TRN2", target_bir_lowering=False, num_devices=1)
    arrays, args = {}, []
    for name in names:
        a = _np.ascontiguousarray(inputs[name])
        arrays[f"in_{name}_dram"] = a
        args.append(nc.dram_tensor(f"in_{name}_dram", a.shape, _mybir.dt.from_np(a.dtype),
                                   kind="ExternalInput").ap())
    for i, (shape, dtype) in enumerate(_OUTS):
        dt = _mybir.dt.from_np(_np.dtype(dtype))
        args.append(nc.dram_tensor(f"out_{i}_dram", shape, dt, kind="ExternalOutput").ap())
    hybrid_trunk(nc, *args)
    r = _run(nc, [arrays], core_ids=[0])
    got = tuple(r.results[0][f"out_{i}_dram"] for i in range(len(_OUTS)))
    return got[0]
```

```python
from contextlib import ExitStack

import numpy as np

import concourse.bass as bass
from concourse import mybir

F32 = mybir.dt.float32
F32R = mybir.dt.float32r
I32 = mybir.dt.int32
U32 = mybir.dt.uint32
ALU = mybir.AluOpType
ACT = mybir.ActivationFunctionType
AX = mybir.AxisListType

P = 128
D = 1024
T = 256
NB = T // P
KC = D // P
W2 = D // 2
NH = 4
DH = W2 // NH
UNIT = 2048
UC = UNIT // KC
HALF = UNIT // 2
HI = 3
SLOTS = 12
E = 32
NG = 4
EG = E // NG
FF = D // 4
QE = 4
CAP = P // QE
NQ = E // QE
XB = 2 * T // CAP
XQ = XB // QE
NBLK = E + XB
S5T = 16
GCH = 16
FIRST_LEVEL = 4
LEVELS = [128, 64, 32, 16, 8, 4, 2, 1]
EPS = 1e-6
NEG = -1e30
TWO_PI = 6.283185


class Steps:

    def __init__(self, eng, sem):
        self.eng, self.sem, self.n = eng, sem, 0

    def add(self, ins):
        ins.then_inc(self.sem, 1)
        self.n += 1
        return self.n

    def wait(self, n=None):
        self.eng.wait_ge(self.sem, n or self.n)

    def then(self, ins):
        self.add(ins)
        self.wait()


def hybrid_trunk(nc, x, norm_mix, norm_ffn, norm_final, ab_w_in, ab_gate_bias, ab_head_norm,
                 ab_conv_w, ab_w_out, cd_w_in, s5_lambda_re, s5_lambda_im, s5_b_re, s5_b_im,
                 s5_c_re, s5_c_im, s5_d, s5_log_dt, s5_w_glu, s5_b_glu, hgrn_lb, hgrn_out_norm,
                 cd_w_out, moe_w_group, moe_b_group, moe_w_router, moe_b_router, moe_w_gate,
                 moe_w_up, moe_w_down, out):
    ctx = ExitStack()
    with ctx:
        def sb(name, shape, dt=F32):
            return ctx.enter_context(nc.sbuf_tensor(name, shape, dt))

        def sem(name):
            return ctx.enter_context(nc.semaphore(name))

        def under(name, shape, dt):
            with nc.sbuf_tensor(name, shape, dt) as t:
                return t

        ring_lo = under("ring_lo", [P, SLOTS, UNIT], F32R)
        ring = sb("ring", [P, SLOTS, UNIT])
        H = sb("H", [P, NB, D])
        XT_lo = under("XT_lo", [P, KC, T], F32R)
        XT = sb("XT", [P, KC, T])
        hi_parts = under("hi_parts", [P, KC * T + HI * HALF], F32R)
        XT_hi = hi_parts[:, 0:KC * T].rearrange("p (c t) -> p c t", t=T)
        W_hi = hi_parts[:, KC * T:].rearrange("p (i n) -> p i n", n=HALF)
        XN = sb("XN", [P, NB, D])
        SIN = sb("SIN", [P, S5T, P])
        COS = sb("COS", [P, S5T, P])
        BT = sb("BT", [P, 2, NH, P])
        CT = sb("CT", [P, 3, NH, P])
        ident = sb("ident", [P, P])
        before = sb("before", [P, P])
        ones = sb("ones", [P, P])
        tables = COS[:, 10:, :].rearrange("p i t -> p (i t)")
        headsel = tables[0:NH, 0:NH * P].rearrange("p (h t) -> p h t", t=P)
        causal = tables[:, NH * P:NH * P + T]
        iota = sb("iota", [P, T])
        iota_i = sb("iota_i", [P, T], I32)
        row_i = sb("row_i", [P, 32], I32)
        lvl_mask = sb("lvl_mask", [P, 6, 32], I32)
        cst = sb("cst", [P, 4])
        caps = sb("caps", [P, 8])
        NW = sb("NW", [P, 4, KC])
        hnw = sb("hnw", [P, W2])
        prow = sb("prow", [P, P])
        PT = sb("PT", [P, 76])
        logdt = sb("logdt", [S5T, 2])
        s5 = sb("s5", [P, 24, S5T])
        lbc = sb("lbc", [P, 6, NH])
        stat = sb("stat", [P, 16])
        rms = sb("rms", [P, 16])
        rinv = sb("rinv", [P, 16])
        posm = sb("posm", [P, NB, NBLK])
        comb = sb("comb", [P, NB, NBLK])
        xid = sb("xid", [P, XB + 1], I32)
        wr = sb("wr", [P, 2, KC, NG + E])
        rb = sb("rb", [P, 2, NG + E])
        mtmp = sb("mtmp", [P, 6, 32])
        chmask = sb("chmask", [P, 2])

        room = (nc.sbuf_bytes_remaining // 4) // 32 * 32
        mix_parts = under("mix_parts", [P, 7 * NH * T], F32R)
        arena = sb("arena", [P, room])

        class Carve:
            def __init__(self, start=0):
                self.at = start

            def __call__(self, *shape, dt=F32):
                a = arena[:, self.at:self.at + int(np.prod(shape))]
                self.at += int(np.prod(shape))
                assert self.at <= room, (self.at, room)
                return shaped(a if dt == F32 else a.bitcast(dt), *shape)

        def shaped(a, *shape):
            names = "abcd"[:len(shape)]
            if len(shape) == 1:
                return a
            return a.rearrange(f"p ({' '.join(names)}) -> p {' '.join(names)}",
                               **dict(zip(names[1:], shape[1:])))

        cut = Carve()
        qT, kT = cut(NH, T), cut(NH, T)
        V0 = cut(NB, NH, DH + 2)
        SO = cut(NB, W2)
        MT_hi = shaped(mix_parts[:, cut.at:cut.at + 2 * NH * T], 2 * NH, T)
        GB, GC = cut(NH, T), cut(NH, T)
        rows = cut(6, T)
        cols = cut(2, NB, NH)
        em = cut(NB, NH)
        den = cut(NB, NH)
        gbias = cut(2)
        wg = cut(KC, 2 * NH)
        prep = cut.at
        conv_in = cut(NH, T + 2)
        DEC = cut(NH, 3 * P)
        HN = cut(NB, NH, DH)
        MT0 = shaped(arena[:, 0:2 * NH * T], 2 * NH, T)
        MT0_lo = shaped(mix_parts[:, 0:2 * NH * T], 2 * NH, T)
        SQ = shaped(DEC.rearrange("p a b -> p (a b)")[:, 0:NB * W2], NB, NH, DH)
        cut = Carve(prep)
        bnat = cut(2, S5T, GCH)
        bbar = cut(2, S5T, GCH)
        BZ = cut(2, S5T, 2, GCH)
        cnat = cut(2, NH, 64)
        CZ = cut(2, NH, 2, 64)
        cut = Carve()
        uT = cut(NH, T)
        mixed = cut.at
        q1T, k1T, bT = cut(NH, T), cut(NH, T), cut(NH, T)
        MT1 = shaped(arena[:, mixed:mixed + 2 * NH * T], 2 * NH, T)
        MT1_lo = shaped(mix_parts[:, mixed:mixed + 2 * NH * T], 2 * NH, T)
        V1 = cut(NB, NH, DH)
        SO1 = cut(NB, W2)
        qk_flat, le_flat = cut(NH * T), cut(NH * T)
        QK, LE = shaped(qk_flat, NH, T), shaped(le_flat, NH, T)
        HN1, SQ1 = shaped(qk_flat, NB, NH, DH), shaped(le_flat, NB, NH, DH)
        FT = LE
        A = cut(NH, 3, P)
        AD = cut(NH * NB, 32)
        zst = shaped(XN[:, 0, :], 2, 4, P)
        mod = shaped(XN[:, 1, :], 2, 4, P)
        prod_flat = cut(16 * P)
        prod = shaped(prod_flat, 4, 4, P)
        glu_gate = shaped(prod_flat[:, 0:NH * T], NH, T)
        zin = cut(2, 4)
        cut = Carve()
        XG = cut(KC, P)
        SG, HID = cut(FF), cut(FF)
        HT = cut(2, P)
        Y = cut(D)
        S = cut(NB, P)
        SW = cut(NB, P)
        Q = cut(NB, P)
        LG = cut(NB, NG + E)
        G8 = cut(NB, 8)
        gmx, smx = cut(NB, 8), cut(NB, 8)
        gix, six = cut(NB, 8, dt=U32), cut(NB, 8, dt=U32)
        ggf, gval, e2 = cut(NB, 1), cut(NB, 1), cut(NB, 1)
        eg, goh = cut(NB, NG), cut(NB, NG)
        selm = cut(NB, EG, NG)
        SEL = cut(NB, EG)
        wt, idc, gs = cut(2, NB, 1), cut(2, NB, 1), cut(2, NB, 1)
        MC = cut(2, NB, E)
        MM, pos, vv = cut(NB, E), cut(NB, E), cut(NB, E)
        cnt, nbk, endb = cut(E), cut(E), cut(E)
        over = cut(E, 8)
        t32 = cut(2, NB, E)
        vk, ink, tk = cut(2, NB, XB), cut(2, NB, XB), cut(2, NB, XB)
        eix = cut(XB, E)
        exf = cut(XB)
        squares = [t.rearrange("p a b -> p (a b)") for t in (XT[:, :, :], XT[:, :, :], XN[:, :, :])]
        squares = [squares[0], arena[:, 7 * D:(7 + NB) * D], squares[1], arena[:, 7 * D:(7 + NB) * D], squares[2]]
        fin = XT[:, :, :].rearrange("p c t -> p (c t)")

        pairs = [ctx.enter_context(nc.psum_tensor(f"pair{i}", [P, 2, 512], F32)) for i in range(2)]
        bank = [pairs[i // 2][:, i % 2, :] for i in range(4)]
        bank += [ctx.enter_context(nc.psum_tensor(f"bank{i}", [P, 512], F32)) for i in range(4, 8)]

        uses = [0] * SLOTS
        at = [0]

        def take():
            s = at[0] % SLOTS
            at[0] += 1
            uses[s] += 1
            return s, uses[s]

        ab_in = ab_w_in[0].rearrange("(p c) n -> p c n", p=P)
        ab_out = ab_w_out[0].rearrange("(k p) n -> p k n", p=P)
        cd_in = cd_w_in[0].rearrange("(p c) n -> p c n", p=P)
        cd_out = cd_w_out[0].rearrange("(k p) n -> p k n", p=P)
        glu = s5_w_glu[0].rearrange("(k p) n -> p k n", p=P)
        GATES = 4 * W2
        CONV = GATES + 2 * NH

        mix0 = [("q", 0), ("q", 1), ("k", 0), ("k", 1), ("v", 0), ("v", 1), ("gb", 0), ("gb", 1),
                ("gc", 0), ("gc", 1), ("x", 0), ("x", 1), ("o", 0), ("o", 1)]
        first0 = {"q": 0, "k": W2, "v": 2 * W2, "o": 3 * W2, "gb": CONV, "gc": CONV + W2,
                  "x": CONV + 2 * W2}
        plan0 = [(kind, half, *take()) for kind, half in mix0]
        outs0 = [(pair, *take()) for pair in (2, 3, 0, 1)]
        moe_use = [None, None]

        def plan_moe(layer):
            slots, base = [], []
            for _ in range(3 * QE):
                s, n = take()
                slots.append(s)
                base.append(n)
            for _ in range(3 * QE * (NQ - 1)):
                take()
            moe_use[layer] = (slots, base)

        plan_moe(0)
        mix1 = [("u", 0), ("u", 1), ("f", 0), ("f", 1), ("q", 0), ("q", 1), ("i", 0), ("i", 1),
                ("g", 0), ("g", 1)]
        first1 = {"u": 0, "q": W2, "f": 2 * W2, "i": 3 * W2, "g": 4 * W2}
        plan1 = [(kind, half, *take()) for kind, half in mix1]
        glu_at = take()
        outs1 = [(pair, *take()) for pair in (2, 3, 0, 1)]
        plan_moe(1)
        split = [(s, n, h, h == 0) for _, _, s, n in plan0[1:] for h in range(2)]
        OUT0 = len(split)
        split += [(s, n, h, h == 0 and m < 3) for m, (_, s, n) in enumerate(outs0) for h in range(2)]
        OUT1 = len(split)
        split += [(s, n, h, h == 0 and m < 3) for m, (_, s, n) in enumerate(outs1) for h in range(2) if m > 0]

        def parts_of(q):
            s, _, h, _ = split[q]
            part = slice(h * HALF, (h + 1) * HALF)
            return ring[:, s, part], ring_lo[:, s, part], W_hi[:, q % HI]

        loaded = [sem(f"loaded{s}") for s in range(SLOTS)]
        done = [sem(f"done{s}") for s in range(SLOTS)]
        x_in = [sem(f"x_in{b}") for b in range(NB)]
        nw_in, wg_in = sem("nw_in"), sem("wg_in")
        small_in, late_in = sem("small_in"), sem("late_in")
        lam_in, bc_in, wr_in = sem("lam_in"), sem("bc_in"), sem("wr_in")
        out_done = sem("out_done")
        act_step, dve_step, pool_step = sem("act_step"), sem("dve_step"), sem("pool_step")
        consts = sem("consts")
        rms_ready, xn_ready = sem("rms_ready"), sem("xn_ready")
        xt_psum, xt_ready = sem("xt_psum"), sem("xt_ready")
        copied0 = sem("copied0")
        gates_psum, gates_biased, softplus = sem("gates_psum"), sem("gates_biased"), sem("softplus")
        rows_ready = sem("rows_ready")
        cols_psum, cols_ready, em_ready = sem("cols_psum"), sem("cols_ready"), sem("em_ready")
        bcast_psum, arg_ready, decay_ready = sem("bcast_psum"), sem("arg_ready"), sem("decay_ready")
        scores_psum, weights_ready, num_psum = sem("scores_psum"), sem("weights_ready"), sem("num_psum")
        hss_ready, hrms_ready, hn_ready = sem("hss_ready"), sem("hrms_ready"), sem("hn_ready")
        hT_psum, mt_ready, conv_ready = sem("hT_psum"), sem("mt_ready"), sem("conv_ready")
        hi_ready, lo_ready, half_used = sem("hi_ready"), sem("lo_ready"), sem("half_used")
        xt_split, x_used = sem("xt_split"), sem("x_used")
        out_lo_ready = sem("out_lo_ready")
        mix_hi_ready, mix_lo_ready = sem("mix_hi_ready"), sem("mix_lo_ready")
        out_psum = sem("out_psum")
        h_ready = sem("h_ready")
        pt_psum, pt_ready = sem("pt_psum"), sem("pt_ready")
        s5_act, s5_dve, tab_ready = sem("s5_act"), sem("s5_dve"), sem("tab_ready")
        bz_ready, bct_psum = sem("bz_ready"), sem("bct_psum")
        bct_ready, phase_ready = sem("bct_ready"), sem("phase_ready")
        logit_psum, rt_act, rt_dve = sem("logit_psum"), sem("rt_act"), sem("rt_dve")
        choice_ready, pos_psum, route_ready = sem("choice_ready"), sem("pos_psum"), sem("route_ready")
        f_ready, f_log = sem("f_ready"), sem("f_log")
        copied1 = sem("copied1")
        bu_psum, bu_used, z_ready = sem("bu_psum"), sem("bu_used"), sem("z_ready")
        pc_ready, ps_ready, y_psum = sem("pc_ready"), sem("ps_ready"), sem("y_psum")
        y_ready, gelu_ready, glu_psum, glu_sig = sem("y_ready"), sem("gelu_ready"), sem("glu_psum"), sem("glu_sig")
        ys5_ready, b_ready, so_ready = sem("ys5_ready"), sem("b_ready"), sem("so_ready")
        larg, lexp, lqk, lpsum = sem("larg"), sem("lexp"), sem("lqk"), sem("lpsum")
        lcopied, o_psum, o_ready = sem("lcopied"), sem("o_psum"), sem("o_ready")
        a_zero, a_full = sem("a_zero"), sem("a_full")

        class Pass:

            def __init__(self, tag):
                self.onehot = sem(f"onehot{tag}")
                self.xg_psum, self.xg = sem(f"xg_psum{tag}"), sem(f"xg{tag}")
                self.q_psum, self.q = sem(f"q_psum{tag}"), sem(f"q{tag}")
                self.silu, self.hid = sem(f"silu{tag}"), sem(f"hid{tag}")
                self.ht_psum, self.ht = sem(f"ht_psum{tag}"), sem(f"ht{tag}")
                self.down0 = sem(f"down0{tag}")
                self.y, self.acc_psum, self.added = sem(f"y{tag}"), sem(f"acc_psum{tag}"), sem(f"added{tag}")

        main = Pass("")
        extra = [Pass(f"_x{layer}") for layer in range(2)]
        xloaded = [sem(f"xloaded{layer}") for layer in range(2)]
        xdone = [sem(f"xdone{layer}") for layer in range(2)]

        block = ctx.enter_context(nc.Block())

        @block.sync
        def _(sp):
            def load(dst, src, s, n):
                if n > 1:
                    sp.wait_ge(done[s], n - 1)
                sp.dma_start(dst, src).then_inc(loaded[s], 16)

            def in_unit(w, first, kind, half, s, n):
                c0 = first[kind] + half * UC
                load(ring[:, s, :].rearrange("p (c n) -> p c n", c=KC), w[:, :, c0:c0 + UC], s, n)

            def out_unit(w, pair, s, n):
                load(ring[:, s, :].rearrange("p (k n) -> p k n", k=2), w[:, 2 * pair:2 * pair + 2, :], s, n)

            def experts(layer):
                slots, base = moe_use[layer]
                mats = [moe_w_gate, moe_w_up, moe_w_down]

                def src(k, e):
                    return mats[k][layer, e].rearrange("(p c) n -> p (c n)", p=P)

                with sp.Fori(0, NQ) as i:
                    for k in range(3):
                        for r in range(QE):
                            s, n = slots[k * QE + r], base[k * QE + r]
                            sp.wait_ge(done[s], i + (n - 1))
                            sp.wait_ge(done[s], n - 1)
                            sp.dma_start(ring[:, s, :], src(k, i * QE + r)).then_inc(loaded[s], 16)
                sp.wait_ge(route_ready, layer + 1)
                n_extra = sp.value_load(xid[0:1, XB:XB + 1], min_val=0, max_val=XB)
                with sp.If(n_extra > 0):
                    for s, n in zip(slots, base):
                        sp.wait_ge(done[s], n - 1 + NQ)
                    with sp.Fori(0, XQ) as i:
                        for k in range(3):
                            for r in range(QE):
                                e = sp.value_load(xid[0:1, bass.ds(i * QE + r, 1)], min_val=0, max_val=E - 1)
                                sp.wait_ge(extra[layer].xg_psum, 2 * i + 1)
                                sp.wait_ge(done[slots[k * QE + r]], 1)
                                sp.dma_start(ring[:, slots[k * QE + r], :], src(k, e)).then_inc(xloaded[layer], 16)
                    sp.wait_ge(xdone[layer], 3 * XQ)

            xv = x[0].rearrange("(b p) n -> p b n", p=P)
            for b in range(NB):
                sp.dma_start(H[:, b, :], xv[:, b, :]).then_inc(x_in[b], 16)
            sp.dma_start(NW[:, 0, :], norm_mix[0].rearrange("(p c) -> p c", p=P)).then_inc(nw_in, 16)
            sp.dma_start(wg, ab_in[:, :, GATES:GATES + 2 * NH]).then_inc(wg_in, 16)
            for k in range(2):
                sp.dma_start(gbias[0:NH, k:k + 1], ab_gate_bias[0, k * NH:(k + 1) * NH].rearrange("(h o) -> h o", o=1))\
                    .then_inc(wg_in, 16)
            for n, unit in enumerate(plan0):
                in_unit(ab_in, first0, *unit)
                if n == 2:
                    sp.dma_start(logdt[:, :], s5_log_dt.rearrange("o (i a) -> (o i) a", a=2)).then_inc(lam_in, 16)
                    for r0, w in ((16, s5_lambda_re[0]), (32, s5_lambda_im[0])):
                        for gg in range(2):
                            sp.dma_start(prow[r0:r0 + S5T, 64 * gg:64 * gg + 64],
                                           w.rearrange("(i a) s -> a i s", a=2)[gg]).then_inc(lam_in, 16)
                    for r0, v in ((48, ab_conv_w[0].rearrange("k (j c) -> (k j) c", c=P)),
                                  (60, s5_d[0].rearrange("(j c) -> j c", c=P)),
                                  (64, s5_b_glu[0].rearrange("(j c) -> j c", c=P)),
                                  (68, hgrn_lb.rearrange("l (j c) -> (l j) c", c=P))):
                        sp.dma_start(prow[r0:r0 + v.shape[0], :], v).then_inc(lam_in, 16)
                if n == 4:
                    for k, w in enumerate((s5_b_re, s5_b_im)):
                        wv = w[0].rearrange("(i a) s c -> a s i c", a=2)
                        for gg in range(2):
                            sp.dma_start(bnat[64 * gg:64 * gg + 64, k], wv[gg]).then_inc(bc_in, 16)
                    for k, w in enumerate((s5_c_re, s5_c_im)):
                        sp.dma_start(cnat[:, k], w[0].rearrange("(j g) c s -> (g c) j s", g=8)).then_inc(bc_in, 16)
                if n == 8:
                    for k, (wg_, we_) in enumerate(((moe_w_group[0], moe_w_router[0]), (moe_w_group[1], moe_w_router[1]))):
                        sp.dma_start(wr[:, k, :, 0:NG], wg_.rearrange("(p c) n -> p c n", p=P)).then_inc(wr_in, 16)
                        sp.dma_start(wr[:, k, :, NG:], we_.rearrange("(p c) n -> p c n", p=P)).then_inc(wr_in, 16)
                        sp.dma_start(rb[:, k, 0:NG], moe_b_group[k:k + 1, :].to_broadcast([P, NG])).then_inc(wr_in, 16)
                        sp.dma_start(rb[:, k, NG:], moe_b_router[k:k + 1, :].to_broadcast([P, E])).then_inc(wr_in, 16)
            for unit in outs0:
                out_unit(ab_out, *unit)
            experts(0)
            for unit in plan1:
                in_unit(cd_in, first1, *unit)
            s, n = glu_at
            load(ring[:, s, :].rearrange("p (k n) -> p k n", k=4), glu, s, n)
            for unit in outs1:
                out_unit(cd_out, *unit)
            experts(1)

        @block.gpsimd
        def _(pool):
            g = Steps(pool, pool_step)
            g.add(pool.memset(ident[:, :], 0.0))
            g.add(pool.memset(ones[:, :], 1.0))
            g.add(pool.memset(before[:, :], 1.0))
            g.add(pool.memset(causal[:, :], 0.0))
            g.add(pool.memset(headsel[:, :, :], 0.0))
            g.add(pool.memset(cst[:, 0:1], EPS))
            g.add(pool.memset(cst[:, 1:2], 1.0))
            g.add(pool.memset(cst[:, 2:3], float(np.pi / 2)))
            g.wait()
            g.add(pool.affine_select(out=ident[:, :], in_=ident[:, :], compare_op=ALU.not_equal, fill=1.0,
                                     base=0, pattern=[[-1, P]], channel_multiplier=1))
            g.add(pool.affine_select(out=before[:, :], in_=before[:, :], compare_op=ALU.is_gt, fill=0.0,
                                     base=0, pattern=[[1, P]], channel_multiplier=-1))
            g.add(pool.affine_select(out=causal[:, :], in_=causal[:, :], compare_op=ALU.is_ge, fill=NEG,
                                     base=0, pattern=[[1, T]], channel_multiplier=-1))
            g.add(pool.affine_select(out=headsel, in_=headsel, compare_op=ALU.not_equal,
                                     fill=1.0, base=0, pattern=[[-1, NH], [0, P]], channel_multiplier=1))
            g.add(pool.iota(iota_i[:, :], [[1, T]], base=0, channel_multiplier=0))
            g.add(pool.iota(row_i[:, :], [[0, 32]], base=0, channel_multiplier=1))
            g.add(pool.memset(V0[:, :, :, DH:DH + 2], 1.0))
            g.wait()
            g.then(pool.tensor_copy(iota[:, :], iota_i[:, :]))
            pool.tensor_scalar(caps[:, :], iota[:, 0:8], float(CAP), float(CAP), ALU.mult, ALU.add)\
                .then_inc(consts, 1)
            for q in range(OUT0):
                w, w_lo, w_hi = parts_of(q)
                pool.wait_ge(hi_ready, q + 1)
                pool.tensor_tensor(w_lo, w, w_hi.bitcast(F32), ALU.subtract).then_inc(lo_ready, 1)
            pool.wait_ge(s5_dve, 1)
            pool.wait_ge(bcast_psum, 2)
            pool.wait_ge(arg_ready, NH)
            pool.wait_ge(done[outs0[-1][1]], outs0[-1][2])
            g.then(pool.tensor_tensor(COS[:, :, :], iota[:, 0:P].unsqueeze(1).to_broadcast([P, S5T, P]),
                                      s5[:, 3, :].unsqueeze(2).to_broadcast([P, S5T, P]), ALU.mult))
            g.then(pool.tensor_copy(SIN[:, :, :].bitcast(I32), COS[:, :, :]))
            g.then(pool.tensor_copy(SIN[:, :, :], SIN[:, :, :].bitcast(I32)))
            pool.tensor_tensor(SIN[:, :, :], COS[:, :, :], SIN[:, :, :], ALU.subtract)\
                .then_inc(phase_ready, 1)

            pool.wait_ge(h_ready, 4)
            pool.memset(A[:, :, :, :], 0.0).then_inc(a_zero, 1)

            def level_arg(l):
                h = LEVELS[l]
                n = NH * T // (2 * h)
                bv = bT.rearrange("p h (n w) -> p (h n) w", w=2 * h)
                ev = LE.rearrange("p h (n w) -> p (h n) w", w=2 * h)
                mid = bv[:, :, h - 1:h].to_broadcast([P, n, h])
                if l == 0:
                    pool.wait_ge(b_ready, NH)
                else:
                    pool.wait_ge(lqk, l)
                g.add(pool.tensor_tensor(ev[:, :, 0:h], mid, bv[:, :, 0:h], ALU.subtract))
                pool.tensor_tensor(ev[:, :, h:2 * h], bv[:, :, h:2 * h], mid, ALU.subtract).then_inc(larg, 1)

            pool.wait_ge(tab_ready, 1)
            for p in range(S5T // 2):
                if p >= FIRST_LEVEL:
                    level_arg(2 * (p - FIRST_LEVEL))
                    level_arg(2 * (p - FIRST_LEVEL) + 1)
                for k in range(2):
                    i = 2 * p + k
                    pool.wait_ge(z_ready, i + 1)
                    if p >= 1:
                        pool.wait_ge(y_psum, p)
                    pool.tensor_tensor(prod[:, 2 * k + 1], zst[:, k], SIN[:, i:i + 1, :].to_broadcast([P, 4, P]),
                                       ALU.mult).then_inc(ps_ready, 1)

        @block.scalar
        def _(act):
            a = Steps(act, act_step)
            sc = nc.scalar
            def norm(k):
                a.add(sc.activation(rms[:, 15:16], cst[:, 1:2], ACT.Sqrt))
                for b in range(NB):
                    j = 2 * k + b
                    if k == 0:
                        act.wait_ge(x_in[b], 16)
                    else:
                        act.wait_ge(h_ready, 2 * (k - 1) + b + 1)
                    junk = squares[k][:, b * D:(b + 1) * D]
                    a.then(sc.activation(junk, H[:, b, :], ACT.Square, accum_out=stat[:, j:j + 1]))
                    sc.activation(rms[:, j:j + 1], stat[:, j:j + 1], ACT.Sqrt, bias=cst[:, 0:1], scale=1.0 / D)\
                        .then_inc(rms_ready, 1)

            def head_rms(k):
                act.wait_ge(hss_ready, k + 1)
                sc.activation(s5[:, 22, 0:8], s5[:, 21, 0:8], ACT.Sqrt, bias=cst[:, 0:1], scale=1.0 / DH)\
                    .then_inc(hrms_ready, 1)

            def tables():
                act.wait_ge(phase_ready, 1)
                a.then(sc.activation(COS[:, :, :], SIN[:, :, :], ACT.Abs))
                a.add(sc.activation(COS[:, :, :], COS[:, :, :], ACT.Sin, bias=cst[:, 2:3], scale=-TWO_PI))
                sc.activation(SIN[:, :, :], SIN[:, :, :], ACT.Sin, scale=TWO_PI).then_inc(tab_ready, 1)

            def moe(layer):
                act.wait_ge(rt_dve, 2 * layer + 1)
                sc.activation(eg, eg, ACT.Exp).then_inc(rt_act, 1)
                act.wait_ge(rt_dve, 2 * layer + 2)
                sc.activation(e2, e2, ACT.Exp).then_inc(rt_act, 1)
                if layer == 0:
                    tables()
                slots, base = moe_use[layer]

                def one(i, sems, n0, wait_gate, wait_down):
                    wait_gate()
                    sc.activation(SG, bank[2][:, 0:FF], ACT.Silu).then_inc(sems.silu, 1)
                    act.wait_ge(sems.down0, i + (n0 + 1))
                    sc.activation(Y[:, 0:512], bank[4][:, :], ACT.Copy).then_inc(sems.y, 1)
                    wait_down()
                    sc.activation(Y[:, 512:1024], bank[5][:, :], ACT.Copy).then_inc(sems.y, 1)

                g_at, d_at = QE - 1, 3 * QE - 1
                with act.Fori(0, NQ) as i:
                    one(i, main, NQ * layer, lambda: act.wait_ge(done[slots[g_at]], i + base[g_at]),
                        lambda: act.wait_ge(done[slots[d_at]], i + base[d_at]))
                act.wait_ge(route_ready, layer + 1)
                n_extra = act.value_load(xid[0:1, XB:XB + 1], min_val=0, max_val=XB)
                with act.If(n_extra > 0):
                    with act.Fori(0, XQ) as i:
                        one(i, extra[layer], 0, lambda: act.wait_ge(xdone[layer], 3 * i + 1),
                            lambda: act.wait_ge(xdone[layer], 3 * i + 3))

            def s5_step():
                act.wait_ge(pt_ready, 2)
                sc.activation(s5[:, 0, :], PT[:, 0:16], ACT.Exp).then_inc(s5_act, 1)

            def s5_parameters():
                act.wait_ge(s5_dve, 1)
                a.add(sc.activation(s5[:, 4, :], s5[:, 3, :], ACT.Sin, scale=TWO_PI))
                a.add(sc.activation(s5[:, 5, :], s5[:, 3, :], ACT.Sin, scale=TWO_PI / 2))
                a.add(sc.activation(s5[:, 17, :], s5[:, 16, :], ACT.Sin, scale=TWO_PI))
                a.add(sc.activation(s5[:, 18, :], s5[:, 16, :], ACT.Sin, scale=TWO_PI / 2))
                a.add(sc.activation(lbc[:, 0:2, :], lbc[:, 0:2, :], ACT.Exp))
                sc.activation(s5[:, 6, :], s5[:, 1, :], ACT.Tanh, scale=0.5).then_inc(s5_act, 1)

            act.wait_ge(consts, 1)
            norm(0)
            for k, w in ((1, norm_ffn[0]), (2, norm_mix[1]), (3, norm_ffn[1])):
                act.dma_start(NW[:, k, :], w.rearrange("(p c) -> p c", p=P)).then_inc(small_in, 16)
            act.dma_start(hnw[:, :], ab_head_norm[0:1, :].to_broadcast([P, W2])).then_inc(small_in, 16)
            act.wait_ge(xt_ready, 4)
            sc.activation(XT_hi, XT[:, :, :], ACT.Copy).then_inc(xt_split, 1)

            def split_hi(q):
                s, use, h, _ = split[q]
                w, _, w_hi = parts_of(q)
                act.wait_ge(loaded[s], 16 * use)
                last = q - HI
                if OUT1 <= q < OUT1 + HI:
                    act.wait_ge(done[outs0[-1][1]], outs0[-1][2])
                    act.wait_ge(pc_ready, S5T)
                    act.wait_ge(ps_ready, S5T)
                elif last >= 0 and split[last][3]:
                    act.wait_ge(half_used, sum(c for _, _, _, c in split[:last + 1]))
                elif last >= 0:
                    act.wait_ge(done[split[last][0]], split[last][1])
                sc.activation(w_hi, w, ACT.Copy).then_inc(hi_ready, 1)

            def mix_hi(mt, k0, k1):
                sc.activation(MT_hi[:, k0:k1, :], mt[:, k0:k1, :], ACT.Copy).then_inc(mix_hi_ready, 1)

            for q in range(HI):
                split_hi(q)
            for n, (kind, half, s, use) in enumerate(plan0):
                if n == 11:
                    head_rms(0)
                if 1 <= n and 2 * n + 1 < OUT0:
                    split_hi(2 * n + 1)
                if n == 13:
                    act.wait_ge(conv_ready, NH)
                    mix_hi(MT0, NH, 2 * NH)
                    split_hi(OUT0)
                if kind == "x":
                    split_hi(2 * n + 2)
                    continue
                act.wait_ge(done[s], use)
                ps = pairs[n % 2][:, :, 0:T]
                two = slice(2 * half, 2 * half + 2)
                if kind == "q":
                    sc.activation(qT[:, two, :], ps, ACT.Copy).then_inc(copied0, 1)
                elif kind == "k":
                    sc.activation(kT[:, two, :], ps, ACT.Copy, scale=DH ** -0.5).then_inc(copied0, 1)
                elif kind == "v":
                    sc.activation(V0[:, :, two, 0:DH], ps.rearrange("p b (h e) -> p b h e", e=DH),
                                  ACT.Copy).then_inc(copied0, 1)
                elif kind == "o":
                    sc.activation(SO[:, :, half * UC:(half + 1) * UC], ps, ACT.Sigmoid).then_inc(copied0, 1)
                elif kind == "gb":
                    sc.activation(GB[:, two, :], ps, ACT.Copy).then_inc(copied0, 1)
                else:
                    sc.activation(GC[:, two, :], ps, ACT.Copy).then_inc(copied0, 1)
                if 1 <= n and 2 * n + 2 < OUT0:
                    split_hi(2 * n + 2)
                if n == 0:
                    act.wait_ge(gates_biased, 1)
                    a.then(sc.activation(rows[0:NH, 3], rows[0:NH, 0], ACT.Abs))
                    a.then(sc.activation(rows[0:NH, 3], rows[0:NH, 3], ACT.Exp, scale=-1.0))
                    sc.activation(rows[0:NH, 3], rows[0:NH, 3], ACT.Ln, bias=cst[0:NH, 1:2]).then_inc(softplus, 1)
                if n == 1:
                    s5_step()
                if n == 2:
                    s5_parameters()
                if n == 7:
                    act.wait_ge(cols_ready, 1)
                    sc.activation(em, cols[:, 1], ACT.Exp).then_inc(em_ready, 1)
                    for h in range(NH):
                        act.wait_ge(arg_ready, h + 1)
                        sc.activation(DEC[:, h], DEC[:, h], ACT.Exp).then_inc(decay_ready, 1)
            for q in range(OUT0 + 1, OUT0 + 4):
                split_hi(q)
            for b in range(NB):
                act.wait_ge(hT_psum, b + 1)
                sc.activation(MT0[:, 0:NH, b * P:(b + 1) * P], bank[5 + b][:, :].rearrange("p (h t) -> p h t", t=P),
                              ACT.Copy).then_inc(mt_ready, 1)
            act.wait_ge(mt_ready, NB)
            mix_hi(MT0, 0, NH)
            for q in range(OUT0 + 4, OUT1):
                split_hi(q)
            norm(1)
            moe(0)
            norm(2)
            act.dma_start(hnw[:, :], hgrn_out_norm[0:1, :].to_broadcast([P, W2])).then_inc(late_in, 16)

            for n, (kind, half, s, use) in enumerate(plan1):
                if n == 4:
                    act.wait_ge(f_ready, 1)
                    sc.activation(FT, FT, ACT.Ln).then_inc(f_log, 1)
                if n >= 6:
                    for l in (2 * (n - 6), 2 * (n - 6) + 1):
                        act.wait_ge(larg, l + 1)
                        sc.activation(LE, LE, ACT.Exp).then_inc(lexp, 1)
                act.wait_ge(done[s], use)
                ps = bank[n % 2][:, :].rearrange("p (g t) -> p g t", g=2)
                two = slice(2 * half, 2 * half + 2)
                if kind == "u":
                    sc.activation(uT[:, two, :], ps, ACT.Copy).then_inc(copied1, 1)
                elif kind == "f":
                    a.add(sc.activation(FT[:, two, :], ps, ACT.Sigmoid))
                    sc.activation(k1T[:, two, :], ps, ACT.Sigmoid, scale=-1.0).then_inc(copied1, 1)
                elif kind == "q":
                    sc.activation(q1T[:, two, :], ps, ACT.Copy).then_inc(copied1, 1)
                elif kind == "i":
                    sc.activation(V1[:, :, two, :], ps.rearrange("p b (h e) -> p b h e", e=DH),
                                  ACT.Copy).then_inc(copied1, 1)
                else:
                    sc.activation(SO1[:, :, half * UC:(half + 1) * UC], ps, ACT.Copy).then_inc(copied1, 1)
            act.wait_ge(copied1, 10)
            sc.activation(SO1, SO1, ACT.Silu).then_inc(so_ready, 1)
            for j in range(NH):
                act.wait_ge(y_ready, j + 1)
                sc.activation(uT[:, j, :], uT[:, j, :], ACT.Gelu_apprx_tanh).then_inc(gelu_ready, 1)
            for b in range(NB):
                act.wait_ge(o_psum, b + 1)
                sc.activation(HN1[:, b], bank[2 + b][:, :].rearrange("p (h e) -> p h e", e=DH), ACT.Copy)\
                    .then_inc(o_ready, 1)
            split_hi(OUT1)
            split_hi(OUT1 + 1)
            head_rms(1)
            for j in range(NH):
                if j < 2:
                    act.wait_ge(glu_psum, 1)
                else:
                    act.wait_ge(done[glu_at[0]], glu_at[1])
                sc.activation(glu_gate[:, j, :], bank[j // 2][:, (j % 2) * T:(j % 2 + 1) * T], ACT.Sigmoid,
                              bias=PT[:, 64 + j:65 + j]).then_inc(glu_sig, 1)
            for b in range(NB):
                act.wait_ge(hT_psum, NB + b + 1)
                sc.activation(MT1[:, NH:2 * NH, b * P:(b + 1) * P],
                              bank[2 + b][:, :].rearrange("p (h t) -> p h t", t=P), ACT.Copy).then_inc(mt_ready, 1)
            act.wait_ge(mt_ready, 2 * NB)
            mix_hi(MT1, 3 * NH // 2, 2 * NH)
            split_hi(OUT1 + 2)
            act.wait_ge(ys5_ready, NH)
            mix_hi(MT1, 0, NH)
            for q in range(OUT1 + 3, len(split)):
                split_hi(q)
            norm(3)
            act.wait_ge(logit_psum, 2)
            act.dma_start(fin[:, 0:D], norm_final.rearrange("(o n) -> o n", o=1).to_broadcast([P, D]))\
                .then_inc(late_in, 16)
            moe(1)
            norm(4)
            ov = out[0].rearrange("(b p) n -> p b n", p=P)
            for b in range(NB):
                act.wait_ge(xn_ready, 2 * 4 + b + 1)
                act.dma_start(ov[:, b, :], XN[:, b, :]).then_inc(out_done, 16)
            act.wait_ge(out_done, NB * 16)

        @block.vector
        def _(dve):
            d = Steps(dve, dve_step)
            v = nc.vector

            def norm_rows(k):
                for b in range(NB):
                    j = 2 * k + b
                    dve.wait_ge(rms_ready, j + 1)
                    d.then(v.reciprocal(rinv[:, j:j + 1], rms[:, j:j + 1]))
                    if k < 4:
                        v.tensor_scalar(XN[:, b, :], H[:, b, :], rinv[:, j:j + 1], None, ALU.mult)\
                            .then_inc(xn_ready, 1)
                        continue
                    dve.wait_ge(late_in, 2 * 16)
                    v.scalar_tensor_tensor(out=XN[:, b, :], in0=H[:, b, :], scalar=rinv[:, j:j + 1],
                                           in1=fin[:, 0:D], op0=ALU.mult, op1=ALU.mult).then_inc(xn_ready, 1)

            def norm_columns(k):
                if k == 0:
                    dve.wait_ge(nw_in, 16)
                elif k == 1:
                    dve.wait_ge(small_in, 4 * 16)
                for b in range(NB):
                    for g in range(2):
                        dve.wait_ge(xt_psum, 4 * k + 2 * b + g + 1)
                        v.tensor_tensor(XT[:, 4 * g:4 * g + 4, b * P:(b + 1) * P],
                                        bank[2 * b + g][:, :].rearrange("p (c t) -> p c t", t=P),
                                        NW[:, k, 4 * g:4 * g + 4].unsqueeze(2).to_broadcast([P, 4, P]), ALU.mult)\
                            .then_inc(xt_ready, 1)

            def norm(k):
                if k in (1, 3):
                    norm_columns(k)
                    norm_rows(k)
                else:
                    norm_rows(k)
                    if k < 4:
                        norm_columns(k)

            def head_squares(hn, sq, wait_rows):
                for b in range(NB):
                    wait_rows(b)
                    d.then(v.tensor_tensor(sq[:, b], hn[:, b], hn[:, b], ALU.mult))
                    ins = v.tensor_reduce(s5[:, 21, NH * b:NH * (b + 1)], sq[:, b], AX.X, ALU.add)
                ins.then_inc(hss_ready, 1)

            def head_scale(k, hn, so):
                dve.wait_ge(hrms_ready, k + 1)
                d.then(v.reciprocal(s5[:, 23, 0:8], s5[:, 22, 0:8]))
                h8 = hn.rearrange("p b h e -> p (b h) e")
                d.then(v.tensor_tensor(h8, h8, s5[:, 23, 0:8].unsqueeze(2).to_broadcast([P, NB * NH, DH]), ALU.mult))
                for b in range(NB):
                    hb = hn[:, b].rearrange("p h e -> p (h e)")
                    v.tensor_tensor(hb, hb, so[:, b], ALU.mult).then_inc(hn_ready, 1)

            def split_lo(q):
                w, w_lo, w_hi = parts_of(q)
                dve.wait_ge(hi_ready, q + 1)
                v.tensor_tensor(w_lo, w, w_hi.bitcast(F32), ALU.subtract).then_inc(out_lo_ready, 1)

            def mix_part(n, mt, mt_lo, k0, k1):
                dve.wait_ge(mix_hi_ready, n)
                v.tensor_tensor(mt_lo[:, k0:k1, :], mt[:, k0:k1, :], MT_hi[:, k0:k1, :].bitcast(F32), ALU.subtract)\
                    .then_inc(mix_lo_ready, 1)

            def gate_weight(so):
                d.then(v.tensor_tensor(so, so, hnw[:, :].unsqueeze(1).to_broadcast([P, NB, W2]), ALU.mult))

            def add_out(first, s, use):
                for b in range(NB):
                    if b == 0:
                        dve.wait_ge(out_psum, first // 4 + 1)
                    else:
                        dve.wait_ge(done[s], use)
                    for n in range(2):
                        hv = H[:, b, n * 512:(n + 1) * 512]
                        ins = v.tensor_tensor(hv, hv, bank[first + 2 * b + n][:, :], ALU.add)
                    ins.then_inc(h_ready, 1)

            def route(layer):
                k = 2 * layer + 1
                d.then(v.memset(G8, -3e38))
                dve.wait_ge(logit_psum, layer + 1)
                m = [0] * NB
                for to, c0, c1 in ((G8[:, :, 0:NG], 0, NG), (LG[:, :, NG:], NG, NG + E)):
                    for b in range(NB):
                        n = d.add(v.scalar_tensor_tensor(out=to[:, b], in0=bank[4][:, b * (NG + E) + c0:b * (NG + E) + c1],
                                                         scalar=rinv[:, 2 * k + b:2 * k + b + 1],
                                                         in1=rb[:, layer, c0:c1], op0=ALU.mult, op1=ALU.add))
                        m[b] = m[b] or n
                for b in range(NB):
                    d.wait(m[b])
                    m[b] = d.add(v.max(gmx[:, b], G8[:, b]))
                for b in range(NB):
                    d.wait(m[b])
                    m[b] = d.add(v.max_index(gix[:, b], gmx[:, b], G8[:, b]))
                v.tensor_tensor(eg, G8[:, :, 0:NG], gmx[:, :, 0:1].to_broadcast([P, NB, NG]), ALU.subtract)\
                    .then_inc(rt_dve, 1)
                d.wait()
                d.then(v.tensor_copy(ggf, gix[:, :, 0:1]))
                d.then(v.tensor_tensor(goh, iota[:, 0:NG].unsqueeze(1).to_broadcast([P, NB, NG]),
                                       ggf.to_broadcast([P, NB, NG]), ALU.is_equal))
                d.then(v.tensor_tensor(selm, LG[:, :, NG:].rearrange("p b (g j) -> p b j g", j=EG),
                                       goh.unsqueeze(2).to_broadcast([P, NB, EG, NG]), ALU.mult))
                d.then(v.tensor_reduce(SEL, selm, AX.X, ALU.add))
                for b in range(NB):
                    m[b] = d.add(v.max(smx[:, b], SEL[:, b]))
                for b in range(NB):
                    d.wait(m[b])
                    m[b] = d.add(v.max_index(six[:, b], smx[:, b], SEL[:, b]))
                v.tensor_tensor(e2, smx[:, :, 1:2], smx[:, :, 0:1], ALU.subtract).then_inc(rt_dve, 1)
                d.wait()
                i2 = idc[:, :, :, 0]
                d.then(v.tensor_copy(i2, six[:, :, 0:2].rearrange("p b c -> p c b")))
                d.then(v.scalar_tensor_tensor(out=i2, in0=ggf[:, :, 0].unsqueeze(1).to_broadcast([P, 2, NB]),
                                              scalar=float(EG), in1=i2, op0=ALU.mult, op1=ALU.add))
                d.then(v.tensor_tensor(MC, iota[:, 0:E].unsqueeze(1).unsqueeze(1).to_broadcast([P, 2, NB, E]),
                                       idc.to_broadcast([P, 2, NB, E]), ALU.is_equal))
                v.tensor_tensor(MM, MC[:, 0], MC[:, 1], ALU.add).then_inc(choice_ready, 1)
                dve.wait_ge(choice_ready, layer + 1)
                dve.wait_ge(pos_psum, 2 * layer + 1)
                d.then(v.scalar_tensor_tensor(out=posm[:, :, 0:E],
                                              in0=bank[5][:, 0:2 * E].rearrange("p (b e) -> p b e", e=E),
                                              scalar=1.0, in1=MM, op0=ALU.add, op1=ALU.mult))

            def choice_weights(layer):
                dve.wait_ge(rt_act, 2 * layer + 2)
                d.then(v.tensor_reduce(gval, eg, AX.X, ALU.add))
                d.then(v.scalar_tensor_tensor(out=gval, in0=e2, scalar=1.0, in1=gval, op0=ALU.add, op1=ALU.mult))
                d.then(v.reciprocal(wt[:, 0], gval))
                d.then(v.tensor_tensor(wt[:, 1], e2, wt[:, 0], ALU.mult))
                for c in range(2):
                    d.then(v.tensor_tensor(t32[:, c], MC[:, c], wt[:, c].to_broadcast([P, NB, E]), ALU.mult))
                d.then(v.tensor_tensor(comb[:, :, 0:E], t32[:, 0], t32[:, 1], ALU.add))

            def further_lists(layer):
                d.add(v.tensor_copy(pos, bank[5][:, 0:2 * E].rearrange("p (b e) -> p b e", e=E)))
                dve.wait_ge(pos_psum, 2 * layer + 2)
                d.then(v.tensor_copy(cnt, bank[4][:, 2 * P:2 * P + E]))
                d.then(v.tensor_tensor(over, cnt.unsqueeze(2).to_broadcast([P, E, 8]),
                                       caps[:, :].unsqueeze(1).to_broadcast([P, E, 8]), ALU.is_gt))
                d.then(v.tensor_reduce(nbk, over, AX.X, ALU.add))
                d.then(v.tensor_tensor_scan(endb, ones[:, 0:E], nbk, 0.0, ALU.mult, ALU.add))
                d.then(v.tensor_tensor(nbk, endb, nbk, ALU.subtract))
                for b in range(NB):
                    d.then(v.scalar_tensor_tensor(out=vv[:, b], in0=nbk, scalar=float(CAP), in1=pos[:, b],
                                                 op0=ALU.mult, op1=ALU.add))
                d.then(v.tensor_scalar(t32[:, 0], pos, float(CAP), -1e6, ALU.is_lt, ALU.mult))
                d.then(v.scalar_tensor_tensor(out=vv, in0=vv, scalar=-float(CAP), in1=t32[:, 0],
                                              op0=ALU.add, op1=ALU.add))

            def further_blocks(layer):
                for c in range(2):
                    d.then(v.tensor_tensor(t32[:, c], MC[:, c], vv, ALU.mult))
                    d.then(v.tensor_reduce(gs[:, c], t32[:, c], AX.X, ALU.add))
                    for b in range(NB):
                        d.then(v.scalar_tensor_tensor(out=vk[:, c, b], in0=iota[:, 0:XB], scalar=-float(CAP),
                                                     in1=gs[:, c, b].to_broadcast([P, XB]),
                                                     op0=ALU.mult, op1=ALU.add))
                    d.then(v.tensor_scalar(ink[:, c], vk[:, c], 0.0, None, ALU.is_ge))
                    d.then(v.tensor_scalar(tk[:, c], vk[:, c], float(CAP), None, ALU.is_lt))
                    d.then(v.tensor_tensor(ink[:, c], ink[:, c], tk[:, c], ALU.mult))
                    d.then(v.scalar_tensor_tensor(out=vk[:, c], in0=vk[:, c], scalar=1.0, in1=ink[:, c],
                                                 op0=ALU.add, op1=ALU.mult))
                    d.then(v.tensor_tensor(tk[:, c], ink[:, c], wt[:, c].to_broadcast([P, NB, XB]), ALU.mult))
                d.then(v.tensor_tensor(posm[:, :, E:], vk[:, 0], vk[:, 1], ALU.add))
                d.then(v.tensor_tensor(comb[:, :, E:], tk[:, 0], tk[:, 1], ALU.add))
                d.then(v.tensor_tensor(eix, endb.unsqueeze(1).to_broadcast([P, XB, E]),
                                       iota[:, 0:XB].unsqueeze(2).to_broadcast([P, XB, E]), ALU.is_le))
                d.then(v.tensor_reduce(exf, eix, AX.X, ALU.add))
                d.then(v.tensor_scalar(xid[:, 0:XB], exf, float(E - 1), None, ALU.min))
                v.tensor_copy(xid[:, XB:XB + 1], endb[:, E - 1:E]).then_inc(route_ready, 1)
                dve.wait_ge(route_ready, layer + 1)

            def moe(layer):
                route(layer)
                slots, base = moe_use[layer]

                def one(i, sems, n0, first, wait_up, routing=False):
                    at = bass.ds(i * QE + first, QE)
                    slot = iota[:, 1:CAP + 1].unsqueeze(1).to_broadcast([P, QE, CAP])
                    for b in range(NB):
                        ins = v.tensor_tensor(S[:, b].rearrange("p (r j) -> p r j", j=CAP), slot,
                                              posm[:, b, at].unsqueeze(2).to_broadcast([P, QE, CAP]), ALU.is_equal)
                    ins.then_inc(sems.onehot, 1)
                    dve.wait_ge(sems.onehot, 2 * i + (2 * n0 + 1))
                    if routing:
                        choice_weights(layer)
                    for b in range(NB):
                        ins = v.tensor_tensor(SW[:, b].rearrange("p (r j) -> p r j", j=CAP),
                                              S[:, b].rearrange("p (r j) -> p r j", j=CAP),
                                              comb[:, b, at].unsqueeze(2).to_broadcast([P, QE, CAP]), ALU.mult)
                    ins.then_inc(sems.onehot, 1)
                    for g in range(2):
                        dve.wait_ge(sems.xg_psum, 2 * i + (2 * n0 + 1 + g))
                        ins = v.tensor_tensor(XG[:, 4 * g:4 * g + 4, :],
                                              bank[g][:, :].rearrange("p (c t) -> p c t", t=P),
                                              NW[:, 2 * layer + 1, 4 * g:4 * g + 4].unsqueeze(2)
                                              .to_broadcast([P, 4, P]), ALU.mult)
                        ins.then_inc(sems.xg, 1)
                    if routing:
                        further_lists(layer)
                    dve.wait_ge(sems.q_psum, i + (n0 + 1))
                    v.tensor_copy(Q.rearrange("p b t -> p (b t)"), bank[1][:, 0:T]).then_inc(sems.q, 1)
                    dve.wait_ge(sems.silu, i + (n0 + 1))
                    wait_up()
                    v.tensor_tensor(HID, SG, bank[3][:, 0:FF], ALU.mult).then_inc(sems.hid, 1)
                    dve.wait_ge(sems.ht_psum, i + (n0 + 1))
                    v.tensor_copy(HT.rearrange("p c t -> p (c t)"), bank[0][:, 0:T]).then_inc(sems.ht, 1)
                    if routing:
                        further_blocks(layer)
                    for n in range(2):
                        dve.wait_ge(sems.acc_psum, 2 * i + (2 * n0 + n + 1))
                        for b in range(NB):
                            hv = H[:, b, n * 512:(n + 1) * 512]
                            ins = v.tensor_tensor(hv, hv, bank[(6 if b == 0 else 2) + n][:, :], ALU.add)
                        ins.then_inc(sems.added, 1)

                u_at = 2 * QE - 1
                one(0, main, NQ * layer, 0, lambda: dve.wait_ge(done[slots[u_at]], base[u_at]), True)
                n_extra = dve.value_load(xid[0:1, XB:XB + 1], min_val=0, max_val=XB)
                with dve.Fori(1, NQ) as i:
                    one(i, main, NQ * layer, 0, lambda: dve.wait_ge(done[slots[u_at]], i + base[u_at]))
                dve.wait_ge(main.added, 2 * NQ * (layer + 1))
                with dve.If(n_extra > 0):
                    with dve.Fori(0, XQ) as i:
                        one(i, extra[layer], 0, E, lambda: dve.wait_ge(xdone[layer], 3 * i + 2))
                    dve.wait_ge(extra[layer].added, 2 * XQ)
                v.memset(stat[:, 15:16], 0.0).then_inc(h_ready, NB)

            dve.wait_ge(consts, 1)
            norm(0)
            dve.wait_ge(gates_psum, 1)
            d.then(v.tensor_scalar(rows[0:NH, 1, :], bank[4][0:NH, 0:T], gbias[0:NH, 0:1], None, ALU.add))
            d.then(v.tensor_copy(rows[0:NH, 0, :], bank[4][32:32 + NH, 0:T]))
            v.tensor_scalar(rows[0:NH, 0, :], rows[0:NH, 0, :], gbias[0:NH, 1:2], None, ALU.add)\
                .then_inc(gates_biased, 1)
            dve.wait_ge(lam_in, 9 * 16)
            for g in range(2):
                ins = v.tensor_copy(prow[0:S5T, 64 * g:64 * g + 64], logdt[:, g:g + 1].to_broadcast([S5T, 64]))
            ins.then_inc(pt_ready, 1)
            dve.wait_ge(xt_split, 1)
            dve.wait_ge(done[plan0[0][2]], plan0[0][3])
            v.tensor_tensor(XT_lo[:, :, :], XT[:, :, :], XT_hi.bitcast(F32), ALU.subtract).then_inc(xt_split, 1)
            dve.wait_ge(pt_psum, 1)
            v.tensor_copy(PT[:, :], bank[7][:, 0:76]).then_inc(pt_ready, 1)
            dve.wait_ge(pt_ready, 2)
            re, im = PT[:, 16:32], PT[:, 32:48]
            lbp = PT[:, 68:76].rearrange("p (l j) -> p l j", l=2)
            d.then(v.tensor_tensor(lbc[:, 2, :], lbp[:, 0], lbp[:, 1], ALU.max))
            d.then(v.tensor_tensor(lbc[:, 0:2, :], lbp, lbc[:, 2:3, :].to_broadcast([P, 2, NH]), ALU.subtract))
            dve.wait_ge(s5_act, 1)
            d.then(v.tensor_tensor(s5[:, 1, :], re, s5[:, 0, :], ALU.mult))
            d.then(v.tensor_tensor(s5[:, 2, :], im, s5[:, 0, :], ALU.mult))
            d.then(v.tensor_scalar(s5[:, 2, :], s5[:, 2, :], float(1.0 / (2 * np.pi)), None, ALU.mult))
            d.then(v.tensor_copy(s5[:, 7, :].bitcast(I32), s5[:, 2, :]))
            d.then(v.tensor_tensor(s5[:, 3, :], s5[:, 2, :], s5[:, 7, :].bitcast(I32), ALU.subtract))
            d.then(v.tensor_scalar(s5[:, 15, :], s5[:, 3, :], float(P), None, ALU.mult))
            d.then(v.tensor_copy(s5[:, 7, :].bitcast(I32), s5[:, 15, :]))
            v.tensor_tensor(s5[:, 16, :], s5[:, 15, :], s5[:, 7, :].bitcast(I32), ALU.subtract).then_inc(s5_dve, 1)
            dve.wait_ge(softplus, 1)
            r4 = rows[0:NH]
            d.then(v.memset(r4[:, 5, :], 1.0))
            d.then(v.scalar_tensor_tensor(out=r4[:, 0, :], in0=r4[:, 0, :], scalar=0.0, in1=r4[:, 3, :],
                                          op0=ALU.min, op1=ALU.subtract))
            d.then(v.tensor_tensor_scan(r4[:, 2, :], r4[:, 5, :], r4[:, 0, :], 0.0, ALU.mult, ALU.add))
            d.then(v.tensor_tensor(r4[:, 3, :], r4[:, 1, :], r4[:, 2, :], ALU.subtract))
            d.then(v.tensor_tensor_scan(r4[:, 4, :], r4[:, 3, :], r4[:, 3, :], NEG, ALU.max, ALU.max))
            d.then(v.tensor_scalar(r4[:, 4, :], r4[:, 4, :], -1.0, None, ALU.mult))
            v.tensor_tensor(r4[:, 5, :], r4[:, 4, :], r4[:, 2, :], ALU.subtract).then_inc(rows_ready, 1)

            dve.wait_ge(s5_act, 2)
            col = [s5[:, k, :] for k in range(24)]
            d.then(v.tensor_scalar(col[7], col[6], -1.0, 1.0, ALU.mult, ALU.add))
            d.then(v.tensor_tensor(col[5], col[5], col[5], ALU.mult))
            d.then(v.reciprocal(col[7], col[7]))
            d.then(v.tensor_scalar(col[5], col[5], 2.0, None, ALU.mult))
            d.then(v.scalar_tensor_tensor(out=col[8], in0=col[6], scalar=1.0, in1=col[7], op0=ALU.add, op1=ALU.mult))
            d.then(v.scalar_tensor_tensor(out=col[9], in0=col[6], scalar=2.0, in1=col[7], op0=ALU.mult, op1=ALU.mult))
            d.then(v.tensor_scalar(col[10], col[5], -1.0, 1.0, ALU.mult, ALU.add))
            d.then(v.tensor_tensor(col[9], col[9], col[10], ALU.mult))
            d.then(v.tensor_tensor(col[9], col[9], col[5], ALU.subtract))
            d.then(v.tensor_tensor(col[11], col[8], col[4], ALU.mult))
            d.then(v.tensor_tensor(col[12], re, re, ALU.mult))
            d.then(v.tensor_tensor(col[13], im, im, ALU.mult))
            d.then(v.tensor_tensor(col[12], col[12], col[13], ALU.add))
            d.then(v.reciprocal(col[12], col[12]))
            d.then(v.tensor_tensor(col[13], col[9], re, ALU.mult))
            d.then(v.tensor_tensor(col[14], col[11], im, ALU.mult))
            d.then(v.tensor_tensor(col[15], col[11], re, ALU.mult))
            d.then(v.tensor_tensor(col[19], col[9], im, ALU.mult))
            d.then(v.tensor_tensor(col[13], col[13], col[14], ALU.add))
            d.then(v.tensor_tensor(col[14], col[15], col[19], ALU.subtract))
            d.then(v.tensor_tensor(col[13], col[13], col[12], ALU.mult))
            d.then(v.tensor_tensor(col[14], col[14], col[12], ALU.mult))
            d.then(v.tensor_tensor(col[18], col[18], col[18], ALU.mult))
            d.then(v.tensor_scalar(col[18], col[18], -2.0, 1.0, ALU.mult, ALU.add))
            cr = col[13].unsqueeze(2).to_broadcast([P, S5T, GCH])
            ci = col[14].unsqueeze(2).to_broadcast([P, S5T, GCH])
            tmp = shaped(BZ.rearrange("p a b c d -> p (a b c d)")[:, 0:S5T * GCH], S5T, GCH)
            dve.wait_ge(bc_in, 6 * 16)
            d.then(v.tensor_tensor(bbar[:, 0], bnat[:, 0], cr, ALU.mult))
            d.then(v.tensor_tensor(tmp, bnat[:, 1], ci, ALU.mult))
            d.then(v.tensor_tensor(bbar[:, 0], bbar[:, 0], tmp, ALU.subtract))
            d.then(v.tensor_tensor(bbar[:, 1], bnat[:, 1], cr, ALU.mult))
            d.then(v.tensor_tensor(tmp, bnat[:, 0], ci, ALU.mult))
            d.then(v.tensor_tensor(bbar[:, 1], bbar[:, 1], tmp, ALU.add))
            d.then(v.memset(BZ.rearrange("p a b c d -> p (a b c d)"), 0.0))
            for k in range(2):
                for g in range(2):
                    half = slice(64 * g, 64 * g + 64)
                    d.then(v.tensor_copy(BZ[half, k, :, g, :], bbar[half, k]))
            par = mtmp[:, 0, 0:2].bitcast(I32)
            d.then(v.tensor_scalar(par, row_i[:, 0:2], 4, 1, ALU.logical_shift_right, ALU.bitwise_and))
            d.then(v.tensor_copy(chmask[:, 0:2], par))
            d.then(v.tensor_scalar(chmask[:, 0:1], chmask[:, 0:1], -1.0, 1.0, ALU.mult, ALU.add))
            for k in range(2):
                for g in range(2):
                    ins = v.tensor_scalar(CZ[:, k, :, g, :], cnat[:, k], chmask[:, g:g + 1], None, ALU.mult)
                    if k == 1 and g == 1:
                        ins.then_inc(bz_ready, 1)
                    else:
                        d.then(ins)
            for k in range(2):
                dve.wait_ge(bct_psum, k + 1)
                v.tensor_copy(BT[:, k], bank[5 + k][:, :].rearrange("p (j s) -> p j s", s=P)).then_inc(bct_ready, 1)
            dve.wait_ge(bct_psum, 3)
            d.then(v.tensor_copy(CT[:, 0], bank[7][:, :].rearrange("p (j s) -> p j s", s=P)))
            v.tensor_scalar(CT[:, 1], bank[7][:, :].rearrange("p (j s) -> p j s", s=P), -1.0, None, ALU.mult)\
                .then_inc(bct_ready, 1)
            dve.wait_ge(bct_psum, 4)
            v.tensor_scalar(CT[:, 2], bank[5][:, :].rearrange("p (j s) -> p j s", s=P), -1.0, None, ALU.mult)\
                .then_inc(bct_ready, 1)
            d.then(v.tensor_tensor(lbc[:, 2, :], lbc[:, 0, :], lbc[:, 1, :], ALU.add))
            d.then(v.reciprocal(lbc[:, 2, :], lbc[:, 2, :]))
            d.then(v.tensor_tensor(lbc[:, 0:2, :], lbc[:, 0:2, :], lbc[:, 2:3, :].to_broadcast([P, 2, NH]), ALU.mult))
            d.then(v.tensor_tensor(lbc[:, 2, :], lbc[:, 0, :], lbc[:, 1, :], ALU.add))
            d.then(v.tensor_tensor(lbc[:, 2, :], lbc[:, 2, :], lbc[:, 0, :], ALU.subtract))
            d.then(v.tensor_scalar(lbc[:, 3, :], lbc[:, 2, :], -1.0, 1.0, ALU.mult, ALU.add))
            mi = [mtmp[:, k, :].bitcast(I32) for k in range(6)]
            mf = [mtmp[:, k, :] for k in range(6)]
            d.then(v.tensor_tensor(mi[0], row_i[:, :], iota_i[:, 0:32], ALU.bitwise_xor))
            d.then(v.tensor_scalar(mi[0], mi[0], 31, None, ALU.bitwise_and))
            d.then(v.tensor_scalar(mi[1], row_i[:, :], 31, None, ALU.bitwise_and))
            d.then(v.tensor_copy(mf[2], mi[0]))
            d.then(v.tensor_copy(mf[3], mi[1]))
            d.then(v.tensor_tensor(mf[3], iota[:, 0:32], mf[3], ALU.subtract))
            d.then(v.tensor_scalar(mf[4], mf[3], 0.0, None, ALU.is_gt))
            d.then(v.tensor_scalar(mf[5], mf[3], 0.0, None, ALU.is_lt))
            d.then(v.tensor_tensor(mf[2], mf[2], mf[4], ALU.mult))
            d.then(v.tensor_tensor(mf[2], mf[2], mf[5], ALU.subtract))
            for k, (lo, hi) in enumerate([(h, 2 * h) for h in LEVELS[3:]] + [(0, 1)]):
                d.then(v.tensor_scalar(mf[3], mf[2], float(lo), None, ALU.is_ge))
                d.then(v.tensor_scalar(mf[4], mf[2], float(hi), None, ALU.is_lt))
                d.then(v.tensor_tensor(lvl_mask[:, k, :], mf[3], mf[4], ALU.mult))

            dve.wait_ge(cols_psum, 1)
            v.tensor_copy(cols.rearrange("p k b h -> p (k b h)"), bank[4][:, 0:4 * NH]).then_inc(cols_ready, 1)
            dve.wait_ge(cols_ready, 1)
            for h in range(NH):
                dve.wait_ge(bcast_psum, h // 2 + 1)
                nm = bank[5 + h // 2][:, (h % 2) * T:(h % 2 + 1) * T]
                d.then(v.scalar_tensor_tensor(out=DEC[:, h, 0:T], in0=nm, scalar=cols[:, 0, 0, h:h + 1],
                                             in1=causal[:, :], op0=ALU.add, op1=ALU.add))
                v.scalar_tensor_tensor(out=DEC[:, h, T:T + P], in0=nm[:, P:T], scalar=cols[:, 0, 1, h:h + 1],
                                       in1=causal[:, 0:P], op0=ALU.add, op1=ALU.add).then_inc(arg_ready, 1)
            for h in range(NH):
                dve.wait_ge(decay_ready, h + 1)
                dve.wait_ge(scores_psum, h + 1)
                v.tensor_tensor(DEC[:, h], DEC[:, h], bank[7 if h % 2 == 0 else 4][:, 0:3 * P], ALU.mult)\
                    .then_inc(weights_ready, 1)
            dve.wait_ge(em_ready, 1)
            for n, (b, hp) in enumerate(((0, 0), (0, 1), (1, 0), (1, 1))):
                dve.wait_ge(num_psum, n + 1)
                ps = bank[(5, 6, 7, 4)[n]][:, 0:2 * (DH + 2)].rearrange("p (h e) -> p h e", e=DH + 2)
                dn = den[:, b, 2 * hp:2 * hp + 2].unsqueeze(2)
                eh = em[:, b, 2 * hp:2 * hp + 2].unsqueeze(2)
                d.then(v.tensor_copy(dn, ps[:, :, DH:DH + 1]))
                d.then(v.scalar_tensor_tensor(out=eh, in0=dn, scalar=-1.0, in1=eh, op0=ALU.mult, op1=ALU.max))
                d.then(v.tensor_tensor(dn, dn, eh, ALU.max))
                d.then(v.reciprocal(dn, dn))
                d.then(v.tensor_tensor(HN[:, b, 2 * hp:2 * hp + 2, :], ps[:, :, 0:DH],
                                      dn.to_broadcast([P, 2, DH]), ALU.mult))
            head_squares(HN, SQ, lambda b: None)
            d.then(v.memset(conv_in[:, :, 0:2], 0.0))
            dve.wait_ge(copied0, 10)
            for half, (_, _, s, use) in enumerate(plan0[10:12]):
                dve.wait_ge(done[s], use)
                two = slice(2 * half, 2 * half + 2)
                v.tensor_tensor(conv_in[:, two, 2:], pairs[half][:, :, 0:T], GC[:, two, :], ALU.mult)\
                    .then_inc(x_used, 1)
            dve.wait_ge(x_used, 2)
            for j in range(NH):
                d.then(v.tensor_scalar(GC[:, j, :], conv_in[:, j, 0:T], PT[:, 48 + j:49 + j], None, ALU.mult))
                for k in (1, 2):
                    d.then(v.scalar_tensor_tensor(out=GC[:, j, :], in0=conv_in[:, j, k:k + T],
                                                  scalar=PT[:, 48 + 4 * k + j:49 + 4 * k + j], in1=GC[:, j, :],
                                                  op0=ALU.mult, op1=ALU.add))
                v.tensor_tensor(MT0[:, NH + j, :], GC[:, j, :], GB[:, j, :], ALU.mult).then_inc(conv_ready, 1)
            mix_part(1, MT0, MT0_lo, NH, 2 * NH)
            split_lo(OUT0)
            split_lo(OUT0 + 1)
            dve.wait_ge(copied0, 12)
            dve.wait_ge(small_in, 4 * 16)
            gate_weight(SO)
            head_scale(0, HN, SO)
            split_lo(OUT0 + 2)
            split_lo(OUT0 + 3)
            mix_part(2, MT0, MT0_lo, 0, NH)
            for q in range(OUT0 + 4, OUT1):
                split_lo(q)
            add_out(0, *outs0[-1][1:])
            norm(1)
            moe(0)
            norm(2)

            dve.wait_ge(a_zero, 1)
            dve.wait_ge(tab_ready, 1)
            d.then(v.memset(AD, 0.0))

            def level_copy(l):
                dve.wait_ge(lpsum, l + 1)
                ps = bank[2 + l % 2]
                if l == 0:
                    ins = v.tensor_copy(A[:, :, 1, :], ps[:, :].rearrange("p (h t) -> p h t", t=P))
                elif l == 1:
                    for b in range(NB):
                        ins = v.tensor_copy(A[0:64, :, 2 * b, 64:P],
                                            ps[0:64, :].rearrange("p (h b t) -> p h b t", b=NB, t=64)[:, :, b])
                elif l == 2:
                    for i in range(2):
                        r = slice(64 * i, 64 * i + 32)
                        for b in range(NB):
                            ins = v.tensor_copy(A[r, :, 2 * b, 64 * i + 32:64 * i + 64],
                                                ps[r, 0:T].rearrange("p (h b t) -> p h b t", b=NB, t=32)[:, :, b])
                else:
                    ins = v.copy_predicated(AD, lvl_mask[:, l - 3:l - 2, :].to_broadcast([P, NH * NB, 32]),
                                            ps[:, 0:T].rearrange("p (n t) -> p n t", t=32))
                ins.then_inc(lcopied, 1)
                dve.wait_ge(lcopied, l + 1)

            def level_scale(l):
                h = LEVELS[l]
                dve.wait_ge(lexp, l + 1)
                cutup = lambda t: t.rearrange("p h (n w) -> p (h n) w", w=2 * h)
                d.then(v.tensor_tensor(cutup(QK)[:, :, 0:h], cutup(k1T)[:, :, 0:h], cutup(LE)[:, :, 0:h], ALU.mult))
                v.tensor_tensor(cutup(QK)[:, :, h:2 * h], cutup(q1T)[:, :, h:2 * h], cutup(LE)[:, :, h:2 * h],
                                ALU.mult).then_inc(lqk, 1)

            def s5_states(p):
                m = [0, 0]
                bu = [bank[4 + k][:, :].rearrange("p (k t) -> p k t", t=P) for k in range(2)]
                cs = [COS[:, i:i + 1, :].to_broadcast([P, 4, P]) for i in (2 * p, 2 * p + 1)]
                sn = [SIN[:, i:i + 1, :].to_broadcast([P, 4, P]) for i in (2 * p, 2 * p + 1)]
                rho = [s5[:, 8, i:i + 1].to_broadcast([P, P]) for i in (2 * p, 2 * p + 1)]
                for k in range(2):
                    dve.wait_ge(bu_psum, 2 * p + k + 1)
                    m[k] = d.add(v.tensor_tensor(mod[:, k], bu[k], sn[k], ALU.mult))
                for k in range(2):
                    if p >= 1:
                        dve.wait_ge(pc_ready, 2 * p)
                        dve.wait_ge(ps_ready, 2 * p)
                    v.tensor_tensor(zst[:, k], bu[k], cs[k], ALU.mult).then_inc(bu_used, 1)
                for k in range(2):
                    d.wait(m[k])
                    dve.wait_ge(bu_used, 2 * p + k + 1)
                    m[k] = d.add(v.tensor_tensor(zst[:, k, 0:2], zst[:, k, 0:2], mod[:, k, 2:4], ALU.add))
                for k in range(2):
                    d.wait(m[k])
                    m[k] = d.add(v.tensor_tensor(zst[:, k, 2:4], zst[:, k, 2:4], mod[:, k, 0:2], ALU.subtract))
                for q in (0, 2):
                    for k in range(2):
                        d.wait(m[k])
                        m[k] = d.add(v.tensor_tensor_scan(zst[:, k, q], rho[k], zst[:, k, q], 0.0, ALU.mult, ALU.add))
                return m

            def s5_products(p, m):
                zr, zi = [zst[:, k, 0, P - 1:P] for k in range(2)], [zst[:, k, 2, P - 1:P] for k in range(2)]
                c128, s128 = [[s5[:, c, 2 * p + k:2 * p + k + 1] for k in range(2)] for c in (18, 17)]
                for k in range(2):
                    d.wait(m[k])
                    d.add(v.tensor_tensor(zin[:, k, 0:1], zi[k], s128[k], ALU.mult))
                    m[k] = d.add(v.tensor_tensor(zin[:, k, 1:2], zr[k], s128[k], ALU.mult))
                for k in range(2):
                    d.wait(m[k])
                    d.add(v.scalar_tensor_tensor(out=zin[:, k, 2:3], in0=zr[k], scalar=c128[k],
                                                 in1=zin[:, k, 0:1], op0=ALU.mult, op1=ALU.subtract))
                    m[k] = d.add(v.scalar_tensor_tensor(out=zin[:, k, 3:4], in0=zi[k], scalar=c128[k],
                                                        in1=zin[:, k, 1:2], op0=ALU.mult, op1=ALU.add))
                rho = [s5[:, 8, i:i + 1].to_broadcast([P, P]) for i in (2 * p, 2 * p + 1)]
                for k in range(2):
                    d.wait(m[k])
                    m[k] = d.add(v.tensor_tensor_scan(zst[:, k, 1], rho[k], zst[:, k, 1], zin[:, k, 2:3],
                                                      ALU.mult, ALU.add))
                    v.tensor_tensor_scan(zst[:, k, 3], rho[k], zst[:, k, 3], zin[:, k, 3:4], ALU.mult, ALU.add)\
                        .then_inc(z_ready, 1)
                if p >= 1:
                    dve.wait_ge(y_psum, p)
                for k in range(2):
                    d.wait(m[k])
                    dve.wait_ge(z_ready, 2 * p + k + 1)
                    v.tensor_tensor(prod[:, 2 * k], zst[:, k], COS[:, 2 * p + k:2 * p + k + 1, :]
                                    .to_broadcast([P, 4, P]), ALU.mult).then_inc(pc_ready, 1)

            def s5_skip(j):
                dve.wait_ge(y_psum, 2 * j + 2)
                v.scalar_tensor_tensor(out=uT[:, j, :], in0=uT[:, j, :], scalar=PT[:, 60 + j:61 + j],
                                       in1=bank[6 + j % 2][:, 0:T], op0=ALU.mult, op1=ALU.add).then_inc(y_ready, 1)

            def level_step(l):
                if l >= 1:
                    level_copy(l - 1)
                level_scale(l)

            for p in range(S5T // 2):
                marks = s5_states(p)
                if p % 2 == 0 and p > 0:
                    s5_skip(p // 2 - 1)
                if p == 2:
                    dve.wait_ge(copied1, 4)
                    for h in range(NH):
                        d.add(v.tensor_scalar(k1T[:, h, :], k1T[:, h, :], lbc[:, 3, h:h + 1], None, ALU.mult))
                        ins = v.tensor_scalar(FT[:, h, :], FT[:, h, :], lbc[:, 3, h:h + 1], lbc[:, 2, h:h + 1],
                                              ALU.mult, ALU.add)
                    ins.then_inc(f_ready, 1)
                if p == 3:
                    dve.wait_ge(f_log, 1)
                    for h in range(NH):
                        v.tensor_tensor_scan(bT[:, h, :], ones[:, 0:1].to_broadcast([P, T]), FT[:, h, :], 0.0,
                                             ALU.mult, ALU.add).then_inc(b_ready, 1)
                if p == FIRST_LEVEL:
                    dve.wait_ge(copied1, 6)
                if p >= FIRST_LEVEL:
                    level_step(2 * (p - FIRST_LEVEL))
                s5_products(p, marks)
                if p >= FIRST_LEVEL:
                    level_step(2 * (p - FIRST_LEVEL) + 1)
            s5_skip(3)
            dve.wait_ge(so_ready, 1)
            dve.wait_ge(late_in, 16)
            gate_weight(SO1)
            level_copy(7)
            level_copy(8)
            for i in range(4):
                r = slice(32 * i, 32 * i + 32)
                for b in range(NB):
                    ins = v.tensor_copy(A[r, :, 2 * b, r], AD.rearrange("p (h b) t -> p h b t", b=NB)[r, :, b])
            ins.then_inc(a_full, 1)
            head_squares(HN1, SQ1, lambda b: dve.wait_ge(o_ready, b + 1))
            head_scale(1, HN1, SO1)
            for j in range(NH):
                dve.wait_ge(glu_sig, j + 1)
                v.tensor_tensor(MT1[:, j, :], uT[:, j, :], glu_gate[:, j, :], ALU.mult).then_inc(ys5_ready, 1)
            split_lo(OUT1)
            split_lo(OUT1 + 1)
            mix_part(3, MT1, MT1_lo, 3 * NH // 2, 2 * NH)
            split_lo(OUT1 + 2)
            mix_part(4, MT1, MT1_lo, 0, NH)
            for q in range(OUT1 + 3, len(split)):
                split_lo(q)
            add_out(4, *outs1[-1][1:])
            norm(3)
            moe(1)
            norm(4)

        @block.tensor
        def _(pe):
            mm, tp = nc.tensor.matmul, nc.tensor.transpose

            def keep_warm(n, ps):
                for _ in range(n):
                    mm(ps[:, 0:P], ones[:, :], ones[:, :], start=True, stop=True)

            def norm(k):
                if k == 2:
                    keep_warm(18, bank[4])
                for b in range(NB):
                    if k in (1, 3):
                        pe.wait_ge(h_ready, 2 * (k - 1) + b + 1)
                    else:
                        pe.wait_ge(xn_ready, 2 * k + b + 1)
                    xc = (H if k in (1, 3) else XN)[:, b, :].rearrange("p (q c) -> p c q", c=KC)
                    for g in range(2):
                        for c in range(4):
                            ins = tp(bank[2 * b + g][:, c * P:(c + 1) * P], xc[:, 4 * g + c, :], ident[:, :])
                        ins.then_inc(xt_psum, 1)

            def unit(s, use):
                pe.wait_ge(loaded[s], 16 * use)
                return ring[:, s, :]

            def project(ps, s, use, transposed, halves=(0, 1)):
                w = (unit(s, use) if 0 in halves else ring[:, s, :]).rearrange("p (c n) -> p c n", c=KC)
                for g in halves:
                    for c in range(KC):
                        if transposed:
                            ins = mm(ps[g], w[:, c, g * P:(g + 1) * P], XT[:, c, :],
                                     start=c == 0, stop=c == KC - 1)
                        else:
                            ins = mm(ps[g], XT[:, c, g * P:(g + 1) * P], w[:, c, :],
                                     start=c == 0, stop=c == KC - 1)
                if 1 in halves:
                    ins.then_inc(done[s], 1)

            def halves_of(ps):
                return [ps[:, 0:T], ps[:, T:2 * T]]

            def first_out_unit(first, pair, s, use):
                w = unit(s, use).rearrange("p (k n) -> p k n", k=2)
                for b in range(NB):
                    pe.wait_ge(mt_ready, NB + b + 1)
                    for k in range(2):
                        for n in range(2):
                            ins = mm(bank[first + 2 * b + n][:, :], MT1[:, 2 * pair + k, b * P:(b + 1) * P],
                                     w[:, k, n * 512:(n + 1) * 512], start=k == 0, stop=False)
                ins.then_inc(done[s], 1)

            def out_parts(first, pair, s, use, q, start, stop):
                mt_lo = MT1_lo if first else MT0_lo
                for b in range(NB):
                    if b > 0 and not stop:
                        break
                    for k in range(2):
                        if b == 0:
                            pe.wait_ge(out_lo_ready, q + k + 1 - OUT0)
                        _, w_lo, w_hi = parts_of(q + k)
                        blocks = (b,) if stop else range(NB)
                        for bb in blocks:
                            t = slice(bb * P, (bb + 1) * P)
                            m_hi, m_lo = MT_hi[:, 2 * pair + k, t], mt_lo[:, 2 * pair + k, t]
                            for n in range(2):
                                cut_n = slice(n * 512, (n + 1) * 512)
                                for j, (m, w) in enumerate(((m_hi, w_hi), (m_lo, w_hi), (m_hi, w_lo))):
                                    ins = mm(bank[first + 2 * bb + n][:, :], m, w[:, cut_n],
                                             start=start and k == 0 and j == 0, stop=stop and k == 1 and j == 2)
                        if not stop:
                            ins.then_inc(half_used if k == 0 else done[s], 1)
                    if stop:
                        ins.then_inc(out_psum if b == 0 else done[s], 1)

            def head_transposes(k, hn, first):
                for b in range(NB):
                    pe.wait_ge(hn_ready, NB * k + b + 1)
                    for h in range(NH):
                        ins = tp(bank[first + b][:, h * P:(h + 1) * P], hn[:, b, h, :], ident[:, :])
                    ins.then_inc(hT_psum, 1)

            def route(layer):
                k = 2 * layer + 1
                pe.wait_ge(wr_in, 8 * 16)
                for b in range(NB):
                    for c in range(KC):
                        if c % 4 == 0:
                            pe.wait_ge(xt_ready, 4 * k + 2 * b + c // 4 + 1)
                        ins = mm(bank[4][:, b * (NG + E):(b + 1) * (NG + E)], XT[:, c, b * P:(b + 1) * P],
                                 wr[:, layer, c, :], start=c == 0, stop=c == KC - 1)
                ins.then_inc(logit_psum, 1)
                keep_warm(16, bank[7])
                pe.wait_ge(choice_ready, layer + 1)
                mm(bank[5][:, 0:E], before[:, :], MM[:, 0], start=True, stop=True)
                mm(bank[5][:, E:2 * E], before[:, :], MM[:, 1], start=True, stop=False)
                mm(bank[5][:, E:2 * E], ones[:, :], MM[:, 0], start=False, stop=True).then_inc(pos_psum, 1)
                mm(bank[4][:, 2 * P:2 * P + E], ones[:, :], MM[:, 0], start=True, stop=False)
                mm(bank[4][:, 2 * P:2 * P + E], ones[:, :], MM[:, 1], start=False, stop=True).then_inc(pos_psum, 1)

            def moe(layer):
                route(layer)
                slots, base = moe_use[layer]

                def one(i, sems, n0, wait_loaded, finish):
                    cols_of = [slice(r * CAP, (r + 1) * CAP) for r in range(QE)]
                    pe.wait_ge(sems.onehot, 2 * i + (2 * n0 + 1))
                    xc = XN[:, :, :].rearrange("p b (q c) -> p b c q", c=KC)
                    for c in range(KC):
                        for b in range(NB):
                            ins = mm(bank[c // 4][:, (c % 4) * P:(c % 4 + 1) * P], xc[:, b, c, :], S[:, b],
                                     start=b == 0, stop=b == NB - 1)
                        if c % 4 == 3:
                            ins.then_inc(sems.xg_psum, 1)
                    for k in range(2):
                        for r in range(QE):
                            wait_loaded(k, r)
                        for c in range(KC):
                            if k == 0 and c % 4 == 0:
                                pe.wait_ge(sems.xg, 2 * i + (2 * n0 + 1 + c // 4))
                            for r in range(QE):
                                w = ring[:, slots[k * QE + r], :].rearrange("p (c n) -> p c n", c=KC)
                                ins = mm(bank[2 + k][cols_of[r], 0:FF], XG[:, c, cols_of[r]], w[:, c, :],
                                         start=c == 0, stop=c == KC - 1)
                                if c == KC - 1:
                                    finish(ins, k, r)
                        if k == 0:
                            pe.wait_ge(sems.onehot, 2 * i + (2 * n0 + 2))
                            for b in range(NB):
                                ins = tp(bank[1][:, b * P:(b + 1) * P], SW[:, b], ident[:, :])
                            ins.then_inc(sems.q_psum, 1)
                    pe.wait_ge(sems.hid, i + (n0 + 1))
                    hc = HID.rearrange("p (q c) -> p c q", c=2)
                    for c in range(2):
                        ins = tp(bank[0][:, c * P:(c + 1) * P], hc[:, c, :], ident[:, :])
                    ins.then_inc(sems.ht_psum, 1)
                    keep_warm(14, bank[6])
                    pe.wait_ge(sems.ht, i + (n0 + 1))
                    for r in range(QE):
                        wait_loaded(2, r)
                    for n in range(2):
                        for c in range(2):
                            for r in range(QE):
                                w = ring[:, slots[2 * QE + r], :].rearrange("p (c n) -> p c n", c=2)
                                ins = mm(bank[4 + n][cols_of[r], :], HT[:, c, cols_of[r]],
                                         w[:, c, n * 512:(n + 1) * 512], start=c == 0, stop=c == 1)
                                if n == 1 and c == 1:
                                    finish(ins, 2, r)
                        if n == 0:
                            ins.then_inc(sems.down0, 1)
                    pe.wait_ge(sems.q, i + (n0 + 1))
                    for n in range(2):
                        pe.wait_ge(sems.y, 2 * i + (2 * n0 + n + 1))
                        for b in range(NB):
                            ins = mm(bank[(6 if b == 0 else 2) + n][:, :], Q[:, b], Y[:, n * 512:(n + 1) * 512],
                                     start=True, stop=True)
                        ins.then_inc(sems.acc_psum, 1)

                with pe.Fori(0, NQ) as i:
                    one(i, main, NQ * layer,
                        lambda k, r: pe.wait_ge(loaded[slots[k * QE + r]], 16 * i + 16 * base[k * QE + r]),
                        lambda ins, k, r: ins.then_inc(done[slots[k * QE + r]], 1))
                pe.wait_ge(route_ready, layer + 1)
                n_extra = pe.value_load(xid[0:1, XB:XB + 1], min_val=0, max_val=XB)
                with pe.If(n_extra > 0):
                    with pe.Fori(0, XQ) as i:
                        one(i, extra[layer], 0,
                            lambda k, r: pe.wait_ge(xloaded[layer], 48 * QE * i + 48 * QE) if k == 0 and r == 0 else None,
                            lambda ins, k, r: ins.then_inc(xdone[layer], 1) if r == QE - 1 else None)

            pe.wait_ge(pool_step, 2)
            keep_warm(16, bank[7])
            pe.wait_ge(consts, 1)
            norm(0)
            pe.wait_ge(xt_ready, 4)
            pe.wait_ge(wg_in, 3 * 16)
            for c in range(KC):
                for k in range(2):
                    ins = mm(bank[4][32 * k:32 * k + NH, 0:T], wg[:, c, k * NH:(k + 1) * NH], XT[:, c, :],
                             start=c == 0, stop=c == KC - 1)
            ins.then_inc(gates_psum, 1)

            def project_parts(ps, n, s, transposed):
                for h in range(2):
                    q = 2 * (n - 1) + h
                    pe.wait_ge(lo_ready, q + 1)
                    w_hi = W_hi[:, q % HI].rearrange("p (c n) -> p c n", n=UC)
                    w_lo = ring_lo[:, s, h * HALF:(h + 1) * HALF].rearrange("p (c n) -> p c n", n=UC)
                    for c in range(KC // 2):
                        cx = h * (KC // 2) + c
                        for g in range(2):
                            for m, (w, xt) in enumerate(((w_hi, XT_hi), (w_hi, XT_lo), (w_lo, XT_hi))):
                                wt, xs = w[:, c, g * P:(g + 1) * P], xt[:, cx, :]
                                if not transposed:
                                    wt, xs = xt[:, cx, g * P:(g + 1) * P], w[:, c, :]
                                ins = mm(ps[g], wt, xs, start=cx == 0 and m == 0,
                                         stop=cx == KC - 1 and m == 2)
                    ins.then_inc(half_used if h == 0 else done[s], 1)

            for n, (kind, half, s, use) in enumerate(plan0):
                ps = [pairs[n % 2][:, g, 0:T] for g in range(2)]
                if n >= 12:
                    pe.wait_ge(x_used, n - 11)
                elif n >= 2:
                    pe.wait_ge(copied0, n - 1)
                if n == 0:
                    project(ps, s, use, True)
                else:
                    if n == 1:
                        pe.wait_ge(xt_split, 2)
                    project_parts(ps, n, s, kind not in "vo")
                if n == 0:
                    pe.wait_ge(lam_in, 9 * 16)
                    pe.wait_ge(pt_ready, 1)
                    tp(bank[7][:, 0:76], prow[0:76, :], ident[0:76, 0:76]).then_inc(pt_psum, 1)
                if n == 5:
                    pe.wait_ge(bz_ready, 1)
                    pe.wait_ge(pt_ready, 2)
                    for k in range(3):
                        m = BZ[:, k].rearrange("p (j r) a c -> p j (r a c)", r=4) if k < 2 else \
                            CZ[:, 0].rearrange("p j a s -> p j (a s)")
                        for j in range(NH):
                            ins = tp(bank[5 + k][:, j * P:(j + 1) * P], m[:, j, :], ident[:, :])
                        ins.then_inc(bct_psum, 1)
                if n == 6:
                    pe.wait_ge(bct_ready, 1)
                    for j in range(NH):
                        ins = tp(bank[5][:, j * P:(j + 1) * P], CZ[:, 1, j].rearrange("p a s -> p (a s)"), ident[:, :])
                    ins.then_inc(bct_psum, 1)
                if n == 7:
                    pe.wait_ge(rows_ready, 1)
                    for b in range(NB):
                        for k, row in enumerate((3, 5)):
                            o = (k * NB + b) * NH
                            ins = tp(bank[4][:, o:o + NH], rows[0:NH, row, b * P:(b + 1) * P], ident[0:NH, 0:NH])
                    ins.then_inc(cols_psum, 1)
                    pe.wait_ge(bct_ready, 4)
                    for h in range(NH):
                        ins = mm(bank[5 + h // 2][:, (h % 2) * T:(h % 2 + 1) * T], headsel[:, h, :], rows[0:NH, 4, :],
                                 start=True, stop=True)
                        if h % 2:
                            ins.then_inc(bcast_psum, 1)
                if n == 8:
                    pe.wait_ge(cols_ready, 1)
                    pe.wait_ge(copied0, 4)
                    for h in range(NH):
                        if h >= 2:
                            pe.wait_ge(weights_ready, h - 1)
                        ps = bank[7 if h % 2 == 0 else 4]
                        mm(ps[:, 0:T], kT[:, h, 0:P], qT[:, h, :], start=True, stop=True)
                        mm(ps[:, T:T + P], kT[:, h, P:T], qT[:, h, P:T], start=True, stop=True).then_inc(scores_psum, 1)
                if n == 10:
                    pe.wait_ge(weights_ready, NH)
                    pe.wait_ge(copied0, 6)
                    for m, (b, hp) in enumerate(((0, 0), (0, 1), (1, 0), (1, 1))):
                        for h in (2 * hp, 2 * hp + 1):
                            ps = bank[(5, 6, 7, 4)[m]][:, (h % 2) * (DH + 2):(h % 2 + 1) * (DH + 2)]
                            if b == 0:
                                ins = mm(ps, DEC[:, h, 0:P], V0[:, 0, h, :], start=True, stop=True)
                            else:
                                mm(ps, DEC[:, h, P:T], V0[:, 0, h, :], start=True, stop=False)
                                ins = mm(ps, DEC[:, h, T:T + P], V0[:, 1, h, :], start=False, stop=True)
                        ins.then_inc(num_psum, 1)
            pe.wait_ge(copied0, 12)
            pe.wait_ge(conv_ready, NH)
            pe.wait_ge(mix_lo_ready, 1)
            for n, (pair, s, use) in enumerate(outs0):
                if n == 1:
                    head_transposes(0, HN, 5)
                if n == 2:
                    pe.wait_ge(mix_lo_ready, 2)
                out_parts(0, pair, s, use, OUT0 + 2 * n, n == 0, n == 3)
            norm(1)
            moe(0)
            norm(2)


            def s5_in(p):
                if p >= 1:
                    pe.wait_ge(bu_used, 2 * p)
                for i in (2 * p, 2 * p + 1):
                    j, r = i // 4, slice(32 * (i % 4), 32 * (i % 4) + 32)
                    for k in range(2):
                        ins = mm(bank[4 + i % 2][:, k * T:(k + 1) * T], BT[r, k, j, :], uT[r, j, :],
                                 start=True, stop=True)
                    ins.then_inc(bu_psum, 1)

            def s5_out(p):
                j = p // 2
                if p % 2 == 0 and j >= 2:
                    pe.wait_ge(y_ready, j - 1)
                pe.wait_ge(pc_ready, 2 * p + 2)
                pe.wait_ge(ps_ready, 2 * p + 2)
                terms = ((0, 0, 0), (1, 1, 2), (2, 1, 0), (2, 0, 2))
                for n, (q, c, z) in enumerate(terms):
                    for k in range(2):
                        r = slice(32 * ((2 * p + k) % 4), 32 * ((2 * p + k) % 4) + 32)
                        ins = mm(bank[6 + j % 2][r, 0:T], CT[:, q, j, r],
                                 prod[:, 2 * k + c, z:z + 2].rearrange("p a t -> p (a t)"),
                                 start=n == 0, stop=n == 3)
                ins.then_inc(y_psum, 1)

            def level(l):
                ps = bank[2 + l % 2]
                if l < 8:
                    pe.wait_ge(lqk, l + 1)
                else:
                    pe.wait_ge(lcopied, 7)
                left, right = (QK, QK) if l < 8 else (k1T, q1T)
                for h in range(NH):
                    if l == 0:
                        ins = mm(ps[:, h * P:(h + 1) * P], left[:, h, 0:P], right[:, h, P:T], start=True, stop=True)
                        continue
                    for b in range(NB):
                        n = h * NB + b
                        if l == 1:
                            o = b * P
                            ins = mm(ps[0:64, n * 64:n * 64 + 64], left[:, h, o:o + 64], right[:, h, o + 64:o + P],
                                     start=True, stop=True)
                        elif l == 2:
                            for i in range(2):
                                o = b * P + 64 * i
                                ins = mm(ps[64 * i:64 * i + 32, n * 32:n * 32 + 32], left[:, h, o:o + 32],
                                         right[:, h, o + 32:o + 64], start=True, stop=True)
                        else:
                            for i in range(4):
                                o = b * P + 32 * i
                                ins = mm(ps[32 * i:32 * i + 32, n * 32:n * 32 + 32], left[:, h, o:o + 32],
                                         right[:, h, o:o + 32], start=True, stop=True)
                ins.then_inc(lpsum, 1)

            _, _, s, use = plan1[0]
            w = unit(s, use).rearrange("p (c n) -> p c n", c=KC)
            for b in range(NB):
                pe.wait_ge(xt_ready, 4 * 2 + 2 * b + 2)
                for g in range(2):
                    for c in range(KC):
                        ins = mm(bank[0][:, g * T + b * P:g * T + (b + 1) * P], w[:, c, g * P:(g + 1) * P],
                                 XT[:, c, b * P:(b + 1) * P], start=c == 0, stop=c == KC - 1)
            ins.then_inc(done[s], 1)
            _, _, s, use = plan1[1]
            project(halves_of(bank[1]), s, use, True)
            pe.wait_ge(copied1, 2)
            pe.wait_ge(bct_ready, 4)
            s5_in(0)
            for p in range(S5T // 2):
                n, l = 2 + p, 2 * (p - FIRST_LEVEL)
                kind, half, s, use = plan1[n]
                pe.wait_ge(copied1, n - 1)
                project(halves_of(bank[n % 2]), s, use, kind not in "ig", (0,))
                if l >= 2:
                    level(l - 1)
                if p >= 1:
                    s5_out(p - 1)
                if p + 1 < S5T // 2:
                    s5_in(p + 1)
                project(halves_of(bank[n % 2]), s, use, kind not in "ig", (1,))
                if l >= 0:
                    level(l)
            s5_out(S5T // 2 - 1)
            level(7)
            level(8)
            pe.wait_ge(copied1, 10)
            def glu(j):
                for k in range(NH):
                    ins = mm(bank[j // 2][:, (j % 2) * T:(j % 2 + 1) * T], w[:, k, j * P:(j + 1) * P], uT[:, k, :],
                             start=k == 0, stop=k == NH - 1)
                return ins

            pe.wait_ge(gelu_ready, NH)
            s, use = glu_at
            w = unit(s, use).rearrange("p (k n) -> p k n", k=NH)
            glu(0)
            pe.wait_ge(a_full, 1)
            for b in range(NB):
                for h in range(NH):
                    ps = bank[2 + b][:, h * P:(h + 1) * P]
                    if b == 0:
                        ins = mm(ps, A[:, h, 0, :], V1[:, 0, h, :], start=True, stop=True)
                    else:
                        mm(ps, A[:, h, 1, :], V1[:, 0, h, :], start=True, stop=False)
                        ins = mm(ps, A[:, h, 2, :], V1[:, 1, h, :], start=False, stop=True)
                ins.then_inc(o_psum, 1)
            glu(1).then_inc(glu_psum, 1)
            glu(2)
            glu(3).then_inc(done[s], 1)
            head_transposes(1, HN1, 2)
            pe.wait_ge(y_ready, NH)
            pe.wait_ge(bu_used, S5T)
            for n, (pair, s, use) in enumerate(outs1):
                if n == 0:
                    first_out_unit(4, pair, s, use)
                else:
                    pe.wait_ge(mix_lo_ready, 3 if n == 1 else 4)
                    out_parts(4, pair, s, use, OUT1 + 2 * (n - 1), False, n == 3)
            norm(3)
            moe(1)


_OUTS = [((1, 256, 1024), 'float32')]


def kernel(**inputs):
    import numpy as _np
    import concourse.bacc as _bacc
    from concourse import mybir as _mybir
    from concourse.bass_utils import run_bass_kernel_spmd as _run

    names = ['x', 'norm_mix', 'norm_ffn', 'norm_final', 'ab_w_in', 'ab_gate_bias', 'ab_head_norm', 'ab_conv_w',
             'ab_w_out', 'cd_w_in', 's5_lambda_re', 's5_lambda_im', 's5_b_re', 's5_b_im', 's5_c_re', 's5_c_im',
             's5_d', 's5_log_dt', 's5_w_glu', 's5_b_glu', 'hgrn_lb', 'hgrn_out_norm', 'cd_w_out', 'moe_w_group',
             'moe_b_group', 'moe_w_router', 'moe_b_router', 'moe_w_gate', 'moe_w_up', 'moe_w_down']
    nc = _bacc.Bacc("TRN2", target_bir_lowering=False, num_devices=1)
    arrays, args = {}, []
    for name in names:
        a = _np.ascontiguousarray(inputs[name])
        arrays[f"in_{name}_dram"] = a
        args.append(nc.dram_tensor(f"in_{name}_dram", a.shape, _mybir.dt.from_np(a.dtype),
                                   kind="ExternalInput").ap())
    for i, (shape, dtype) in enumerate(_OUTS):
        dt = _mybir.dt.from_np(_np.dtype(dtype))
        args.append(nc.dram_tensor(f"out_{i}_dram", shape, dt, kind="ExternalOutput").ap())
    hybrid_trunk(nc, *args)
    r = _run(nc, [arrays], core_ids=[0])
    got = tuple(r.results[0][f"out_{i}_dram"] for i in range(len(_OUTS)))
    return got[0]
```
